# Optimizing a Trainium2 kernel written in Bass

```python
import math
import jax, jax.numpy as jnp
from jax import lax
import numpy as np

D_MODEL = 1024
BATCH = 1
SEQ = 256
DEPTH = 2
DEC_BATCH = 1
DEC_SEQ = 1024
PAST_LEN = 256

GRID_W = 64
EPS = 1e-6
ADA_CHUNKS = 6
DN_HEADS = 4
DN_DK = 128
DN_DV = 128
DN_CONV = 3
DN_CHUNK = 64
QK_WIDTH = DN_HEADS * DN_DK
V_WIDTH = DN_HEADS * DN_DV
POOL_WINDOWS = (2, 4, 8, 16)
POOL_GROUPS = 4
POOL_WIDTH = D_MODEL // 2
POOL_GW = POOL_WIDTH // POOL_GROUPS
OFF_Z = 2 * QK_WIDTH + V_WIDTH
OFF_AB = OFF_Z + V_WIDTH
OFF_POOL = OFF_AB + 4 * DN_HEADS
MIX0_IN = OFF_POOL + POOL_WIDTH
HY_WIDTH = D_MODEL
HY_ORDER = 2
HY_SHORT = 3
HY_EMB = 33
HY_BANDS = (HY_EMB - 1) // 2
HY_FFN = 64
HY_MAX_DECAY = math.log(1e-2) / 0.3
HY_MIN_DECAY = math.log(1e-2) / 1.5
FFN_HIDDEN = 2816
FFN_CONV = 3

kernel_name = 'hybrid_deltanet_pool_hyena_diffusion_step'

def rmsnorm(x, g):
    xf = x.astype(jnp.float32)
    y = xf * lax.rsqrt(jnp.mean(xf * xf, axis=-1, keepdims=True) + EPS)
    return (y * g.astype(jnp.float32)).astype(x.dtype)

def adaln(cond, w, b):
    m = jax.nn.silu(cond) @ w + b
    return [t[:, None, :] for t in jnp.split(m, ADA_CHUNKS, axis=-1)]

def dwconv1d(x, w):
    k_w = w.shape[0]
    pad = k_w // 2
    L = x.shape[1]
    xp = jnp.pad(x, ((0, 0), (pad, pad), (0, 0)))
    y = xp[:, 0:L] * w[0]
    for j in range(1, k_w):
        y = y + xp[:, j:j + L] * w[j]
    return y

def dwconv_grid(x, w, rows):
    B, L, C = x.shape
    xi = x.reshape(B, rows, L // rows, C)
    y = lax.conv_general_dilated(xi, w[:, :, None, :], window_strides=(1, 1), padding='SAME',
                                 dimension_numbers=('NHWC', 'HWIO', 'NHWC'), feature_group_count=C)
    return y.reshape(B, L, C)

def l2norm(a):
    return a * lax.rsqrt(jnp.sum(a * a, axis=-1, keepdims=True) + EPS)

def to_chunks(a, n_chunks):
    B, T, H = a.shape[:3]
    a = a.reshape((B, n_chunks, DN_CHUNK, H) + a.shape[3:])
    return jnp.moveaxis(a, 3, 2)

def gated_delta_chunked(q, k, v, g, beta, s0):
    B, T, H, _ = q.shape
    C = DN_CHUNK
    N = T // C
    qc, kc, vc = to_chunks(q, N), to_chunks(k, N), to_chunks(v, N)
    gcum = jnp.cumsum(to_chunks(g, N), axis=-1)
    bc = to_chunks(beta, N)
    tri_incl = jnp.tril(jnp.ones((C, C), dtype=bool))
    tri_strict = jnp.tril(jnp.ones((C, C), dtype=bool), -1)
    diff = gcum[..., :, None] - gcum[..., None, :]
    decay = jnp.where(tri_incl, jnp.exp(jnp.where(tri_incl, diff, 0.0)), 0.0)
    kb = kc * bc[..., None]
    vb = vc * bc[..., None]
    lmat = jnp.where(tri_strict, jnp.einsum('bnhik,bnhjk->bnhij', kb, kc) * decay, 0.0)
    amat = lmat + jnp.eye(C, dtype=q.dtype)
    rhs = jnp.concatenate([vb, kb * jnp.exp(gcum)[..., None]], axis=-1)
    sol = lax.linalg.triangular_solve(amat, rhs, left_side=True, lower=True, unit_diagonal=True)
    u_c, w_c = sol[..., :DN_DV], sol[..., DN_DV:]
    qk = jnp.einsum('bnhik,bnhjk->bnhij', qc, kc) * decay
    q_dec = qc * jnp.exp(gcum)[..., None]
    k_dec = kc * jnp.exp(gcum[..., -1:] - gcum)[..., None]
    chunk_decay = jnp.exp(gcum[..., -1])

    def step(s, xs):
        qk_i, qd_i, kd_i, u_i, w_i, cd_i = xs
        v_new = u_i - jnp.einsum('bhck,bhkv->bhcv', w_i, s)
        o = jnp.einsum('bhck,bhkv->bhcv', qd_i, s) + jnp.einsum('bhij,bhjv->bhiv', qk_i, v_new)
        s = s * cd_i[..., None, None] + jnp.einsum('bhck,bhcv->bhkv', kd_i, v_new)
        return s, o

    xs = tuple(jnp.moveaxis(a, 1, 0) for a in (qk, q_dec, k_dec, u_c, w_c, chunk_decay))
    s_final, o = lax.scan(step, s0, xs)
    o = jnp.moveaxis(o, 0, 1)
    o = jnp.moveaxis(o, 2, 3).reshape(B, T, H, DN_DV)
    return o, s_final

def deltanet_mixer(qkv_pre, z, ab, conv_w, a_log, dt_bias, norm_w, s0_f, s0_b):
    B, L, _ = qkv_pre.shape
    f32 = jnp.float32
    qkv = jax.nn.silu(dwconv1d(qkv_pre, conv_w)).astype(f32)
    q = l2norm(qkv[..., :QK_WIDTH].reshape(B, L, DN_HEADS, DN_DK)) * (DN_DK ** -0.5)
    k = l2norm(qkv[..., QK_WIDTH:2 * QK_WIDTH].reshape(B, L, DN_HEADS, DN_DK))
    v = qkv[..., 2 * QK_WIDTH:].reshape(B, L, DN_HEADS, DN_DV)
    ab = ab.astype(f32).reshape(B, L, 4, DN_HEADS)
    a_dec = jnp.exp(a_log.astype(f32))
    dtb = dt_bias.astype(f32)
    g_f = -a_dec[0] * jax.nn.softplus(ab[:, :, 0] + dtb[0])
    beta_f = jax.nn.sigmoid(ab[:, :, 1])
    g_b = -a_dec[1] * jax.nn.softplus(ab[:, :, 2] + dtb[1])
    beta_b = jax.nn.sigmoid(ab[:, :, 3])
    o_f, s_f = gated_delta_chunked(q, k, v, g_f, beta_f, s0_f.astype(f32))
    rev = lambda t: jnp.flip(t, axis=1)
    o_b, s_b = gated_delta_chunked(rev(q), rev(k), rev(v), rev(g_b), rev(beta_b), s0_b.astype(f32))
    o = o_f + rev(o_b)
    o = o * lax.rsqrt(jnp.mean(o * o, axis=-1, keepdims=True) + EPS) * norm_w.astype(f32)
    o = o * jax.nn.silu(z.astype(f32).reshape(B, L, DN_HEADS, DN_DV))
    return o.reshape(B, L, V_WIDTH).astype(qkv_pre.dtype), s_f, s_b

def multiscale_pool(u, pool_w, pool_scale):
    B, L, _ = u.shape
    uf = u.astype(jnp.float32).reshape(B, L, POOL_GROUPS, POOL_GW)
    cs = jnp.pad(jnp.cumsum(uf, axis=1), ((0, 0), (1, 0), (0, 0), (0, 0)))
    t = jnp.arange(L)
    win = jnp.array(POOL_WINDOWS)
    lo = jnp.clip(t[:, None] - win // 2, 0, L)
    hi = jnp.clip(t[:, None] + win - win // 2, 0, L)
    gi = jnp.arange(POOL_GROUPS)
    mean = (cs[:, hi, gi] - cs[:, lo, gi]) / (hi - lo).astype(jnp.float32)[None, :, :, None]
    d = (mean - uf).astype(u.dtype)
    y = jnp.einsum('blgi,gio->blgo', d, pool_w).reshape(B, L, POOL_WIDTH)
    return y * pool_scale

def mixer_even(h, lp, s0_f, s0_b):
    proj = h @ lp['w_in']
    a_out, s_f, s_b = deltanet_mixer(proj[..., :OFF_Z], proj[..., OFF_Z:OFF_AB], proj[..., OFF_AB:OFF_POOL],
                                     lp['dn_conv_w'], lp['dn_a_log'], lp['dn_dt_bias'], lp['dn_norm_w'], s0_f, s0_b)
    b_out = multiscale_pool(proj[..., OFF_POOL:], lp['pool_w'], lp['pool_scale'])
    y = jnp.concatenate([a_out, b_out], axis=-1) @ lp['w_out']
    return y, s_f, s_b

def hyena_filters(L, lp):
    f32 = jnp.float32
    pos = jnp.arange(L, dtype=f32)
    t01 = pos / (L - 1)
    bands = jnp.linspace(1e-4, HY_BANDS - 1, HY_BANDS, dtype=f32)
    ang = (2.0 * math.pi / L) * pos[:, None] * bands[None, :]
    feat = jnp.concatenate([t01[:, None], jnp.cos(ang), -jnp.sin(ang)], axis=-1)
    fr = lp['hy_freq'].astype(f32)
    hdn = jnp.sin(fr * (feat @ lp['hy_w1'].astype(f32) + lp['hy_b1'].astype(f32)))
    hdn = jnp.sin(fr * (hdn @ lp['hy_w2'].astype(f32) + lp['hy_b2'].astype(f32)))
    hdn = jnp.sin(fr * (hdn @ lp['hy_w3'].astype(f32) + lp['hy_b3'].astype(f32)))
    filt = (hdn @ lp['hy_w4'].astype(f32)).reshape(L, 2, HY_ORDER, HY_WIDTH)
    deltas = jnp.abs(jnp.linspace(HY_MIN_DECAY, HY_MAX_DECAY, HY_WIDTH, dtype=f32))
    window = jnp.exp(-t01[:, None] * deltas[None, :])
    lag_mask = jnp.ones((L, 2, 1, 1), f32).at[0, 1].set(0.0)
    return filt * window[:, None, None, :] * lag_mask

def mixer_hyena(h, lp):
    B, L, _ = h.shape
    f32 = jnp.float32
    u = (dwconv1d(h @ lp['w_in'], lp['hy_short_w']) + lp['hy_short_b']).astype(f32)
    v, x1, x2 = u[..., :HY_WIDTH], u[..., HY_WIDTH:2 * HY_WIDTH], u[..., 2 * HY_WIDTH:]
    filt_f = jnp.fft.rfft(hyena_filters(L, lp), n=2 * L, axis=0)
    resp = filt_f[:, 0] + jnp.conj(filt_f[:, 1])
    bias = lp['hy_bias'].astype(f32)
    z = v
    for o, gate in enumerate((x1, x2)):
        zf = jnp.fft.rfft(z, n=2 * L, axis=1)
        conv = jnp.fft.irfft(zf * resp[None, :, o], n=2 * L, axis=1)[:, :L]
        z = gate * (conv + z * bias[o])
    return z.astype(h.dtype) @ lp['w_out']

def conv_glu(h, lp, rows):
    up = h @ lp['ffn_up']
    a, gte = up[..., :FFN_HIDDEN], up[..., FFN_HIDDEN:]
    a = dwconv_grid(a, lp['ffn_conv_w'], rows) + lp['ffn_conv_b']
    return (jax.nn.gelu(a, approximate=True) * gte) @ lp['ffn_down']

def trunk(x, cond, rows, layers, init_states):
    states = []
    for i in range(DEPTH):
        lp = layers[i]
        sh1, sc1, g1, sh2, sc2, g2 = adaln(cond, lp['ada_w'], lp['ada_b'])
        h = rmsnorm(x, lp['norm1']) * (1 + sc1) + sh1
        if i % 2 == 0:
            y, s_f, s_b = mixer_even(h, lp, init_states[i][0], init_states[i][1])
            states.append((s_f, s_b))
        else:
            y = mixer_hyena(h, lp)
            states.append(None)
        x = x + g1 * y
        h = rmsnorm(x, lp['norm2']) * (1 + sc2) + sh2
        x = x + g2 * conv_glu(h, lp, rows)
    return x, states

def setup_inputs(seed: int = 0) -> dict:
    key = jax.random.key(seed)
    keys = list(jax.random.split(key, 64))
    f32 = jnp.float32
    D = D_MODEL

    def nrm(shape, scale):
        return scale * jax.random.normal(keys.pop(), shape, f32)

    def gain(shape):
        return 1.0 + nrm(shape, 0.02)

    inp = {}
    inp['x_prompt'] = nrm((BATCH, SEQ, D), 1.0)
    inp['x_sample'] = nrm((DEC_BATCH, DEC_SEQ, D), 1.0)
    inp['state_l0_fwd'] = nrm((DEC_BATCH, DN_HEADS, DN_DK, DN_DV), 0.1)
    inp['state_l0_bwd'] = nrm((DEC_BATCH, DN_HEADS, DN_DK, DN_DV), 0.1)
    inp['c'] = nrm((DEC_BATCH, D), 1.0)
    inp['c_ctx'] = nrm((D,), 1.0)
    inp['l0_ada_w'] = nrm((D, ADA_CHUNKS * D), 0.02)
    inp['l0_ada_b'] = nrm((ADA_CHUNKS * D,), 0.02)
    inp['l0_norm1'] = gain((D,))
    inp['l0_w_in'] = nrm((D, MIX0_IN), D ** -0.5)
    inp['l0_dn_conv_w'] = nrm((DN_CONV, OFF_Z), DN_CONV ** -0.5)
    inp['l0_dn_a_log'] = jnp.log(jax.random.uniform(keys.pop(), (2, DN_HEADS), f32, 1.0, 16.0))
    dt = jnp.exp(jax.random.uniform(keys.pop(), (2, DN_HEADS), f32, math.log(1e-3), math.log(1e-1)))
    inp['l0_dn_dt_bias'] = dt + jnp.log(-jnp.expm1(-dt))
    inp['l0_dn_norm_w'] = gain((DN_DV,))
    inp['l0_pool_w'] = nrm((POOL_GROUPS, POOL_GW, POOL_GW), POOL_GW ** -0.5)
    inp['l0_pool_scale'] = gain((POOL_WIDTH,))
    inp['l0_w_out'] = nrm((V_WIDTH + POOL_WIDTH, D), (V_WIDTH + POOL_WIDTH) ** -0.5)
    inp['l0_norm2'] = gain((D,))
    inp['l0_ffn_up'] = nrm((D, 2 * FFN_HIDDEN), D ** -0.5)
    inp['l0_ffn_conv_w'] = nrm((FFN_CONV, FFN_CONV, FFN_HIDDEN), 1.0 / FFN_CONV)
    inp['l0_ffn_conv_b'] = nrm((FFN_HIDDEN,), 0.02)
    inp['l0_ffn_down'] = nrm((FFN_HIDDEN, D), FFN_HIDDEN ** -0.5)
    inp['l1_ada_w'] = nrm((D, ADA_CHUNKS * D), 0.02)
    inp['l1_ada_b'] = nrm((ADA_CHUNKS * D,), 0.02)
    inp['l1_norm1'] = gain((D,))
    inp['l1_w_in'] = nrm((D, 3 * HY_WIDTH), D ** -0.5)
    inp['l1_hy_short_w'] = nrm((HY_SHORT, 3 * HY_WIDTH), HY_SHORT ** -0.5)
    inp['l1_hy_short_b'] = nrm((3 * HY_WIDTH,), 0.02)
    inp['l1_hy_w1'] = nrm((HY_EMB, HY_FFN), HY_EMB ** -0.5)
    inp['l1_hy_b1'] = nrm((HY_FFN,), 0.1)
    inp['l1_hy_w2'] = nrm((HY_FFN, HY_FFN), HY_FFN ** -0.5)
    inp['l1_hy_b2'] = nrm((HY_FFN,), 0.1)
    inp['l1_hy_w3'] = nrm((HY_FFN, HY_FFN), HY_FFN ** -0.5)
    inp['l1_hy_b3'] = nrm((HY_FFN,), 0.1)
    inp['l1_hy_w4'] = nrm((HY_FFN, 2 * HY_ORDER * HY_WIDTH), 0.1 * HY_FFN ** -0.5)
    inp['l1_hy_freq'] = gain((HY_FFN,))
    inp['l1_hy_bias'] = nrm((HY_ORDER, HY_WIDTH), 0.1)
    inp['l1_w_out'] = nrm((HY_WIDTH, D), HY_WIDTH ** -0.5)
    inp['l1_norm2'] = gain((D,))
    inp['l1_ffn_up'] = nrm((D, 2 * FFN_HIDDEN), D ** -0.5)
    inp['l1_ffn_conv_w'] = nrm((FFN_CONV, FFN_CONV, FFN_HIDDEN), 1.0 / FFN_CONV)
    inp['l1_ffn_conv_b'] = nrm((FFN_HIDDEN,), 0.02)
    inp['l1_ffn_down'] = nrm((FFN_HIDDEN, D), FFN_HIDDEN ** -0.5)
    inp['final_norm'] = gain((D,))
    return inp

def reference(x_prompt, x_sample, state_l0_fwd, state_l0_bwd, c, c_ctx,
              l0_ada_w, l0_ada_b, l0_norm1, l0_w_in, l0_dn_conv_w, l0_dn_a_log, l0_dn_dt_bias, l0_dn_norm_w,
              l0_pool_w, l0_pool_scale, l0_w_out, l0_norm2, l0_ffn_up, l0_ffn_conv_w, l0_ffn_conv_b, l0_ffn_down,
              l1_ada_w, l1_ada_b, l1_norm1, l1_w_in, l1_hy_short_w, l1_hy_short_b, l1_hy_w1, l1_hy_b1,
              l1_hy_w2, l1_hy_b2, l1_hy_w3, l1_hy_b3, l1_hy_w4, l1_hy_freq, l1_hy_bias, l1_w_out, l1_norm2,
              l1_ffn_up, l1_ffn_conv_w, l1_ffn_conv_b, l1_ffn_down, final_norm):
    layers = (
        dict(ada_w=l0_ada_w, ada_b=l0_ada_b, norm1=l0_norm1, w_in=l0_w_in, dn_conv_w=l0_dn_conv_w,
             dn_a_log=l0_dn_a_log, dn_dt_bias=l0_dn_dt_bias, dn_norm_w=l0_dn_norm_w, pool_w=l0_pool_w,
             pool_scale=l0_pool_scale, w_out=l0_w_out, norm2=l0_norm2, ffn_up=l0_ffn_up,
             ffn_conv_w=l0_ffn_conv_w, ffn_conv_b=l0_ffn_conv_b, ffn_down=l0_ffn_down),
        dict(ada_w=l1_ada_w, ada_b=l1_ada_b, norm1=l1_norm1, w_in=l1_w_in, hy_short_w=l1_hy_short_w,
             hy_short_b=l1_hy_short_b, hy_w1=l1_hy_w1, hy_b1=l1_hy_b1, hy_w2=l1_hy_w2, hy_b2=l1_hy_b2,
             hy_w3=l1_hy_w3, hy_b3=l1_hy_b3, hy_w4=l1_hy_w4, hy_freq=l1_hy_freq, hy_bias=l1_hy_bias,
             w_out=l1_w_out, norm2=l1_norm2, ffn_up=l1_ffn_up, ffn_conv_w=l1_ffn_conv_w,
             ffn_conv_b=l1_ffn_conv_b, ffn_down=l1_ffn_down),
    )
    zeros = jnp.zeros((x_prompt.shape[0], DN_HEADS, DN_DK, DN_DV), jnp.float32)
    ctx_init = [(zeros, zeros), None]
    xp, ctx_states = trunk(x_prompt, c_ctx[None, :], 1, layers, ctx_init)
    y_prompt = rmsnorm(xp, final_norm)
    rows = x_sample.shape[1] // GRID_W
    lat_init = [(state_l0_fwd, state_l0_bwd), None]
    xs, _ = trunk(x_sample, c, rows, layers, lat_init)
    y_sample = rmsnorm(xs, final_norm)
    new_state_l0_fwd = ctx_states[0][0].astype(x_prompt.dtype)
    new_state_l0_bwd = ctx_states[0][1].astype(x_prompt.dtype)
    return (y_prompt, y_sample, new_state_l0_fwd, new_state_l0_bwd)


_drawn_inputs = setup_inputs


def setup_inputs(seed=0):
    import zlib

    import numpy as np

    out = dict(_drawn_inputs(seed))
    spreads = {}
    factors = {'state_l0_fwd': 8.0,
     'state_l0_bwd': 8.0,
     'l0_dn_norm_w': 8.0,
     'l0_pool_scale': 8.0,
     'l0_norm2': 7.304,
     'l0_ffn_conv_b': 8.0,
     'l1_norm1': 4.765,
     'l1_hy_freq': 2.894,
     'l1_norm2': 24.928,
     'l1_ffn_conv_b': 21.363,
     'final_norm': 8.277,
     'l1_hy_short_b': 3.174}
    for name, (base, spread) in spreads.items():
        noise = np.random.default_rng([zlib.crc32(name.encode()), seed]).standard_normal(out[name].shape)
        drawn = base * np.exp(spread * noise) if base else spread * noise
        out[name] = __import__('jax').numpy.asarray(drawn.astype(out[name].dtype))
    for name, factor in factors.items():
        out[name] = (out[name] * factor).astype(out[name].dtype)
    return out
```

```python
import math
from contextlib import ExitStack

import concourse.bass as bass
import numpy as np
from concourse import mybir

F32 = mybir.dt.float32
ALU = mybir.AluOpType
ACT = mybir.ActivationFunctionType

P = 128
D = 1024
KD = D // P
NS, NP_ = 1024, 256
N = NS + NP_
NT = N // P
GROUPS = [(0, NS, 0), (NS, NP_, 1)]
CHUNKS = [(0, 512), (512, 512), (1024, 256)]
EPS = 1e-6
HEADS = 4
GRID_W = 64
ROWS = NS // GRID_W
HIDDEN = 2816
KH = HIDDEN // P
HALF = KH // 2
WINDOWS = (2, 4, 8, 16)
MIX_IN = 2576
AB_AT = 2048
POOL_AT = 2064
BIG = 1e30
FFN64 = 64
EMB = 33
HC = 256
NCH = D // HC
LEVELS = 7

VECTORS = [("l0_ada_b", 48), ("l0_norm1", 8), ("l0_norm2", 8), ("l0_dn_conv_w", 36), ("l0_dn_norm_w", 1),
           ("l0_pool_scale", 4), ("l0_ffn_conv_w", 198), ("l0_ffn_conv_b", 22), ("l1_ada_b", 48),
           ("l1_norm1", 8), ("l1_norm2", 8), ("l1_hy_short_w", 72), ("l1_hy_short_b", 24),
           ("l1_ffn_conv_w", 198), ("l1_ffn_conv_b", 22), ("final_norm", 8),
           ("l1_hy_freq", 1), ("l1_hy_b1", 1), ("l1_hy_b2", 1), ("l1_hy_b3", 1)]
VCOL, _at = {}, 0
for _n, _r in VECTORS:
    VCOL[_n] = _at
    _at += _r
VTILES = -(-_at // P)

SQUARES = {"ident": 0, "ones": 1, "cum_f": 2, "cum_b": 3, "mA_f": 4, "mB_f": 5, "mA_b": 6, "mB_b": 7}


def constants():
    i = np.arange(P)
    r, c = i[:, None], i[None, :]
    sq = np.zeros((P, 8, P))
    sq[:, 0] = r == c
    sq[:, 1] = 1
    sq[:, 2] = r <= c
    sq[:, 3] = r >= c
    sq[:, 4] = np.where(c < r, 0, BIG)
    sq[:, 5] = np.where(c >= r, 0, -BIG)
    sq[:, 6] = np.where(c > r, 0, BIG)
    sq[:, 7] = np.where(c <= r, 0, -BIG)
    level = np.zeros((P, 2, LEVELS, P))
    for v in range(LEVELS):
        b = 1 << v
        m = (r // (2 * b) == c // (2 * b)) & ((r // b) % 2 == 1) & ((c // b) % 2 == 0)
        level[:, 0, v], level[:, 1, v] = m, m.T
    inv = np.zeros((4, N))
    for g, w in enumerate(WINDOWS):
        for a, n, _ in GROUPS:
            t = np.arange(n)
            inv[g, a:a + n] = 1.0 / (np.clip(t + w - w // 2, 0, n) - np.clip(t - w // 2, 0, n))
    out = {"k_squares": sq.reshape(P, -1), "k_level": level.reshape(P, -1), "k_inv": inv}

    for name, L in (("s", NS), ("p", NP_)):
        T = L // P
        pos = np.concatenate([np.arange(L), L - np.arange(L)]).astype(np.float32)
        t01 = (pos / np.float32(L - 1)).astype(np.float32)
        bands = np.linspace(1e-4, 15, 16, dtype=np.float32)
        ang = (np.float32(2.0 * math.pi / L) * pos[:, None] * bands[None, :]).astype(np.float32)
        feat = np.concatenate([t01[:, None], np.cos(ang), -np.sin(ang)], axis=-1)
        out["k_feat_" + name] = feat.T
        cols = np.zeros((P, 2, 2 * T))
        cols[:, 0] = -t01.reshape(2 * T, P).T
        cols[0, 1, T] = -1e4
        out["k_win_" + name] = cols.reshape(P, -1)
    lo, hi = math.log(1e-2) / 1.5, math.log(1e-2) / 0.3
    out["k_delta"] = np.abs(np.linspace(lo, hi, D, dtype=np.float32))[None, :]

    fwd, inv8, spec = np.zeros((P, 8, 2, 2, P)), np.zeros((P, 8, 2, 2, P)), np.zeros((P, 2, 2, P))
    n = j = np.arange(128.0)
    for leaf, th in enumerate(LEAF_ANGLES):
        if leaf == 0:
            for half in range(2):
                m = n + 128 * half
                a = 2 * math.pi * np.outer(m, j) / 256
                alt = (-1.0) ** m
                fwd[:, 0, half, 0] = np.cos(a)
                fwd[:, 0, half, 1] = np.sin(a)
                fwd[:, 0, half, 1, 0] = alt
                spec[:, half, 0] = np.sin(a)
                spec[:, half, 0, 0] = 0
                spec[:, half, 1] = np.cos(a)
                spec[:, half, 1, 0] = alt
                ci, si = np.cos(a).T / 128, np.sin(a).T / 128
                ci[0], si[0] = 1 / 256, alt / 256
                inv8[:, 0, 0, half], inv8[:, 0, 1, half] = ci / 8, si / 8
            continue
        a = np.outer(n, (th + 2 * math.pi * j) / 128)
        fwd[:, leaf, 0, 0], fwd[:, leaf, 1, 0] = np.cos(a), -np.sin(a)
        fwd[:, leaf, 0, 1], fwd[:, leaf, 1, 1] = np.sin(a), np.cos(a)
        b = a.T
        inv8[:, leaf, 0, 0], inv8[:, leaf, 1, 0] = np.cos(b) / 1024, np.sin(b) / 1024
        inv8[:, leaf, 0, 1], inv8[:, leaf, 1, 1] = -np.sin(b) / 1024, np.cos(b) / 1024
    def packed(m, sin, neg):
        rest = np.stack([m[:, 1:, 0, 0], m[:, 1:, sin[0], sin[1]], m[:, 1:, neg[0], neg[1]]], axis=2)
        return np.concatenate([m[:, 0].reshape(P, -1), rest.reshape(P, -1)], axis=1)
    out["k_fwd"], out["k_inv8"] = packed(fwd, (0, 1), (1, 0)), packed(inv8, (1, 0), (0, 1))
    out["k_spec"] = spec.reshape(P, -1)
    return {k: np.ascontiguousarray(v, dtype=np.float32) for k, v in out.items()}


LEAF_ANGLES = [0.0, math.pi / 2, math.pi / 4, 5 * math.pi / 4, math.pi / 8, 9 * math.pi / 8,
               5 * math.pi / 8, 13 * math.pi / 8]


class Steps:

    def __init__(self, sem, names, rounds=1, before=0):
        self.sem, self.names, self.rounds, self.before = sem, list(names), rounds, before
        self.index = {s: i for i, s in enumerate(self.names)}
        assert len(self.index) == len(self.names)
        self.made = 0

    def at(self, step, round_=0):
        return self.before + round_ * len(self.names) + self.index[step] + 1

    def end(self):
        return self.before + self.rounds * len(self.names)

    def did(self, step, round_=0):
        self.made += 1
        assert self.before + self.made == self.at(step, round_), (self.names, step, round_, self.made)
        return self.sem, 1


def build(nc, A, OUT):
    with ExitStack() as ctx:
        def sem(name):
            return ctx.enter_context(nc.semaphore(name))

        arena = ctx.enter_context(nc.sbuf_tensor("arena", [P, 53200], F32))
        PS = ctx.enter_context(nc.psum_tensor("PS", [P, 8, 512], F32))
        PSF = PS[:, :, :].rearrange("p b n -> p (b n)")

        class Region:

            def __init__(self, a, b):
                self.a, self.b = a, b

            def take(self, *shape):
                n = math.prod(shape)
                assert self.a + n <= self.b, (self.a, n, self.b)
                v = arena[:, self.a:self.a + n]
                self.a += n
                if len(shape) == 2:
                    v = v.rearrange("p (a b) -> p a b", b=shape[1])
                if len(shape) == 3:
                    v = v.rearrange("p (a b c) -> p a b c", b=shape[1], c=shape[2])
                return v

        XT_AT, HT_AT, FIX_AT, W_AT = 0, KD * N, 2 * KD * N, 2 * KD * N + 1400
        XT = Region(XT_AT, HT_AT).take(KD, N)
        HT = Region(HT_AT, FIX_AT).take(KD, N)
        fix = Region(FIX_AT, W_AT)
        VC = fix.take(VTILES * P)
        ident = fix.take(P)
        ones = fix.take(P)
        MOD = fix.take(2, 48, 2)
        SCALE_A = fix.take(5, KD, 2)
        eps = fix.take(1)
        half_pi = fix.take(1)
        CS = fix.take(KD, 2)

        cur = {"x": XT, "h": HT}

        def vec(name, i=0, n=1):
            return VC[:, VCOL[name] + i:VCOL[name] + i + n]

        def psum(bank, n):
            return PSF[:, bank * 512:bank * 512 + n]

        def bcast(ap, n):
            return ap.unsqueeze(2).to_broadcast([P, ap.shape[1], n])

        def over(ap, n):
            return ap.unsqueeze(1).to_broadcast([P, n, ap.shape[1]])

        everything = []

        def steps(name, names, rounds=1):
            s = Steps(sem(name), names, rounds)
            everything.append(s)
            return s

        def ended(eng, *which):
            for s in which:
                eng.wait_ge(s.sem, s.end())

        progs = {"sp": [], "pe": [], "ve": [], "ac": [], "po": []}

        def program(engine):
            def add(f):
                progs[engine].append(f)
                return f
            return add

        w = Region(W_AT, 53200)
        VR = w.take(VTILES, P)
        s_const, s_rows, s_cond = sem("const_landed"), sem("vector_rows_landed"), sem("cond_landed")
        ve0 = steps("ve_setup", ["zero_rows", "eps", "half_pi", "pair"])
        pe0 = steps("pe_setup", ["turn0", "turn1"])
        ac0 = steps("ac_setup", ["cols0", "cols1", "silu"])
        CR = w.take(2, KD)
        nvec = [0]

        @program("sp")
        def _(sp):
            for dst, k in ((ident, 0), (ones, 1)):
                sp.dma_start(dst, A["k_squares"][:, k * P:(k + 1) * P]).then_inc(s_const, 16)
            for j, name in enumerate(("c", "c_ctx")):
                src = A[name].rearrange("a b -> (a b)") if name == "c" else A[name]
                sp.dma_start(CR[:, j, :], src.rearrange("(p k) -> p k", p=P)).then_inc(s_cond, 16)
            sp.wait_ge(ve0.sem, ve0.at("zero_rows"))
            for name, rows in VECTORS:
                src = A[name]
                src = src if len(src.shape) == 1 else (src.rearrange("a b -> (a b)") if len(src.shape) == 2 else src.rearrange("a b c -> (a b c)"))
                width = min(P, src.shape[0])
                src = src.rearrange("(r c) -> r c", c=width)
                at, done = VCOL[name], 0
                while done < rows:
                    n = min(rows - done, P - at % P)
                    sp.dma_start(VR[at % P:at % P + n, at // P, 0:width], src[done:done + n, :]).then_inc(s_rows, 16)
                    nvec[0] += 1
                    done += n
                    at += n

        @program("pe")
        def _(pe):
            pe.wait_ge(s_const, 32)
            pe.wait_ge(s_rows, 16 * nvec[0])
            for half in range(2):
                for t in range(3):
                    m = pe.transpose(PS[:, half, t * P:(t + 1) * P], VR[:, 3 * half + t, :], ident)
                m.then_inc(*pe0.did(f"turn{half}"))

        @program("ve")
        def _(ve):
            ve.memset(VR, 0.0).then_inc(*ve0.did("zero_rows"))
            ve.memset(eps, EPS).then_inc(*ve0.did("eps"))
            ve.memset(half_pi, math.pi / 2).then_inc(*ve0.did("half_pi"))
            ve.wait_ge(s_cond, 32)
            ve.tensor_copy(CS.rearrange("p k j -> p j k"), CR).then_inc(*ve0.did("pair"))

        @program("ac")
        def _(ac):
            for half in range(2):
                ac.wait_ge(pe0.sem, pe0.at(f"turn{half}"))
                ac.activation(VC[:, half * 384:(half + 1) * 384], PS[:, half, 0:384], ACT.Copy)\
                    .then_inc(*ac0.did(f"cols{half}"))
            ac.wait_ge(ve0.sem, ve0.at("pair"))
            ac.activation(CS, CS, ACT.Silu).then_inc(*ac0.did("silu"))

        w = Region(W_AT + 1024, 53200)
        AW = [w.take(KD, 512) for _ in range(2)]
        AR = [w.take(512) for _ in range(2)]
        NA = 24
        s_aw = [sem(f"ada_w_landed{i}") for i in range(2)]
        peA = steps("pe_ada", ["rows", "turn"], NA)
        veA = steps("ve_ada", ["rows"], NA)
        veM = steps("ve_mod", ["mod0", "mod1"] + [f"plus{i}" for i in range(4)] + [f"scale{i}" for i in range(5)])

        @program("sp")
        def _(sp):
            for n in range(NA):
                if n >= 2:
                    sp.wait_ge(peA.sem, peA.at("rows", n - 2))
                layer, m = divmod(n, 12)
                src = A[f"l{layer}_ada_w"].rearrange("(p k) n -> p k n", k=KD)[:, :, m * 512:(m + 1) * 512]
                sp.dma_start(AW[n % 2], src).then_inc(s_aw[n % 2], 16)

        @program("pe")
        def _(pe):
            pe.wait_ge(ac0.sem, ac0.at("silu"))
            for n in range(NA):
                pe.wait_ge(s_aw[n % 2], 16 * (n // 2 + 1))
                if n >= 2:
                    pe.wait_ge(veA.sem, veA.at("rows", n - 2))
                for k in range(KD):
                    m = pe.matmul(PS[0:2, 2 + n % 2, :], CS[:, k, :], AW[n % 2][:, k, :], start=k == 0, stop=k == KD - 1)
                m.then_inc(*peA.did("rows", n))
                pe.wait_ge(veA.sem, veA.at("rows", n))
                for j in range(4):
                    c = (4 * n + j) * 2
                    m = pe.transpose(PS[:, 4, c:c + 2], AR[n % 2][0:2, j * P:(j + 1) * P], ident[0:2, 0:2])
                m.then_inc(*peA.did("turn", n))

        @program("ve")
        def _(ve):
            for n in range(NA):
                ve.wait_ge(peA.sem, peA.at("rows", n))
                if n >= 2:
                    ve.wait_ge(peA.sem, peA.at("turn", n - 2))
                ve.tensor_copy(AR[n % 2][0:2, :], PS[0:2, 2 + n % 2, :]).then_inc(*veA.did("rows", n))
            ve.wait_ge(peA.sem, peA.at("turn", NA - 1))
            ve.wait_ge(ac0.sem, ac0.at("cols1"))
            for layer in range(2):
                ve.tensor_tensor(MOD[:, layer], PS[:, 4, 96 * layer:96 * layer + 96].rearrange("p (m j) -> p m j", j=2),
                                 bcast(vec(f"l{layer}_ada_b", 0, 48), 2), ALU.add).then_inc(*veM.did(f"mod{layer}"))
            ve.wait_ge(veM.sem, veM.at("mod1"))
            for i in range(4):
                layer, second = divmod(i, 2)
                at = 8 + 24 * second
                ve.tensor_scalar(SCALE_A[:, i], MOD[:, layer, at:at + 8, :], 1.0, None, ALU.add)\
                    .then_inc(*veM.did(f"plus{i}"))
            ve.wait_ge(veM.sem, veM.at("plus3"))
            for i in range(4):
                layer, second = divmod(i, 2)
                ve.tensor_tensor(SCALE_A[:, i], SCALE_A[:, i], bcast(vec(f"l{layer}_norm{second + 1}", 0, 8), 2),
                                 ALU.mult).then_inc(*veM.did(f"scale{i}"))
            ve.tensor_copy(SCALE_A[:, 4], bcast(vec("final_norm", 0, 8), 2)).then_inc(*veM.did("scale4"))

        prev = [pe0, ve0, ac0, peA, veA, veM]

        def load_x(tag, prev):
            r = Region(HT_AT, FIX_AT)
            XR = [r.take(D) for _ in range(3)]
            s_x = [sem(f"x{tag}_landed{i}") for i in range(3)]
            pe = steps(f"pe_x{tag}", ["lo", "hi"], NT)
            ve = steps(f"ve_x{tag}", ["lo"], NT)
            ac = steps(f"ac_x{tag}", ["hi"], NT)

            @program("sp")
            def _(sp):
                ended(sp, *prev)
                for t in range(NT):
                    if t >= 3:
                        sp.wait_ge(pe.sem, pe.at("hi", t - 3))
                    src = A["x_sample"][0, t * P:(t + 1) * P, :] if t < NS // P else A["x_prompt"][0, t * P - NS:(t + 1) * P - NS, :]
                    sp.dma_start(XR[t % 3], src).then_inc(s_x[t % 3], 16)

            @program("pe")
            def _(eng):
                ended(eng, *prev)
                for t in range(NT):
                    eng.wait_ge(s_x[t % 3], 16 * (t // 3 + 1))
                    for half, who in ((0, ve), (1, ac)):
                        b = (2 * t) % 8 + half
                        if t >= 4:
                            eng.wait_ge(who.sem, who.at(("lo", "hi")[half], t - 4))
                        for k in range(4):
                            kk = 4 * half + k
                            m = eng.transpose(PS[:, b, k * P:(k + 1) * P], XR[t % 3][:, kk * P:(kk + 1) * P], ident)
                        m.then_inc(*pe.did(("lo", "hi")[half], t))

            @program("ve")
            def _(eng):
                ended(eng, *prev)
                for t in range(NT):
                    eng.wait_ge(pe.sem, pe.at("lo", t))
                    eng.tensor_copy(XT[:, 0:4, t * P:(t + 1) * P], PS[:, (2 * t) % 8, :].rearrange("p (k t) -> p k t", t=P))\
                        .then_inc(*ve.did("lo", t))

            @program("ac")
            def _(eng):
                ended(eng, *prev)
                for t in range(NT):
                    eng.wait_ge(pe.sem, pe.at("hi", t))
                    eng.activation(XT[:, 4:8, t * P:(t + 1) * P], PS[:, (2 * t) % 8 + 1, :].rearrange("p (k t) -> p k t", t=P), ACT.Copy)\
                        .then_inc(*ac.did("hi", t))
            return [pe, ve, ac]

        prev = load_x("a", prev)

        def norm(tag, prev, which, shift):
            XI, HI = cur["x"], cur["h"]
            r = Region(W_AT, W_AT + 3 * N)
            SQ = [r.take(N) for _ in range(2)]
            RS = r.take(N)
            ac = steps(f"ac_n{tag}", ["sq"], KD)
            ac2 = steps(f"ac_nr{tag}", ["root"])
            ac3 = steps(f"ac_nm{tag}", ["s", "p"], KD)
            pe = steps(f"pe_n{tag}", ["sum"], KD)
            ve = steps(f"ve_nr{tag}", ["inv"])
            ve2 = steps(f"ve_n{tag}", ["mul"], KD)

            @program("pe")
            def _(eng):
                ended(eng, *prev)
                for k in range(KD):
                    eng.wait_ge(ac.sem, ac.at("sq", k))
                    for b, (a, n) in enumerate(CHUNKS):
                        m = eng.matmul(PS[:, b, 0:n], ones, SQ[k % 2][:, a:a + n], start=k == 0, stop=k == KD - 1)
                    m.then_inc(*pe.did("sum", k))

            @program("ac")
            def _(eng):
                ended(eng, *prev)
                for k in range(KD):
                    if k >= 2:
                        eng.wait_ge(pe.sem, pe.at("sum", k - 2))
                    eng.activation(SQ[k % 2], XI[:, k, :], ACT.Square).then_inc(*ac.did("sq", k))
                eng.wait_ge(pe.sem, pe.end())
                eng.activation(RS, psum(0, N), ACT.Sqrt, scale=1.0 / D, bias=eps).then_inc(*ac2.did("root"))
                for k in range(KD):
                    eng.wait_ge(ve2.sem, ve2.at("mul", k))
                    for (a, n, j), g in zip(GROUPS, ("s", "p")):
                        eng.activation(HI[:, k, a:a + n], HI[:, k, a:a + n], ACT.Identity, scale=SCALE_A[:, which, k, j:j + 1],
                                       bias=0.0 if shift is None else shift(k, j)).then_inc(*ac3.did(g, k))

            @program("ve")
            def _(eng):
                eng.wait_ge(ac2.sem, ac2.at("root"))
                eng.reciprocal(RS, RS).then_inc(*ve.did("inv"))
                eng.wait_ge(ve.sem, ve.at("inv"))
                for k in range(KD):
                    eng.tensor_tensor(HI[:, k, :], XI[:, k, :], RS, ALU.mult).then_inc(*ve2.did("mul", k))
            return [pe, ac, ac2, ac3, ve, ve2]

        def mod(layer, part):
            return lambda k, j: MOD[:, layer, 8 * part + k, j:j + 1]

        def mixer_even(before_norm, prev):
            r = Region(W_AT, 53200)
            QT, KT, VT, ZT, PO = (r.take(HEADS, N) for _ in range(5))
            WB = [r.take(KD, P) for _ in range(2)]
            PADN = N + 4
            PAD, CV = r.take(PADN), r.take(PADN)
            POW, ABW = r.take(4, P), r.take(KD, 16)
            ABS, GG, BT, TA = r.take(NT, 16), r.take(NT, 8), r.take(NT, 8), r.take(NT, 8)
            DTB, ALOG = r.take(8), r.take(8)
            r = Region(XT_AT, HT_AT)
            SQM, LVM = r.take(6, P), r.take(2, LEVELS, P)
            top = Region(r.a, r.b)
            OT = r.take(HEADS, N)
            spare = Region(r.a, r.b)
            GAP = 8
            WU = GAP + NS + GAP + NP_ + GAP
            UPAD, PA, PB, INV = top.take(WU), top.take(WU), top.take(WU), top.take(N)
            h = Region(HT_AT, FIX_AT)
            SQ = [h.take(N) for _ in range(2)]
            RB = [h.take(N) for _ in range(2)]
            w_in = A["l0_w_in"].rearrange("(k p) n -> p k n", p=P)
            tiles = [("pool", g, POOL_AT + g * P) for g in range(4)]
            for kind, at in (("k", 512), ("q", 0), ("v", 1024), ("z", 1536)):
                tiles += [(kind, g, at + g * P) for g in range(HEADS)]
            n_t = len(tiles)
            dest = {"q": QT, "k": KT, "v": VT, "z": ZT}
            pos = {"q": 0, "k": 4, "v": 8}
            s_w = [sem(f"in0_landed{i}") for i in range(2)]
            s_small, s_mask, s_inv = sem("mix0_small_landed"), sem("masks_landed"), sem("inv_landed")
            pe = steps("pe_in0", ["t"], n_t)
            peAB = steps("pe_ab", ["ab"])
            ac = steps("ac_in0", ["s", "p"], n_t)
            acS = steps("ac_silu0", ["s", "p"], 12)
            veZ = steps("ve_zero0", ["pad", "upad"])
            ve_names, doubled = [], {}
            for g, w in enumerate(WINDOWS):
                doubled[g] = int(math.log2(w))
                ve_names += [f"pool{g}.d{i}" for i in range(doubled[g])] + [f"pool{g}.m{j}" for j in "sp"] + [f"pool{g}.u{j}" for j in "sp"]
            ve_names += [f"conv{i}.{k}" for i in range(12) for k in range(3)]
            ve = steps("ve_in0", ve_names)

            @program("sp")
            def _(eng):
                ended(eng, *before_norm)
                for i, (_, _, at) in enumerate(tiles):
                    if i >= 2:
                        eng.wait_ge(pe.sem, pe.at("t", i - 2))
                    eng.dma_start(WB[i % 2], w_in[:, :, at:at + P]).then_inc(s_w[i % 2], 16)
                    if i == 1:
                        ended(eng, *prev)
                        eng.dma_start(POW, A["l0_pool_w"].rearrange("g i o -> i g o")).then_inc(s_small, 16)
                        eng.dma_start(ABW, w_in[:, :, AB_AT:AB_AT + 16]).then_inc(s_small, 16)
                        for dst, name in ((DTB, "l0_dn_dt_bias"), (ALOG, "l0_dn_a_log")):
                            eng.dma_start(dst, A[name].rearrange("a b -> (a b)").partition_broadcast(P)).then_inc(s_small, 16)
                        eng.dma_start(SQM, A["k_squares"][:, 2 * P:8 * P].rearrange("p (a b) -> p a b", b=P)).then_inc(s_mask, 16)
                        eng.dma_start(LVM.rearrange("p a b c -> p (a b c)"), A["k_level"]).then_inc(s_mask, 16)
                    if i < 4:
                        if i:
                            eng.wait_ge(ve.sem, ve.at(f"pool{i - 1}.mp"))
                        else:
                            ended(eng, *prev)
                        eng.dma_start(INV, A["k_inv"][i, :].partition_broadcast(P)).then_inc(s_inv, 16)

            @program("pe")
            def _(eng):
                ended(eng, *prev)
                for i in range(n_t):
                    eng.wait_ge(s_w[i % 2], 16 * (i // 2 + 1))
                    if i >= 2:
                        eng.wait_ge(ac.sem, ac.at("p", i - 2))
                    for k in range(KD):
                        for b, (a, n) in enumerate(CHUNKS):
                            m = eng.matmul(PS[:, 3 * (i % 2) + b, 0:n], WB[i % 2][:, k, :], HT[:, k, a:a + n],
                                           start=k == 0, stop=k == KD - 1)
                    m.then_inc(*pe.did("t", i))
                eng.wait_ge(s_small, 64)
                for c in range(NT):
                    for k in range(KD):
                        m = eng.matmul(PS[:, 6, c * 16:(c + 1) * 16], HT[:, k, c * P:(c + 1) * P], ABW[:, k, :],
                                       start=k == 0, stop=k == KD - 1)
                m.then_inc(*peAB.did("ab"))

            def silu(eng, i):
                kind, g, _ = tiles[4 + i]
                eng.wait_ge(ve.sem, ve.at(f"conv{i}.2"))
                for a, n, j in GROUPS:
                    eng.activation(dest[kind][:, g, a:a + n], CV[:, 1 + a + 2 * j:1 + a + 2 * j + n], ACT.Silu).then_inc(*acS.did("sp"[j], i))

            @program("ac")
            def _(eng):
                ended(eng, *prev)
                eng.wait_ge(veZ.sem, veZ.end())
                for i, (kind, g, _) in enumerate(tiles):
                    eng.wait_ge(pe.sem, pe.at("t", i))
                    if kind == "pool" and g:
                        eng.wait_ge(ve.sem, ve.at(f"pool{g - 1}.up"))
                    if 5 <= i < 16:
                        eng.wait_ge(ve.sem, ve.at(f"conv{i - 5}.2"))
                    for a, n, j in GROUPS:
                        src = PSF[:, 1536 * (i % 2) + a:1536 * (i % 2) + a + n]
                        if kind == "pool":
                            at = GAP + a + GAP * j
                            m = eng.activation(UPAD[:, at:at + n], src, ACT.Copy)
                        elif kind == "z":
                            m = eng.activation(ZT[:, g, a:a + n], src, ACT.Silu)
                        else:
                            at = 1 + a + 2 * j
                            m = eng.activation(PAD[:, at:at + n], src, ACT.Copy)
                        m.then_inc(*ac.did("sp"[j], i))
                    if 5 <= i < 17:
                        silu(eng, i - 5)

            @program("ve")
            def _(eng):
                ended(eng, *prev)
                eng.memset(PAD, 0.0).then_inc(*veZ.did("pad"))
                eng.memset(UPAD, 0.0).then_inc(*veZ.did("upad"))
                for g, w in enumerate(WINDOWS):
                    eng.wait_ge(ac.sem, ac.at("p", g))
                    src = UPAD
                    for i in range(doubled[g]):
                        if i:
                            eng.wait_ge(ve.sem, ve.at(f"pool{g}.d{i - 1}"))
                        elif g:
                            eng.wait_ge(ve.sem, ve.at(f"pool{g - 1}.mp"))
                        dst, sh = (PA, PB)[i % 2], 1 << i
                        width = WU - (2 << i) + 1
                        eng.tensor_tensor(dst[:, 0:width], src[:, 0:width], src[:, sh:sh + width], ALU.add).then_inc(*ve.did(f"pool{g}.d{i}"))
                        src = dst
                    eng.wait_ge(s_inv, 16 * (g + 1))
                    eng.wait_ge(ve.sem, ve.at(f"pool{g}.d{doubled[g] - 1}"))
                    for a, n, j in GROUPS:
                        at = GAP + a + GAP * j
                        eng.tensor_tensor(PO[:, g, a:a + n], src[:, at - w // 2:at - w // 2 + n], INV[:, a:a + n], ALU.mult)\
                            .then_inc(*ve.did(f"pool{g}.m{'sp'[j]}"))
                    eng.wait_ge(ve.sem, ve.at(f"pool{g}.mp"))
                    for a, n, j in GROUPS:
                        at = GAP + a + GAP * j
                        eng.tensor_tensor(PO[:, g, a:a + n], PO[:, g, a:a + n], UPAD[:, at:at + n], ALU.subtract)\
                            .then_inc(*ve.did(f"pool{g}.u{'sp'[j]}"))
                for i in range(12):
                    kind, g, _ = tiles[4 + i]
                    eng.wait_ge(ac.sem, ac.at("p", 4 + i))
                    if i:
                        eng.wait_ge(acS.sem, acS.at("p", i - 1))
                    for k in range(3):
                        wcol = vec("l0_dn_conv_w", 12 * k + pos[kind] + g)
                        src, dst = PAD[:, k:k + PADN - 2], CV[:, 1:PADN - 1]
                        if k:
                            eng.wait_ge(ve.sem, ve.at(f"conv{i}.{k - 1}"))
                            m = eng.scalar_tensor_tensor(dst, src, wcol, dst, ALU.mult, ALU.add)
                        else:
                            m = eng.tensor_scalar(dst, src, wcol, None, ALU.mult)
                        m.then_inc(*ve.did(f"conv{i}.{k}"))

            part1 = [pe, peAB, ac, acS, ve]

            peN = steps("pe_l2", ["t"], 12)
            acN = steps("ac_l2", ["sq"], 8)
            acR = steps("ac_l2r", ["root"], 8)
            acP = steps("ac_pool", ["p"], 4)
            acG = steps("ac_gate", ["exp_a", "ln", "sig", "a"])
            veN = steps("ve_l2", ["inv", "mul"], 8)
            veG = steps("ve_gate", ["copy", "dt", "abs", "g", "ga", "one", "beta"])
            norm_tiles = [(KT, g, 1.0) for g in range(4)] + [(QT, g, float(P) ** -0.5) for g in range(4)]
            a_cols = ABS.rearrange("p t (a b c) -> p t a b c", a=2, b=2)

            def pair(ap):
                return ap.rearrange("p t (a c) -> p t a c", a=2)

            @program("pe")
            def _(eng):
                for i in range(12):
                    if i < 8:
                        eng.wait_ge(acN.sem, acN.at("sq", i))
                        if i == 0:
                            ended(eng, *part1)
                        if i >= 2:
                            eng.wait_ge(acR.sem, acR.at("root", i - 2))
                    else:
                        eng.wait_ge(*((acR.sem, acR.at("root", i - 2)) if i < 10 else (acP.sem, acP.at("p", i - 10))))
                    for b, (a, n) in enumerate(CHUNKS):
                        lhs, rhs = (ones, SQ[i % 2]) if i < 8 else (POW[:, i - 8, :], PO[:, i - 8, :])
                        m = eng.matmul(PS[:, 3 * (i % 2) + b, 0:n], lhs, rhs[:, a:a + n], start=True, stop=True)
                    m.then_inc(*peN.did("t", i))

            @program("ac")
            def _(eng):
                ended(eng, *part1)
                for i in range(9):
                    if i < 8:
                        t, g, _ = norm_tiles[i]
                        if i >= 2:
                            eng.wait_ge(peN.sem, peN.at("t", i - 2))
                        eng.activation(SQ[i % 2], t[:, g, :], ACT.Square).then_inc(*acN.did("sq", i))
                    if i:
                        eng.wait_ge(peN.sem, peN.at("t", i - 1))
                        if i >= 3:
                            eng.wait_ge(veN.sem, veN.at("mul", i - 3))
                        eng.activation(RB[(i - 1) % 2], psum(3 * ((i - 1) % 2), N), ACT.Sqrt, bias=eps).then_inc(*acR.did("root", i - 1))
                for g in range(4):
                    eng.wait_ge(peN.sem, peN.at("t", 8 + g))
                    eng.activation(PO[:, g, :], psum(3 * (g % 2), N), ACT.Identity, bias=0.0, scale=vec("l0_pool_scale", g)).then_inc(*acP.did("p", g))
                eng.wait_ge(veG.sem, veG.at("abs"))
                eng.activation(TA, TA, ACT.Exp, scale=-1.0).then_inc(*acG.did("exp_a"))
                eng.wait_ge(acG.sem, acG.at("exp_a"))
                eng.activation(TA, TA, ACT.Ln, bias=1.0).then_inc(*acG.did("ln"))
                eng.activation(pair(BT), a_cols[:, :, :, 1, :], ACT.Exp, scale=-1.0).then_inc(*acG.did("sig"))
                eng.activation(ALOG, ALOG, ACT.Exp).then_inc(*acG.did("a"))

            @program("ve")
            def _(eng):
                eng.wait_ge(peAB.sem, peAB.end())
                eng.tensor_copy(ABS.rearrange("p t c -> p (t c)"), PS[:, 6, 0:160]).then_inc(*veG.did("copy"))
                eng.wait_ge(veG.sem, veG.at("copy"))
                eng.tensor_tensor(pair(GG), a_cols[:, :, :, 0, :], pair(over(DTB, NT)), ALU.add).then_inc(*veG.did("dt"))
                eng.wait_ge(veG.sem, veG.at("dt"))
                eng.scalar_tensor_tensor(TA, GG, -1.0, GG, ALU.mult, ALU.max).then_inc(*veG.did("abs"))
                for i in range(8):
                    t, g, scale = norm_tiles[i]
                    eng.wait_ge(acR.sem, acR.at("root", i))
                    eng.reciprocal(RB[i % 2], RB[i % 2]).then_inc(*veN.did("inv", i))
                    eng.wait_ge(veN.sem, veN.at("inv", i))
                    eng.scalar_tensor_tensor(t[:, g, :], RB[i % 2], scale, t[:, g, :], ALU.mult, ALU.mult).then_inc(*veN.did("mul", i))
                eng.wait_ge(acG.sem, acG.at("a"))
                eng.scalar_tensor_tensor(GG, GG, 0.0, TA, ALU.max, ALU.add).then_inc(*veG.did("g"))
                eng.wait_ge(veG.sem, veG.at("g"))
                eng.scalar_tensor_tensor(GG, GG, -1.0, over(ALOG, NT), ALU.mult, ALU.mult).then_inc(*veG.did("ga"))
                eng.tensor_scalar(BT, BT, 1.0, None, ALU.add).then_inc(*veG.did("one"))
                eng.wait_ge(veG.sem, veG.at("one"))
                eng.reciprocal(BT, BT).then_inc(*veG.did("beta"))

            part2 = [peN, acN, acR, acP, acG, veN, veG]

            h = Region(HT_AT, FIX_AT)

            def buf(name):
                reg = h if h.a + 512 <= h.b else spare
                return reg.take(HEADS, P)
            B = [{nm: buf(nm) for nm in ("L", "M0", "M1", "X", "Y", "R", "QK", "QD", "KD", "VB", "VN", "S")} for _ in range(2)]
            C = [{nm: TA.rearrange("p a b -> p (a b)")[:, 0:4] if False else spare.take(4) for nm in ("gc", "gl", "eg", "egl", "cd", "nb")} for _ in range(2)]
            IT = NT
            LV = range(1, LEVELS)
            pn = ["gb", "gc", "kk", "qk", "kt", "vt", "xt"]
            for v in LV:
                pn += [f"r{v}"] + ([f"q{v}"] if v < LEVELS - 1 else []) + [f"u{v}"]
            pn += ["ks", "vn", "o", "ds"]
            vn = ["gu", "gc", "ta", "tb", "tc", "gl", "l", "qk", "nb", "kd", "vb", "x"]
            for v in LV:
                vn += ([f"x{v}"] if v < LEVELS - 1 else []) + [f"y{v}"]
            vn += ["r1", "r2", "o", "s1", "s2"]
            pe_d = [steps(f"pe_dn{d}", pn, IT) for d in "fb"]
            ve_d = [steps(f"ve_dn{d}", vn, IT) for d in "fb"]
            ac_d = [steps(f"ac_dn{d}", ["eb", "ea", "cd", "eq", "eg", "egl", "y"] + [f"r{v}" for v in LV] + ["vn"], IT) for d in "fb"]
            po_d = [steps(f"po_dn{d}", ["lb", "lm0", "qd"] + [f"lm{v}" for v in LV], IT) for d in "fb"]
            s_state, s_new = sem("state_landed"), sem("state_stored")

            def chunk(it, d):
                first, count = (0, NS // P) if it < NS // P else (NS // P, NP_ // P)
                return it if d == 0 else first + count - 1 - (it - first)

            def cols(it, d):
                c = chunk(it, d)
                return slice(c * P, (c + 1) * P)

            def bank(d, b):
                return PS[:, 4 * d + b, :].rearrange("p (h t) -> p h t", t=P)
            LAST = (P - 1, 0)
            DIRS = (0, 1)

            @program("sp")
            def _(eng):
                ended(eng, *part2)
                for d, name in enumerate(("state_l0_fwd", "state_l0_bwd")):
                    eng.dma_start(B[d]["S"], A[name][0].rearrange("h k v -> k h v")).then_inc(s_state, 16)
                for d, name in enumerate(("new_f", "new_b")):
                    eng.wait_ge(ve_d[d].sem, ve_d[d].end())
                    eng.dma_start(OUT[name][0].rearrange("h k v -> k h v"), B[d]["S"]).then_inc(s_new, 16)
                eng.wait_ge(s_new, 32)

            @program("pe")
            def _(eng):
                ended(eng, *part2)
                eng.wait_ge(s_mask, 32)

                def heads(d, b, f):
                    for hd in range(HEADS):
                        m = f(bank(d, b)[:, hd, :], hd)
                    return m
                for it in range(IT):
                    for d in DIRS:
                        pe, ve, ac, po, bf = pe_d[d], ve_d[d], ac_d[d], po_d[d], B[d]
                        eng.wait_ge(ve.sem, ve.at("gu", it))
                        if it:
                            eng.wait_ge(ac.sem, ac.at("vn", it - 1))
                        eng.matmul(PS[:, 4 * d, :], ones, bf["R"].rearrange("p h t -> p (h t)"), start=True, stop=True).then_inc(*pe.did("gb", it))
                        eng.matmul(PS[:, 4 * d + 3, 0:4], SQM[:, d, :], GG[:, chunk(it, d), 4 * d:4 * d + 4], start=True, stop=True).then_inc(*pe.did("gc", it))
                        cs = cols(it, d)
                        heads(d, 1, lambda o, hd: eng.matmul(o, KT[:, hd, cs], KT[:, hd, cs], start=True, stop=True)).then_inc(*pe.did("kk", it))
                        heads(d, 2, lambda o, hd: eng.matmul(o, KT[:, hd, cs], QT[:, hd, cs], start=True, stop=True)).then_inc(*pe.did("qk", it))
                    for d in DIRS:
                        pe, ve, ac, po, bf = pe_d[d], ve_d[d], ac_d[d], po_d[d], B[d]
                        cs = cols(it, d)
                        eng.wait_ge(ve.sem, ve.at("gc", it))
                        heads(d, 3, lambda o, hd: eng.transpose(o, KT[:, hd, cs], ident)).then_inc(*pe.did("kt", it))
                        eng.wait_ge(ve.sem, ve.at("gl", it))
                        eng.wait_ge(ac.sem, ac.at("eq", it))
                        heads(d, 0, lambda o, hd: eng.transpose(o, VT[:, hd, cs], ident)).then_inc(*pe.did("vt", it))
                    for d in DIRS:
                        pe, ve, ac, po, bf = pe_d[d], ve_d[d], ac_d[d], po_d[d], B[d]
                        eng.wait_ge(ve.sem, ve.at("x", it))
                        heads(d, 3, lambda o, hd: eng.transpose(o, bf["X"][:, hd, :], ident)).then_inc(*pe.did("xt", it))
                    for v in LV:
                        for d in DIRS:
                            pe, ve, ac, po, bf = pe_d[d], ve_d[d], ac_d[d], po_d[d], B[d]
                            if v == 1:
                                eng.wait_ge(ac.sem, ac.at("y", it))
                            else:
                                eng.wait_ge(ve.sem, ve.at(f"y{v - 1}", it))
                            eng.wait_ge(po.sem, po.at(f"lm{v}", it))
                            lm = bf[f"M{v % 2}"]
                            heads(d, 0, lambda o, hd: eng.matmul(o, lm[:, hd, :], bf["Y"][:, hd, :], start=True, stop=True)).then_inc(*pe.did(f"r{v}", it))
                        for d in DIRS:
                            pe, ve, ac, po, bf = pe_d[d], ve_d[d], ac_d[d], po_d[d], B[d]
                            eng.wait_ge(ac.sem, ac.at(f"r{v}", it))
                            if v < LEVELS - 1:
                                heads(d, 1, lambda o, hd: eng.matmul(o, bf["R"][:, hd, :], bf["X"][:, hd, :], start=True, stop=True)).then_inc(*pe.did(f"q{v}", it))
                            heads(d, 2, lambda o, hd: eng.matmul(o, bf["X"][:, hd, :], bf["R"][:, hd, :], start=True, stop=True)).then_inc(*pe.did(f"u{v}", it))
                    for d in DIRS:
                        pe, ve, ac, po, bf = pe_d[d], ve_d[d], ac_d[d], po_d[d], B[d]
                        cs = cols(it, d)
                        if it == 0:
                            eng.wait_ge(s_state, 32)
                        else:
                            eng.wait_ge(ve.sem, ve.at("s2", it - 1))
                        heads(d, 3, lambda o, hd: eng.matmul(o, KT[:, hd, cs], bf["S"][:, hd, :], start=True, stop=True)).then_inc(*pe.did("ks", it))
                    for d in DIRS:
                        pe, ve, ac, po, bf = pe_d[d], ve_d[d], ac_d[d], po_d[d], B[d]
                        eng.wait_ge(ve.sem, ve.at("r2", it))
                        heads(d, 0, lambda o, hd: eng.matmul(o, bf["Y"][:, hd, :], bf["R"][:, hd, :], start=True, stop=True)).then_inc(*pe.did("vn", it))
                    for d in DIRS:
                        pe, ve, ac, po, bf = pe_d[d], ve_d[d], ac_d[d], po_d[d], B[d]
                        eng.wait_ge(ac.sem, ac.at("vn", it))
                        eng.wait_ge(po.sem, po.at("qd", it))

                        def out(o, hd):
                            eng.matmul(o, bf["S"][:, hd, :], bf["QD"][:, hd, :], start=True, stop=False)
                            return eng.matmul(o, bf["VN"][:, hd, :], bf["QK"][:, hd, :], start=False, stop=True)
                        heads(d, 1, out).then_inc(*pe.did("o", it))
                        heads(d, 2, lambda o, hd: eng.matmul(o, bf["KD"][:, hd, :], bf["VN"][:, hd, :], start=True, stop=True)).then_inc(*pe.did("ds", it))

            @program("ve")
            def _(eng):
                ended(eng, *part2)
                eng.wait_ge(s_mask, 32)

                def tt(d, it, step, out, a, b, op):
                    eng.tensor_tensor(out, a, b, op).then_inc(*ve_d[d].did(step, it))
                for it in range(IT):
                    for d in DIRS:
                        ve, bf, cc, c = ve_d[d], B[d], C[d], chunk(it, d)
                        tt(d, it, "gu", bf["R"], over(SQM[:, d, :], HEADS), bcast(GG[:, c, 4 * d:4 * d + 4], P), ALU.mult)
                    for d in DIRS:
                        pe, ve, bf, cc, c = pe_d[d], ve_d[d], B[d], C[d], chunk(it, d)
                        eng.wait_ge(pe.sem, pe.at("gc", it))
                        eng.tensor_copy(cc["gc"], PS[:, 4 * d + 3, 0:4]).then_inc(*ve.did("gc", it))
                        eng.wait_ge(ve.sem, ve.at("gc", it))
                        tt(d, it, "ta", bf["L"], bank(d, 0), bcast(cc["gc"], P), ALU.subtract)
                        eng.wait_ge(ve.sem, ve.at("ta", it))
                        tt(d, it, "tb", bf["QK"], bf["L"], over(SQM[:, 3 + 2 * d, :], HEADS), ALU.add)
                        tt(d, it, "tc", bf["L"], bf["L"], over(SQM[:, 2 + 2 * d, :], HEADS), ALU.add)
                        tt(d, it, "gl", cc["gl"], bank(d, 0)[:, :, LAST[d]], cc["gc"], ALU.subtract)
                    for d in DIRS:
                        pe, ve, ac, po, bf, cc, c = pe_d[d], ve_d[d], ac_d[d], po_d[d], B[d], C[d], chunk(it, d)
                        beta = BT[:, c, 4 * d:4 * d + 4]
                        eng.wait_ge(ac.sem, ac.at("ea", it))
                        eng.wait_ge(pe.sem, pe.at("qk", it))
                        tt(d, it, "l", bf["L"], bf["L"], bank(d, 1), ALU.mult)
                        tt(d, it, "qk", bf["QK"], bf["QK"], bank(d, 2), ALU.mult)
                        eng.wait_ge(ac.sem, ac.at("egl", it))
                        eng.scalar_tensor_tensor(cc["nb"], cc["eg"], -1.0, beta, ALU.mult, ALU.mult).then_inc(*ve.did("nb", it))
                        eng.wait_ge(pe.sem, pe.at("kt", it))
                        tt(d, it, "kd", bf["KD"], bank(d, 3), bcast(cc["egl"], P), ALU.mult)
                        eng.wait_ge(pe.sem, pe.at("vt", it))
                        tt(d, it, "vb", bf["VB"], bank(d, 0), bcast(beta, P), ALU.mult)
                        eng.wait_ge(po.sem, po.at("lm0", it))
                        tt(d, it, "x", bf["X"], over(ident, HEADS), bf["M0"], ALU.subtract)
                    for v in LV:
                        for d in DIRS:
                            pe, ve, bf = pe_d[d], ve_d[d], B[d]
                            eng.wait_ge(pe.sem, pe.at(f"u{v}", it))
                            if v == 1:
                                eng.wait_ge(ve.sem, ve.at("x", it))
                                eng.wait_ge(ac_d[d].sem, ac_d[d].at("y", it))
                            else:
                                eng.wait_ge(ve.sem, ve.at(f"y{v - 1}", it))
                            if v < LEVELS - 1:
                                tt(d, it, f"x{v}", bf["X"], bf["X"], bank(d, 1), ALU.subtract)
                            tt(d, it, f"y{v}", bf["Y"], bf["Y"], bank(d, 2), ALU.subtract)
                    for d in DIRS:
                        pe, ve, bf, cc = pe_d[d], ve_d[d], B[d], C[d]
                        eng.wait_ge(pe.sem, pe.at("ks", it))
                        tt(d, it, "r1", bf["R"], bank(d, 3), bcast(cc["nb"], P), ALU.mult)
                        eng.wait_ge(ve.sem, ve.at("r1", it))
                        tt(d, it, "r2", bf["R"], bf["R"], bf["VB"], ALU.add)
                    for d in DIRS:
                        pe, ve, bf, cc = pe_d[d], ve_d[d], B[d], C[d]
                        eng.wait_ge(pe.sem, pe.at("ds", it))
                        o = OT[:, :, cols(it, d)]
                        seen = [j for j in range(it) if chunk(j, 1 - d) == chunk(it, d)]
                        if seen:
                            eng.wait_ge(ve_d[1 - d].sem, ve_d[1 - d].at("o", seen[0]))
                            tt(d, it, "o", o, o, bank(d, 1), ALU.add)
                        else:
                            eng.tensor_copy(o, bank(d, 1)).then_inc(*ve.did("o", it))
                        if it == 0:
                            eng.wait_ge(s_state, 32)
                        if it == NS // P - 1:
                            eng.memset(bf["S"], 0.0).then_inc(*ve.did("s1", it))
                            eng.wait_ge(ve.sem, ve.at("s1", it))
                            eng.memset(bf["S"], 0.0).then_inc(*ve.did("s2", it))
                        else:
                            if it:
                                eng.wait_ge(ve.sem, ve.at("s2", it - 1))
                            tt(d, it, "s1", bf["S"], bf["S"], bcast(cc["cd"], P), ALU.mult)
                            eng.wait_ge(ve.sem, ve.at("s1", it))
                            tt(d, it, "s2", bf["S"], bf["S"], bank(d, 2), ALU.add)

            @program("ac")
            def _(eng):
                ended(eng, *part2)
                for it in range(IT):
                    for d in DIRS:
                        pe, ve, ac, bf, cc = pe_d[d], ve_d[d], ac_d[d], B[d], C[d]
                        eng.wait_ge(ve.sem, ve.at("gl", it))
                        eng.activation(bf["QK"], bf["QK"], ACT.Exp).then_inc(*ac.did("eb", it))
                        eng.activation(bf["L"], bf["L"], ACT.Exp, scale=-1.0).then_inc(*ac.did("ea", it))
                        eng.activation(cc["cd"], bank(d, 0)[:, :, LAST[d]], ACT.Exp).then_inc(*ac.did("cd", it))
                        eng.activation(bf["QD"], bank(d, 0), ACT.Exp).then_inc(*ac.did("eq", it))
                        eng.activation(cc["eg"], cc["gc"], ACT.Exp).then_inc(*ac.did("eg", it))
                        eng.activation(cc["egl"], cc["gl"], ACT.Exp).then_inc(*ac.did("egl", it))
                    for d in DIRS:
                        pe, ac, bf = pe_d[d], ac_d[d], B[d]
                        eng.wait_ge(pe.sem, pe.at("xt", it))
                        eng.activation(bf["Y"], bank(d, 3), ACT.Copy).then_inc(*ac.did("y", it))
                    for v in LV:
                        for d in DIRS:
                            pe, ac, bf = pe_d[d], ac_d[d], B[d]
                            eng.wait_ge(pe.sem, pe.at(f"r{v}", it))
                            eng.activation(bf["R"], bank(d, 0), ACT.Copy).then_inc(*ac.did(f"r{v}", it))
                    for d in DIRS:
                        pe, ac, bf = pe_d[d], ac_d[d], B[d]
                        eng.wait_ge(pe.sem, pe.at("vn", it))
                        eng.activation(bf["VN"], bank(d, 0), ACT.Copy).then_inc(*ac.did("vn", it))

            @program("po")
            def _(eng):
                eng.wait_ge(s_mask, 32)
                for it in range(IT):
                    for d in DIRS:
                        pe, ve, ac, po, bf, c = pe_d[d], ve_d[d], ac_d[d], po_d[d], B[d], chunk(it, d)
                        eng.wait_ge(ve.sem, ve.at("l", it))
                        eng.tensor_tensor(bf["L"], bf["L"], bcast(BT[:, c, 4 * d:4 * d + 4], P), ALU.mult).then_inc(*po.did("lb", it))
                        eng.wait_ge(po.sem, po.at("lb", it))
                        eng.tensor_tensor(bf["M0"], bf["L"], over(LVM[:, d, 0, :], HEADS), ALU.mult).then_inc(*po.did("lm0", it))
                    for d in DIRS:
                        ac, po, bf = ac_d[d], po_d[d], B[d]
                        eng.wait_ge(ac.sem, ac.at("eq", it))
                        eng.tensor_tensor(bf["QD"], bf["QD"], QT[:, :, cols(it, d)], ALU.mult).then_inc(*po.did("qd", it))
                    for v in LV:
                        for d in DIRS:
                            pe, ve, po, bf = pe_d[d], ve_d[d], po_d[d], B[d]
                            if v == 2:
                                eng.wait_ge(ve.sem, ve.at("x", it))
                            if v > 2:
                                eng.wait_ge(pe.sem, pe.at(f"r{v - 2}", it))
                            eng.tensor_tensor(bf[f"M{v % 2}"], bf["L"], over(LVM[:, d, v, :], HEADS), ALU.mult).then_inc(*po.did(f"lm{v}", it))

            part3 = pe_d + ve_d + ac_d + po_d

            h = Region(HT_AT, FIX_AT)
            SQ2 = [h.take(N) for _ in range(2)]
            RB2 = [h.take(N) for _ in range(2)]
            peH = steps("pe_head", ["t"], HEADS)
            acH = steps("ac_head", ["sq", "root"], HEADS)
            veH = steps("ve_head", ["inv", "mul", "gate"], HEADS)

            @program("pe")
            def _(eng):
                for i in range(HEADS):
                    eng.wait_ge(acH.sem, acH.at("sq", i))
                    if i == 0:
                        ended(eng, *part3)
                    if i >= 2:
                        eng.wait_ge(acH.sem, acH.at("root", i - 2))
                    for b, (a, n) in enumerate(CHUNKS):
                        m = eng.matmul(PS[:, 3 * (i % 2) + b, 0:n], ones, SQ2[i % 2][:, a:a + n], start=True, stop=True)
                    m.then_inc(*peH.did("t", i))

            @program("ac")
            def _(eng):
                ended(eng, *part3)
                eng.wait_ge(s_new, 32)
                for i in range(HEADS):
                    if i >= 2:
                        eng.wait_ge(peH.sem, peH.at("t", i - 2))
                    eng.activation(SQ2[i % 2], OT[:, i, :], ACT.Square).then_inc(*acH.did("sq", i))
                    eng.wait_ge(peH.sem, peH.at("t", i))
                    if i >= 2:
                        eng.wait_ge(veH.sem, veH.at("mul", i - 2))
                    eng.activation(RB2[i % 2], psum(3 * (i % 2), N), ACT.Sqrt, bias=eps, scale=1.0 / P).then_inc(*acH.did("root", i))

            @program("ve")
            def _(eng):
                ended(eng, *part3)
                for i in range(HEADS):
                    eng.wait_ge(acH.sem, acH.at("root", i))
                    eng.reciprocal(RB2[i % 2], RB2[i % 2]).then_inc(*veH.did("inv", i))
                    eng.wait_ge(veH.sem, veH.at("inv", i))
                    eng.tensor_tensor(QT[:, i, :], OT[:, i, :], RB2[i % 2], ALU.mult).then_inc(*veH.did("mul", i))
                    eng.wait_ge(veH.sem, veH.at("mul", i))
                    eng.scalar_tensor_tensor(QT[:, i, :], QT[:, i, :], vec("l0_dn_norm_w"), ZT[:, i, :], ALU.mult, ALU.mult).then_inc(*veH.did("gate", i))

            part4 = [peH, acH, veH]
            part5 = load_x("b", part3 + part4)
            rhs = [QT[:, i, :] for i in range(4)] + [PO[:, i, :] for i in range(4)]
            return part5 + project("0", A["l0_w_out"], rhs, WB, part3, part5 + part4, 0)

        def project(tag, weight, rhs, WB, w_free, prev, layer, x_back=None):
            s_w = [sem(f"out_landed{tag}{i}") for i in range(2)]
            pe = steps("pe_proj" + tag, ["t"], KD)
            ve = steps("ve_proj" + tag, ["s", "p"], KD)
            wv = weight.rearrange("(k p) n -> p k n", p=P)

            @program("sp")
            def _(eng):
                ended(eng, *w_free)
                for i in range(KD):
                    if i >= 2:
                        eng.wait_ge(pe.sem, pe.at("t", i - 2))
                    eng.dma_start(WB[i % 2], wv[:, :, i * P:(i + 1) * P]).then_inc(s_w[i % 2], 16)

            @program("pe")
            def _(eng):
                ended(eng, *prev)
                for i in range(KD):
                    eng.wait_ge(s_w[i % 2], 16 * (i // 2 + 1))
                    if i >= 2:
                        eng.wait_ge(ve.sem, ve.at("p", i - 2))
                    for k in range(KD):
                        for b, (a, n) in enumerate(CHUNKS):
                            m = eng.matmul(PS[:, 3 * (i % 2) + b, 0:n], WB[i % 2][:, k, :], rhs[k][:, a:a + n], start=k == 0, stop=k == KD - 1)
                    m.then_inc(*pe.did("t", i))

            X = cur["x"]

            @program("ve")
            def _(eng):
                ended(eng, *prev)
                if x_back:
                    eng.wait_ge(*x_back)
                for i in range(KD):
                    eng.wait_ge(pe.sem, pe.at("t", i))
                    for a, n, j in GROUPS:
                        at = 1536 * (i % 2) + a
                        eng.scalar_tensor_tensor(X[:, i, a:a + n], PSF[:, at:at + n], MOD[:, layer, 16 + i, j:j + 1],
                                                 X[:, i, a:a + n], ALU.mult, ALU.add).then_inc(*ve.did("sp"[j], i))
            return [pe, ve]

        def conv_glu(layer, before_norm, prev):
            r = Region(W_AT, 53200)
            HID = r.take(HALF, N)
            UW = [r.take(KD, 2 * P) for _ in range(2)]
            DW = [r.take(HALF, P) for _ in range(2)]
            GRID = (ROWS + 2) * (GRID_W + 2)
            PAD = [r.take(GRID + NP_ + 2) for _ in range(2)]
            CV = [r.take(N) for _ in range(2)]
            t = f"f{layer}"
            s_up = [sem(f"up_landed{layer}{i}") for i in range(2)]
            s_down = [sem(f"down_landed{layer}{i}") for i in range(2)]
            taps = [f"grid{i}" for i in range(9)] + [f"line{i}" for i in range(3)]
            pe = steps("pe_up" + t, ["a", "g"], KH)
            peD = steps("pe_down" + t, ["d"], 2 * KD)
            ac = steps("ac_" + t, ["grid", "line", "gelu"], KH)
            veZ = steps("ve_zero" + t, ["pad0", "pad1"])
            ve = steps("ve_" + t, taps + ["hid"], KH)
            veD = steps("ve_res" + t, ["s", "p"], 2 * KD)
            XT_, HT_ = cur["x"], cur["h"]
            up, down = A[f"l{layer}_ffn_up"], A[f"l{layer}_ffn_down"]
            w_name, b_name = f"l{layer}_ffn_conv_w", f"l{layer}_ffn_conv_b"

            @program("sp")
            def _(eng):
                ended(eng, *before_norm)
                upv = up.rearrange("(k p) n -> p k n", p=P)
                for j in range(KH + 2 * KD):
                    half = 0 if j < HALF + KD else 1
                    u = j - half * (HALF + KD)
                    if u < HALF:
                        i = half * HALF + u
                        if i >= 2:
                            eng.wait_ge(pe.sem, pe.at("g", i - 2))
                        for part in range(2):
                            at = part * HIDDEN + i * P
                            eng.dma_start(UW[i % 2][:, :, part * P:(part + 1) * P], upv[:, :, at:at + P]).then_inc(s_up[i % 2], 16)
                    else:
                        m = u - HALF
                        i = half * KD + m
                        if i >= 2:
                            eng.wait_ge(peD.sem, peD.at("d", i - 2))
                        src = down[half * HALF * P:(half + 1) * HALF * P, m * P:(m + 1) * P].rearrange("(k p) n -> p k n", p=P)
                        eng.dma_start(DW[i % 2], src).then_inc(s_down[i % 2], 16)

            @program("pe")
            def _(eng):
                ended(eng, *prev)
                for half in range(2):
                    for i in range(half * HALF, (half + 1) * HALF):
                        eng.wait_ge(s_up[i % 2], 32 * (i // 2 + 1))
                        for part, name in ((0, "a"), (1, "g")):
                            if i == HALF and half:
                                eng.wait_ge(veD.sem, veD.at("p", KD - 2 + part))
                            elif i:
                                who, what = ((ac, "line"), (ve, "hid"))[part]
                                eng.wait_ge(who.sem, who.at(what, i - 1))
                            for k in range(KD):
                                for b, (a, n) in enumerate(CHUNKS):
                                    m = eng.matmul(PS[:, 3 * part + b, 0:n], UW[i % 2][:, k, part * P:(part + 1) * P],
                                                   HT_[:, k, a:a + n], start=k == 0, stop=k == KD - 1)
                            m.then_inc(*pe.did(name, i))
                    eng.wait_ge(ve.sem, ve.at("hid", (half + 1) * HALF - 1))
                    for mm in range(KD):
                        i = half * KD + mm
                        eng.wait_ge(s_down[i % 2], 16 * (i // 2 + 1))
                        if mm >= 2:
                            eng.wait_ge(veD.sem, veD.at("p", i - 2))
                        for k in range(HALF):
                            for b, (a, n) in enumerate(CHUNKS):
                                m = eng.matmul(PS[:, 3 * (i % 2) + b, 0:n], DW[i % 2][:, k, :], HID[:, k, a:a + n],
                                               start=k == 0, stop=k == HALF - 1)
                        m.then_inc(*peD.did("d", i))

            @program("ac")
            def _(eng):
                for i in range(KH):
                    eng.wait_ge(pe.sem, pe.at("a", i))
                    if i >= 2:
                        eng.wait_ge(ve.sem, ve.at("line2", i - 2))
                    else:
                        eng.wait_ge(veZ.sem, veZ.end())
                    pad = PAD[i % 2]
                    inner = pad[:, 0:GRID].rearrange("p (r c) -> p r c", c=GRID_W + 2)[:, 1:ROWS + 1, 1:GRID_W + 1]
                    eng.activation(inner, psum(0, NS).rearrange("p (r c) -> p r c", c=GRID_W), ACT.Copy).then_inc(*ac.did("grid", i))
                    eng.activation(pad[:, GRID + 1:GRID + 1 + NP_], PSF[:, NS:N], ACT.Copy).then_inc(*ac.did("line", i))
                    eng.wait_ge(ve.sem, ve.at("line2", i))
                    eng.activation(CV[i % 2], CV[i % 2], ACT.Gelu_apprx_tanh).then_inc(*ac.did("gelu", i))

            @program("ve")
            def _(eng):
                ended(eng, *prev)
                for i in range(2):
                    eng.memset(PAD[i], 0.0).then_inc(*veZ.did(f"pad{i}"))
                for half in range(2):
                    for i in range(half * HALF, (half + 1) * HALF):
                        pad = PAD[i % 2]
                        grid = pad[:, 0:GRID].rearrange("p (r c) -> p r c", c=GRID_W + 2)
                        acc = CV[i % 2][:, 0:NS].rearrange("p (r c) -> p r c", c=GRID_W)
                        eng.wait_ge(ac.sem, ac.at("line", i))
                        for k in range(9):
                            w = vec(w_name, k * KH + i)
                            src = grid[:, k // 3:k // 3 + ROWS, k % 3:k % 3 + GRID_W]
                            if k == 0:
                                eng.tensor_scalar(acc, src, w, vec(b_name, i), ALU.mult, ALU.add).then_inc(*ve.did("grid0", i))
                            else:
                                eng.wait_ge(ve.sem, ve.at(f"grid{k - 1}", i))
                                eng.scalar_tensor_tensor(acc, src, w, acc, ALU.mult, ALU.add).then_inc(*ve.did(f"grid{k}", i))
                        for k in range(3):
                            w = vec(w_name, (3 + k) * KH + i)
                            src, dst = pad[:, GRID + k:GRID + k + NP_], CV[i % 2][:, NS:N]
                            if k == 0:
                                eng.tensor_scalar(dst, src, w, vec(b_name, i), ALU.mult, ALU.add).then_inc(*ve.did("line0", i))
                            else:
                                eng.wait_ge(ve.sem, ve.at(f"line{k - 1}", i))
                                eng.scalar_tensor_tensor(dst, src, w, dst, ALU.mult, ALU.add).then_inc(*ve.did(f"line{k}", i))
                        eng.wait_ge(ac.sem, ac.at("gelu", i))
                        eng.wait_ge(pe.sem, pe.at("g", i))
                        if i == HALF:
                            eng.wait_ge(peD.sem, peD.at("d", KD - 1))
                        eng.tensor_tensor(HID[:, i % HALF, :], CV[i % 2], psum(3, N), ALU.mult).then_inc(*ve.did("hid", i))
                    for mm in range(KD):
                        i = half * KD + mm
                        eng.wait_ge(peD.sem, peD.at("d", i))
                        for a, n, j in GROUPS:
                            at = 1536 * (i % 2) + a
                            eng.scalar_tensor_tensor(XT_[:, mm, a:a + n], PSF[:, at:at + n], MOD[:, layer, 40 + mm, j:j + 1],
                                                     XT_[:, mm, a:a + n], ALU.mult, ALU.add).then_inc(*veD.did("sp"[j], i))
            return [pe, peD, ac, veZ, ve, veD]

        def ffn_layer(layer, prev):
            before = prev
            prev = norm(f"2{layer}", prev, 2 * layer + 1, mod(layer, 3))
            return conv_glu(layer, before, prev)

        def mixer_hyena(before_norm, prev, spilled, spill):
            r = Region(W_AT, 53200)
            KT_, TT, HH = r.take(16, HC), r.take(16, HC), r.take(17, HC)
            ZTM, XTM = r.take(NT, HC), r.take(NT, HC)
            WB = [r.take(KD, P) for _ in range(2)]
            FW, IV, SP = r.take(25, P), r.take(25, P), r.take(4, P)
            NPOS = 2 * N
            HD = r.take(NPOS)
            W4 = r.take(4, HC)
            DELTA, BIAS = r.take(HC), r.take(2, HC)
            WIN = {"s": r.take(2, 16), "p": r.take(2, 4)}
            t = Region(W_AT + 16 * HC, W_AT + 32 * HC)
            PADN = N + 4
            PAD, CV = t.take(PADN), t.take(PADN)
            h = Region(W_AT, W_AT + 49 * HC)
            FEAT, ARG, TMP, RED, MLPW = h.take(NPOS), h.take(512), h.take(512), h.take(512), h.take(3, FFN64)
            Z2 = XT
            T_OF = {"s": NS // P, "p": NP_ // P}
            FIRST = {"s": 0, "p": NS // P}
            MAGIC = 1.5 * 2.0 ** 23
            TWO_PI_HI = 6.28125
            TWO_PI_LO = 2 * math.pi - TWO_PI_HI

            def mats(which, leaf):
                at = (FW, IV)[which]
                if leaf == 0:
                    return [[at[:, 0, :], at[:, 1, :]], [at[:, 2, :], at[:, 3, :]]]
                b = 4 + 3 * (leaf - 1)
                cos, sin, neg = at[:, b, :], at[:, b + 1, :], at[:, b + 2, :]
                return [[cos, sin], [neg, cos]] if which == 0 else [[cos, neg], [sin, cos]]

            s_k = sem("hyena_tables_landed")
            s_sp = sem("x_spilled")
            s_mlp = sem("mlp_landed")
            peM = steps("pe_mlp", ["t"], 15)
            veMl = steps("ve_mlp", ["arg", "turns", "whole", "hi", "lo", "clamp"], 15)
            acM = steps("ac_mlp", ["sin"], 15)
            vecs = {"fr": vec("l1_hy_freq"), "b": [vec("l1_hy_b1"), vec("l1_hy_b2"), vec("l1_hy_b3")]}

            @program("sp")
            def _(eng):
                ended(eng, *spilled)
                eng.dma_start(spill, XT).then_inc(s_sp, 16)
                ended(eng, *prev)
                eng.dma_start(FEAT[0:EMB, 0:2 * NS], A["k_feat_s"]).then_inc(s_mlp, 16)
                eng.dma_start(FEAT[0:EMB, 2 * NS:NPOS], A["k_feat_p"]).then_inc(s_mlp, 16)
                eng.dma_start(MLPW[0:EMB, 0, :], A["l1_hy_w1"]).then_inc(s_mlp, 16)
                eng.dma_start(MLPW[0:FFN64, 1, :], A["l1_hy_w2"]).then_inc(s_mlp, 16)
                eng.dma_start(MLPW[0:FFN64, 2, :], A["l1_hy_w3"]).then_inc(s_mlp, 16)
                for dst, name in ((FW, "k_fwd"), (IV, "k_inv8"), (SP, "k_spec"), (WIN["s"], "k_win_s"), (WIN["p"], "k_win_p")):
                    eng.dma_start(dst.rearrange("p a b -> p (a b)"), A[name]).then_inc(s_k, 16)

            @program("pe")
            def _(eng):
                ended(eng, *prev)
                eng.wait_ge(s_mlp, 80)
                for i in range(15):
                    layer, c = divmod(i, 5)
                    kk = EMB if layer == 0 else FFN64
                    src = FEAT if layer == 0 else HD
                    if i >= 5:
                        eng.wait_ge(acM.sem, acM.at("sin", i - 5))
                    if i >= 2:
                        eng.wait_ge(veMl.sem, veMl.at("arg", i - 2))
                    eng.matmul(PS[0:FFN64, i % 2, :], MLPW[0:kk, layer, :], src[0:kk, c * 512:(c + 1) * 512], start=True, stop=True).then_inc(*peM.did("t", i))

            @program("ve")
            def _(eng):
                ended(eng, *prev)
                lo, hi = slice(0, FFN64), (slice(0, FFN64), slice(None))
                for i in range(15):
                    layer, c = divmod(i, 5)
                    eng.wait_ge(peM.sem, peM.at("t", i))
                    if i:
                        eng.wait_ge(veMl.sem, veMl.at("clamp", i - 1))
                    eng.tensor_scalar(ARG[hi], PS[0:FFN64, i % 2, :], vecs["b"][layer][lo, :], vecs["fr"][lo, :], ALU.add, ALU.mult).then_inc(*veMl.did("arg", i))
                    eng.wait_ge(veMl.sem, veMl.at("arg", i))
                    eng.tensor_scalar(TMP[hi], ARG[hi], 1 / (2 * math.pi), MAGIC, ALU.mult, ALU.add).then_inc(*veMl.did("turns", i))
                    eng.wait_ge(veMl.sem, veMl.at("turns", i))
                    eng.tensor_scalar(TMP[hi], TMP[hi], MAGIC, None, ALU.subtract).then_inc(*veMl.did("whole", i))
                    eng.wait_ge(veMl.sem, veMl.at("whole", i))
                    eng.scalar_tensor_tensor(ARG[hi], TMP[hi], -TWO_PI_HI, ARG[hi], ALU.mult, ALU.add).then_inc(*veMl.did("hi", i))
                    eng.wait_ge(veMl.sem, veMl.at("hi", i))
                    if i:
                        eng.wait_ge(acM.sem, acM.at("sin", i - 1))
                    eng.scalar_tensor_tensor(RED[hi], TMP[hi], -TWO_PI_LO, ARG[hi], ALU.mult, ALU.add).then_inc(*veMl.did("lo", i))
                    eng.wait_ge(veMl.sem, veMl.at("lo", i))
                    eng.tensor_scalar(RED[hi], RED[hi], 3.1415925, -3.1415925, ALU.min, ALU.max).then_inc(*veMl.did("clamp", i))

            @program("ac")
            def _(eng):
                ended(eng, *prev)
                for i in range(15):
                    layer, c = divmod(i, 5)
                    eng.wait_ge(veMl.sem, veMl.at("clamp", i))
                    eng.activation(HD[0:FFN64, c * 512:(c + 1) * 512], RED[0:FFN64, :], ACT.Sin).then_inc(*acM.did("sin", i))

            mlp = [peM, veMl, acM]

            s_w = [sem(f"in1_landed{i}") for i in range(2)]
            s_c = sem("hyena_chunk_landed")
            n_p = 6 * NCH
            peW = steps("pe_in1", ["w", "t"], n_p)
            acW = steps("ac_in1", ["s", "p", "e"], n_p)
            veW = steps("ve_in1", ["c0", "c1", "c2"], n_p)
            veZ = steps("ve_zero1", ["pad"], 2 * NCH)
            jobs = 2 * NCH
            N_TREE = {"s": 20, "p": 0}
            N_INV = {"s": 29, "p": 1}
            PEJ, ACJ, VEJ, POJ = {}, {}, {}, {}
            for g in "sp":
                T, lv = T_OF[g], range(8 if g == "s" else 2)
                PEJ[g] = steps("pe_conv_" + g, [f"tap{b}" for b in range(T)] + [f"h{l}" for l in lv] + ["hx"] + [f"z{l}" for l in lv] + [f"i{l}" for l in lv], jobs)
                ACJ[g] = steps("ac_conv_" + g, [f"win{b}" for b in range(T)] + [f"h{l}" for l in lv] + ["hx"] + [f"iv{l}" for l in lv], jobs)
                VEJ[g] = steps("ve_conv_" + g, [f"k{b}" for b in range(T)] + ["bias", "r", "q"] + [f"ft{i}" for i in range(N_TREE[g])]
                               + [f"zt{i}" for i in range(N_TREE[g])] + sum([[f"t1{l}", f"t2{l}", f"t3{l}"] for l in lv], []) + ["t4"]
                               + [f"it{i}" for i in range(N_INV[g])] + ["gate"], jobs)
                POJ[g] = steps("po_conv_" + g, sum([[f"a{l}", f"b{l}"] for l in lv], []), jobs)
            peO = steps("pe_turn", ["t0", "t1"], NCH)
            acO = steps("ac_turn", ["t0", "t1"], NCH)

            def pair(ap, a, b, n=1):
                step = b - a
                v = ap[:, a:a + 2 * step, :].rearrange("p (u v) c -> p u v c", v=step)[:, :, 0:n, :]
                return v.rearrange("p u v c -> p u (v c)")

            def row(ap, a, n):
                return ap[:, a:a + n, :].rearrange("p a c -> p (a c)")

            def chain(eng, st, tag, rnd):
                n = [0]

                def run(f, *args, **kw):
                    if n[0]:
                        eng.wait_ge(st.sem, st.at(f"{tag}{n[0] - 1}", rnd))
                    f(*args, **kw).then_inc(*st.did(f"{tag}{n[0]}", rnd))
                    n[0] += 1
                return run

            def butterfly(eng, run, X, x0, x1r, x1i, m, th, tmp, plus, minus):
                c, s = math.cos(th), math.sin(th)
                S = KT_
                run(eng.scalar_tensor_tensor, row(S, tmp, m), x1r, c / s, x1i, ALU.mult, ALU.subtract)
                run(eng.scalar_tensor_tensor, row(S, tmp + m, m), x1i, c / s, x1r, ALU.mult, ALU.add)
                tv = row(S, tmp, 2 * m).rearrange("p (u c) -> p u c", u=2)
                run(eng.scalar_tensor_tensor, plus.rearrange("p (u c) -> p u c", u=2), tv, s, x0, ALU.mult, ALU.add)
                run(eng.scalar_tensor_tensor, minus.rearrange("p (u c) -> p u c", u=2), tv, -s, x0, ALU.mult, ALU.add)

            def tree(eng, st, tag, rnd, R, Q, r0, q0):
                run = chain(eng, st, tag, rnd)
                K = KT_
                run(eng.tensor_tensor, row(K, 0, 4), row(R, r0, 4), row(R, r0 + 4, 4), ALU.add)
                run(eng.tensor_tensor, row(K, 4, 4), row(R, r0, 4), row(R, r0 + 4, 4), ALU.subtract)
                run(eng.tensor_tensor, row(TT, 0, 2), row(K, 0, 2), row(K, 2, 2), ALU.add)
                run(eng.tensor_tensor, row(TT, 2, 2), row(K, 0, 2), row(K, 2, 2), ALU.subtract)
                butterfly(eng, run, K, pair(K, 4, 6), row(K, 5, 1), row(K, 7, 1), 1, math.pi / 4, 8, row(TT, 4, 2), row(TT, 6, 2))
                butterfly(eng, run, K, pair(Q, q0, q0 + 4, 2), row(Q, q0 + 2, 2), row(Q, q0 + 6, 2), 2, math.pi / 4, 8, row(K, 0, 4), row(K, 4, 4))
                butterfly(eng, run, K, pair(K, 0, 2), row(K, 1, 1), row(K, 3, 1), 1, math.pi / 8, 8, row(TT, 8, 2), row(TT, 10, 2))
                butterfly(eng, run, K, pair(K, 4, 6), row(K, 5, 1), row(K, 7, 1), 1, 5 * math.pi / 8, 8, row(TT, 12, 2), row(TT, 14, 2))

            def unfold(eng, run, a, b, m, th, tmp, out, dst0):
                c, s = math.cos(th), math.sin(th)
                split = lambda v: v.rearrange("p (u c) -> p u c", u=2)
                run(eng.tensor_tensor, pair(out, dst0, dst0 + 2 * m, m), split(a), split(b), ALU.add)
                run(eng.tensor_tensor, row(KT_, tmp, 2 * m), a, b, ALU.subtract)
                yr, yi = row(KT_, tmp, m), row(KT_, tmp + m, m)
                ur, ui = row(KT_, tmp + 2 * m, m), row(KT_, tmp + 3 * m, m)
                run(eng.scalar_tensor_tensor, ur, yr, c / s, yi, ALU.mult, ALU.add)
                run(eng.scalar_tensor_tensor, ui, yi, c / s, yr, ALU.mult, ALU.subtract)
                for k, u in ((0, ur), (1, ui)):
                    run(eng.tensor_scalar, row(out, dst0 + m + 2 * m * k, m), u, s, None, ALU.mult)

            def untree(eng, st, tag, rnd):
                run = chain(eng, st, tag, rnd)
                K, T = KT_, TT
                unfold(eng, run, row(T, 8, 2), row(T, 10, 2), 1, math.pi / 8, 8, K, 0)
                unfold(eng, run, row(T, 12, 2), row(T, 14, 2), 1, 5 * math.pi / 8, 8, K, 4)
                unfold(eng, run, row(K, 0, 4), row(K, 4, 4), 2, math.pi / 4, 8, T, 8)
                unfold(eng, run, row(T, 4, 2), row(T, 6, 2), 1, math.pi / 4, 8, K, 4)
                run(eng.tensor_tensor, row(K, 0, 2), row(T, 0, 2), row(T, 2, 2), ALU.add)
                run(eng.tensor_tensor, row(K, 2, 2), row(T, 0, 2), row(T, 2, 2), ALU.subtract)
                run(eng.tensor_tensor, row(T, 0, 4), row(K, 0, 4), row(K, 4, 4), ALU.add)
                run(eng.tensor_tensor, row(T, 4, 4), row(K, 0, 4), row(K, 4, 4), ALU.subtract)
                run(eng.tensor_tensor, row(T, 0, 8), row(T, 0, 8), row(T, 8, 8), ALU.add)

            w_in = A["l1_w_in"].rearrange("(k p) n -> p k n", p=P)

            def made(c):
                return [(6 * c + 2 * kind + half, kind, half, 8 * kind + 2 * c + half) for kind in range(3) for half in range(2)]

            def produce_pe(eng, c, which):
                for n, kind, half, col in made(c)[which]:
                    eng.wait_ge(s_w[n % 2], 16 * (n // 2 + 1))
                    first = n == made(c)[which][0][0]
                    if first:
                        start_of(eng, c, which)
                    else:
                        eng.wait_ge(acW.sem, acW.at("p", n - 1))
                    for k in range(KD):
                        for b, (a, w) in enumerate(CHUNKS):
                            m = eng.matmul(PS[:, b, 0:w], WB[n % 2][:, k, :], HT[:, k, a:a + w], start=k == 0, stop=k == KD - 1)
                    m.then_inc(*peW.did("w", n))
                    eng.wait_ge(veW.sem, veW.at("c2", n))
                    if not first:
                        eng.wait_ge(acW.sem, acW.at("e", n - 1))
                    for tt in range(NT):
                        at = 1 + tt * P + (2 if tt >= NS // P else 0)
                        m = eng.transpose(PS[:, 3 + tt // 4, (tt % 4) * P:(tt % 4 + 1) * P], CV[:, at:at + P], ident)
                    m.then_inc(*peW.did("t", n))

            def start_of(eng, c, which):
                if which.start:
                    eng.wait_ge(VEJ["p"].sem, VEJ["p"].at("gate", 2 * c))
                elif c:
                    eng.wait_ge(acO.sem, acO.at("t1", c - 1))
                    eng.wait_ge(VEJ["p"].sem, VEJ["p"].at("gate", 2 * c - 1))
                else:
                    ended(eng, *mlp)

            def produce_ac(eng, c, which):
                for n, kind, half, col in made(c)[which]:
                    eng.wait_ge(peW.sem, peW.at("w", n))
                    first = n == made(c)[which][0][0]
                    if first:
                        eng.wait_ge(veZ.sem, veZ.at("pad", 2 * c + (1 if which.start else 0)))
                    else:
                        eng.wait_ge(veW.sem, veW.at("c2", n - 1))
                    for a, w, j in GROUPS:
                        at = 1 + a + 2 * j
                        eng.activation(PAD[:, at:at + w], PSF[:, a:a + w], ACT.Copy).then_inc(*acW.did("sp"[j], n))
                    eng.wait_ge(peW.sem, peW.at("t", n))
                    dst = (ZTM if kind == 0 else XTM)[:, :, half * P:(half + 1) * P]
                    eng.activation(dst, psum(3, N).rearrange("p (t c) -> p t c", c=P), ACT.Copy).then_inc(*acW.did("e", n))

            def produce_ve(eng, c, which):
                rnd = 2 * c + (1 if which.start else 0)
                start_of(eng, c, which)
                eng.memset(PAD, 0.0).then_inc(*veZ.did("pad", rnd))
                for n, kind, half, col in made(c)[which]:
                    eng.wait_ge(acW.sem, acW.at("p", n))
                    if n != made(c)[which][0][0]:
                        eng.wait_ge(peW.sem, peW.at("t", n - 1))
                    for k in range(3):
                        wcol = vec("l1_hy_short_w", 24 * k + col)
                        src, dst = PAD[:, k:k + PADN - 2], CV[:, 1:PADN - 1]
                        if k:
                            eng.wait_ge(veW.sem, veW.at(f"c{k - 1}", n))
                            m = eng.scalar_tensor_tensor(dst, src, wcol, dst, ALU.mult, ALU.add)
                        else:
                            m = eng.tensor_scalar(dst, src, wcol, vec("l1_hy_short_b", col), ALU.mult, ALU.add)
                        m.then_inc(*veW.did(f"c{k}", n))

            def before_job(eng, c, order, g):
                if g == "p":
                    eng.wait_ge(VEJ["s"].sem, VEJ["s"].at("gate", 2 * c + order))
                else:
                    eng.wait_ge(acW.sem, acW.at("e", 6 * c + (5 if order else 3)))

            def lhs_pairs(eng, leaf, which, out, bank, rhs):
                M = mats(which, leaf)
                for o in range(2):
                    for i in range(2):
                        m = eng.matmul(PS[:, bank, o * HC:(o + 1) * HC], M[i][o], rhs[i], start=i == 0, stop=i == 1)
                return m

            def job_pe(eng, c, order, g):
                rnd, T = 2 * c + order, T_OF[g]
                pe, ac, ve, po = PEJ[g], ACJ[g], VEJ[g], POJ[g]
                n_l = 8 if g == "s" else 2
                before_job(eng, c, order, g)
                if order == 0 and g == "s":
                    eng.wait_ge(s_c, 48 * (c + 1))
                    if c == 0:
                        eng.wait_ge(s_k, 80)
                base = 0 if g == "s" else 2 * NS
                for b in range(T):
                    for u in range(2):
                        tap = 2 * b + u
                        m = eng.matmul(PS[:, b, u * HC:(u + 1) * HC], HD[0:FFN64, base + tap * P:base + (tap + 1) * P],
                                       W4[0:FFN64, 2 * (tap // T) + order, :], start=True, stop=True)
                    m.then_inc(*pe.did(f"tap{b}", rnd))
                eng.wait_ge(ve.sem, ve.at(f"ft{N_TREE[g] - 1}" if N_TREE[g] else "q", rnd))
                for l in range(n_l):
                    if l == 0:
                        for o, M in ((0, [FW[:, 0, :], FW[:, 2, :]]), (1, [SP[:, 0, :], SP[:, 2, :]])):
                            for i in range(2):
                                m = eng.matmul(PS[:, 0, o * HC:(o + 1) * HC], M[i], TT[:, i, :], start=i == 0, stop=i == 1)
                    else:
                        m = lhs_pairs(eng, l, 0, None, l, [TT[:, 2 * l, :], TT[:, 2 * l + 1, :]])
                    m.then_inc(*pe.did(f"h{l}", rnd))
                eng.wait_ge(ac.sem, ac.at("h0", rnd))
                for i in range(2):
                    m = eng.matmul(PS[:, 0, 0:HC], SP[:, 1 + 2 * i, :], TT[:, i, :], start=i == 0, stop=i == 1)
                m.then_inc(*pe.did("hx", rnd))
                if N_TREE[g]:
                    eng.wait_ge(ve.sem, ve.at(f"zt{N_TREE[g] - 1}", rnd))
                eng.wait_ge(ac.sem, ac.at("hx", rnd))
                for l in range(n_l):
                    rhs = [TT[:, 2 * l, :], TT[:, 2 * l + 1, :]] if g == "s" else [ZTM[:, NS // P + i, :] for i in range(2)]
                    lhs_pairs(eng, l, 0, None, l, rhs).then_inc(*pe.did(f"z{l}", rnd))
                for l in range(n_l):
                    eng.wait_ge(po.sem, po.at(f"b{l}", rnd))
                    lhs_pairs(eng, l, 1, None, l, [KT_[:, 2 * l, :], KT_[:, 2 * l + 1, :]]).then_inc(*pe.did(f"i{l}", rnd))

            def job_ac(eng, c, order, g):
                rnd, T = 2 * c + order, T_OF[g]
                pe, ac, ve, po = PEJ[g], ACJ[g], VEJ[g], POJ[g]
                n_l = 8 if g == "s" else 2
                before_job(eng, c, order, g)
                if order == 0 and g == "s":
                    eng.wait_ge(s_c, 48 * (c + 1))
                    if c == 0:
                        eng.wait_ge(s_k, 80)
                for b in range(T):
                    for u in range(2):
                        tap = 2 * b + u
                        m = eng.activation(KT_[:, tap, :], DELTA, ACT.Exp, scale=WIN[g][:, 0, tap:tap + 1], bias=WIN[g][:, 1, tap:tap + 1])
                    m.then_inc(*ac.did(f"win{b}", rnd))
                for l in range(n_l):
                    eng.wait_ge(pe.sem, pe.at(f"h{l}", rnd))
                    eng.activation(row(HH, 2 * l, 2), PS[:, l, :], ACT.Copy).then_inc(*ac.did(f"h{l}", rnd))
                eng.wait_ge(pe.sem, pe.at("hx", rnd))
                eng.activation(HH[:, 16, :], PS[:, 0, 0:HC], ACT.Copy).then_inc(*ac.did("hx", rnd))
                for l in range(n_l):
                    eng.wait_ge(pe.sem, pe.at(f"i{l}", rnd))
                    eng.activation(row(TT, 2 * l, 2), PS[:, l, :], ACT.Copy).then_inc(*ac.did(f"iv{l}", rnd))

            def job_po(eng, c, order, g):
                rnd = 2 * c + order
                ve, po = VEJ[g], POJ[g]
                for l in range(8 if g == "s" else 2):
                    eng.wait_ge(ve.sem, ve.at(f"t3{l}" if l else "t3" + "0", rnd))
                    eng.tensor_tensor(KT_[:, 2 * l, :], KT_[:, 2 * l, :], TT[:, 2 * l, :], ALU.subtract).then_inc(*po.did(f"a{l}", rnd))
                    if l == 0:
                        eng.wait_ge(ve.sem, ve.at("t4", rnd))
                    eng.tensor_tensor(KT_[:, 2 * l + 1, :], KT_[:, 2 * l + 1, :], TT[:, 2 * l + 1, :], ALU.add).then_inc(*po.did(f"b{l}", rnd))

            def job_ve(eng, c, order, g):
                rnd, T = 2 * c + order, T_OF[g]
                pe, ac, ve, po = PEJ[g], ACJ[g], VEJ[g], POJ[g]
                n_l = 8 if g == "s" else 2
                before_job(eng, c, order, g)
                for b in range(T):
                    eng.wait_ge(pe.sem, pe.at(f"tap{b}", rnd))
                    eng.wait_ge(ac.sem, ac.at(f"win{b}", rnd))
                    eng.tensor_tensor(row(KT_, 2 * b, 2), row(KT_, 2 * b, 2), PS[:, b, :], ALU.mult).then_inc(*ve.did(f"k{b}", rnd))
                eng.wait_ge(ve.sem, ve.at("k0", rnd))
                eng.tensor_tensor(KT_[0:1, 0, :], KT_[0:1, 0, :], BIAS[0:1, order, :], ALU.add).then_inc(*ve.did("bias", rnd))
                eng.wait_ge(ve.sem, ve.at("bias", rnd))
                eng.tensor_tensor(row(TT, 0, T), row(KT_, 0, T), row(KT_, T, T), ALU.add).then_inc(*ve.did("r", rnd))
                eng.tensor_tensor(row(TT, T, T), row(KT_, 0, T), row(KT_, T, T), ALU.subtract).then_inc(*ve.did("q", rnd))
                if g == "s":
                    eng.wait_ge(ve.sem, ve.at("q", rnd))
                    tree(eng, ve, "ft", rnd, TT, TT, 0, 8)
                    eng.wait_ge(pe.sem, pe.at("hx", rnd))
                    tree(eng, ve, "zt", rnd, ZTM, ZTM, 0, 0)
                t4_done = False
                order_l = range(n_l)
                for l in order_l:
                    eng.wait_ge(pe.sem, pe.at(f"z{l}", rnd))
                    if l == 0:
                        eng.wait_ge(ac.sem, ac.at("hx", rnd))
                    if l == 0:
                        eng.tensor_tensor(KT_[:, 0, :], PS[:, 0, 0:HC], HH[:, 0, :], ALU.mult).then_inc(*ve.did("t10", rnd))
                    else:
                        eng.tensor_tensor(KT_[:, 2 * l:2 * l + 2, :], PS[:, l, :].rearrange("p (u c) -> p u c", u=2), over(HH[:, 2 * l, :], 2), ALU.mult).then_inc(*ve.did(f"t1{l}", rnd))
                    eng.tensor_tensor(TT[:, 2 * l, :], PS[:, l, HC:2 * HC], HH[:, 2 * l + 1, :], ALU.mult).then_inc(*ve.did(f"t2{l}", rnd))
                    eng.tensor_tensor(TT[:, 2 * l + 1, :], PS[:, l, 0:HC], HH[:, 2 * l + 1, :], ALU.mult).then_inc(*ve.did(f"t3{l}", rnd))
                eng.tensor_tensor(KT_[:, 1, :], PS[:, 0, HC:2 * HC], HH[:, 16, :], ALU.mult).then_inc(*ve.did("t4", rnd))
                eng.wait_ge(ac.sem, ac.at(f"iv{n_l - 1}", rnd))
                f = FIRST[g]
                if g == "s":
                    untree(eng, ve, "it", rnd)
                    last = f"it{N_INV[g] - 1}"
                else:
                    eng.tensor_tensor(row(TT, 0, 2), row(TT, 0, 2), row(TT, 2, 2), ALU.add).then_inc(*ve.did("it0", rnd))
                    last = "it0"
                eng.wait_ge(ve.sem, ve.at(last, rnd))
                scale = 1.0 if g == "s" else 4.0
                eng.scalar_tensor_tensor(row(ZTM, f, T), row(TT, 0, T), scale, row(XTM, f, T), ALU.mult, ALU.mult).then_inc(*ve.did("gate", rnd))

            @program("sp")
            def _(eng):
                for c in range(NCH):
                    for n, kind, half, col in made(c):
                        if n >= 2:
                            eng.wait_ge(peW.sem, peW.at("w", n - 2))
                        eng.dma_start(WB[n % 2], w_in[:, :, col * P:(col + 1) * P]).then_inc(s_w[n % 2], 16)
                        if n % 6 == 1:
                            if c:
                                eng.wait_ge(VEJ["p"].sem, VEJ["p"].at("gate", 2 * c - 1))
                            else:
                                ended(eng, *mlp)
                            cs = slice(c * HC, (c + 1) * HC)
                            eng.dma_start(W4[0:FFN64, :, :], A["l1_hy_w4"].rearrange("k (a c) -> k a c", a=4)[:, :, cs]).then_inc(s_c, 16)
                            eng.dma_start(DELTA, A["k_delta"][0, cs].partition_broadcast(P)).then_inc(s_c, 16)
                            eng.dma_start(BIAS[0:1, :, :], A["l1_hy_bias"][:, cs].unsqueeze(0)).then_inc(s_c, 16)
                eng.wait_ge(peW.sem, peW.end())
                eng.wait_ge(s_sp, 16)
                eng.dma_start(HT, spill).then_inc(s_sp, 16)

            A_, B_ = slice(0, 4), slice(4, 6)

            def run_all(eng, produce, job, turn):
                for c in range(NCH):
                    if produce:
                        produce(eng, c, A_)
                    job(eng, c, 0, "s")
                    job(eng, c, 0, "p")
                    if produce:
                        produce(eng, c, B_)
                    job(eng, c, 1, "s")
                    job(eng, c, 1, "p")
                    if turn:
                        turn(eng, c)

            def turn_pe(eng, c):
                eng.wait_ge(VEJ["p"].sem, VEJ["p"].at("gate", 2 * c + 1))
                for half in range(2):
                    for tt in range(NT):
                        m = eng.transpose(PS[:, 3 * half + tt // 4, (tt % 4) * P:(tt % 4 + 1) * P], ZTM[:, tt, half * P:(half + 1) * P], ident)
                    m.then_inc(*peO.did(f"t{half}", c))

            def turn_ac(eng, c):
                if c == 0:
                    eng.wait_ge(s_sp, 16)
                for half in range(2):
                    eng.wait_ge(peO.sem, peO.at(f"t{half}", c))
                    eng.activation(Z2[:, 2 * c + half, :], psum(3 * half, N), ACT.Copy).then_inc(*acO.did(f"t{half}", c))

            @program("pe")
            def _(eng):
                run_all(eng, produce_pe, job_pe, turn_pe)

            @program("ac")
            def _(eng):
                run_all(eng, produce_ac, job_ac, turn_ac)

            @program("ve")
            def _(eng):
                run_all(eng, produce_ve, job_ve, None)

            @program("po")
            def _(eng):
                run_all(eng, None, job_po, None)

            done = [peW, acW, veW, peO, acO, veZ] + [x[g] for x in (PEJ, ACJ, VEJ, POJ) for g in "sp"]
            x_back = (s_sp, 32)
            return WB, Z2, done, x_back
        before = prev
        prev = norm("10", prev, 0, mod(0, 0))
        prev = mixer_even(before, prev)
        prev = ffn_layer(0, prev)
        before = prev
        spill = nc.dram_tensor("x_spill", (P, KD, N), F32, kind="Internal").ap()
        prev = norm("11", prev, 2, mod(1, 0))
        WBh, Z2, done, x_back = mixer_hyena(before, prev, before, spill)
        cur.update(x=HT, h=XT)
        prev = project("1", A["l1_w_out"], [Z2[:, k, :] for k in range(KD)], WBh, done, done, 1, x_back)
        prev = ffn_layer(1, prev)
        def store(prev, final):
            src = cur["h" if final else "x"]
            r = Region(W_AT, 53200)
            OR = [r.take(D) for _ in range(3)]
            pe = steps("pe_out", ["lo", "hi"], NT)
            ve = steps("ve_out", ["lo"], NT)
            ac = steps("ac_out", ["hi"], NT)
            s_o = [sem(f"stored{i}") for i in range(3)]

            @program("pe")
            def _(eng):
                ended(eng, *prev)
                for t in range(NT):
                    for half, who in ((0, ve), (1, ac)):
                        if t >= 4:
                            eng.wait_ge(who.sem, who.at(("lo", "hi")[half], t - 4))
                        for k in range(4):
                            m = eng.transpose(PS[:, (2 * t) % 8 + half, k * P:(k + 1) * P], src[:, 4 * half + k, t * P:(t + 1) * P], ident)
                        m.then_inc(*pe.did(("lo", "hi")[half], t))

            @program("ve")
            def _(eng):
                for t in range(NT):
                    eng.wait_ge(pe.sem, pe.at("lo", t))
                    if t >= 3:
                        eng.wait_ge(s_o[t % 3], 16 * (t // 3))
                    eng.tensor_copy(OR[t % 3][:, 0:512], PS[:, (2 * t) % 8, :]).then_inc(*ve.did("lo", t))

            @program("ac")
            def _(eng):
                for t in range(NT):
                    eng.wait_ge(pe.sem, pe.at("hi", t))
                    if t >= 3:
                        eng.wait_ge(s_o[t % 3], 16 * (t // 3))
                    eng.activation(OR[t % 3][:, 512:1024], PS[:, (2 * t) % 8 + 1, :], ACT.Copy).then_inc(*ac.did("hi", t))

            @program("sp")
            def _(eng):
                for t in range(NT):
                    eng.wait_ge(ve.sem, ve.at("lo", t))
                    eng.wait_ge(ac.sem, ac.at("hi", t))
                    dst = OUT["y_sample"][0, t * P:(t + 1) * P, :] if t < NS // P else OUT["y_prompt"][0, t * P - NS:(t + 1) * P - NS, :]
                    eng.dma_start(dst, OR[t % 3]).then_inc(s_o[t % 3], 16)
                for i in range(3):
                    eng.wait_ge(s_o[i], 16 * len(range(i, NT, 3)))

        prev = norm("f", prev, 4, None)
        store(prev, True)

        block = ctx.enter_context(nc.Block())

        @block.sync
        def _(eng):
            for f in progs["sp"]:
                f(eng)

        @block.tensor
        def _(eng):
            for f in progs["pe"]:
                f(eng)

        @block.vector
        def _(eng):
            for f in progs["ve"]:
                f(eng)

        @block.scalar
        def _(eng):
            for f in progs["ac"]:
                f(eng)

        @block.gpsimd
        def _(eng):
            for f in progs["po"]:
                f(eng)


_OUTS = {"y_prompt": (1, NP_, D), "y_sample": (1, NS, D), "new_f": (1, HEADS, P, P), "new_b": (1, HEADS, P, P)}


def kernel(**inputs):
    import concourse.bacc as bacc
    from concourse.bass_utils import run_bass_kernel_spmd

    nc = bacc.Bacc("TRN2", target_bir_lowering=False, num_devices=1)
    arrays, A, OUT = {}, {}, {}
    for name, a in {**inputs, **constants()}.items():
        a = np.ascontiguousarray(a)
        arrays[f"in_{name}"] = a
        A[name] = nc.dram_tensor(f"in_{name}", a.shape, mybir.dt.from_np(a.dtype), kind="ExternalInput").ap()
    for name, shape in _OUTS.items():
        OUT[name] = nc.dram_tensor(f"out_{name}", shape, F32, kind="ExternalOutput").ap()
    build(nc, A, OUT)
    r = run_bass_kernel_spmd(nc, [arrays], core_ids=[0])
    return tuple(r.results[0][f"out_{name}"] for name in _OUTS)
```

```python
import math
from contextlib import ExitStack

import concourse.bass as bass
import numpy as np
from concourse import mybir

F32 = mybir.dt.float32
F32R = mybir.dt.float32r
ALU = mybir.AluOpType
ACT = mybir.ActivationFunctionType

P = 128
D = 1024
KD = D // P
NS, NP_ = 1024, 256
N = NS + NP_
NT = N // P
GROUPS = [(0, NS, 0), (NS, NP_, 1)]
CHUNKS = [(0, 512), (512, 512), (1024, 256)]
EPS = 1e-6
HEADS = 4
GRID_W = 64
ROWS = NS // GRID_W
HIDDEN = 2816
KH = HIDDEN // P
HALF = KH // 2
WINDOWS = (2, 4, 8, 16)
MIX_IN = 2576
AB_AT = 2048
POOL_AT = 2064
BIG = 1e30
BASE, ARENA = 16512, 53200
FFN64 = 64
EMB = 33
HC = 256
NCH = D // HC
LEVELS = 7

VECTORS = [("l0_ada_b", 48), ("l0_norm1", 8), ("l0_norm2", 8), ("l0_dn_conv_w", 36), ("l0_dn_norm_w", 1),
           ("l0_pool_scale", 4), ("l0_ffn_conv_w", 198), ("l0_ffn_conv_b", 22), ("l1_ada_b", 48),
           ("l1_norm1", 8), ("l1_norm2", 8), ("l1_hy_short_w", 72), ("l1_hy_short_b", 24),
           ("l1_ffn_conv_w", 198), ("l1_ffn_conv_b", 22), ("final_norm", 8),
           ("l1_hy_freq", 1), ("l1_hy_b1", 1), ("l1_hy_b2", 1), ("l1_hy_b3", 1)]
VCOL, _at = {}, 0
for _n, _r in VECTORS:
    VCOL[_n] = _at
    _at += _r
VTILES = -(-_at // P)

SQUARES = {"ident": 0, "ones": 1, "cum_f": 2, "cum_b": 3, "mA_f": 4, "mB_f": 5, "mA_b": 6, "mB_b": 7}


def constants():
    i = np.arange(P)
    r, c = i[:, None], i[None, :]
    sq = np.zeros((P, 8, P))
    sq[:, 0] = r == c
    sq[:, 1] = 1
    sq[:, 2] = r <= c
    sq[:, 3] = r >= c
    sq[:, 4] = np.where(c < r, 0, BIG)
    sq[:, 5] = np.where(c >= r, 0, -BIG)
    sq[:, 6] = np.where(c > r, 0, BIG)
    sq[:, 7] = np.where(c <= r, 0, -BIG)
    level = np.zeros((P, 2, LEVELS, P))
    for v in range(LEVELS):
        b = 1 << v
        m = (r // (2 * b) == c // (2 * b)) & ((r // b) % 2 == 1) & ((c // b) % 2 == 0)
        level[:, 0, v], level[:, 1, v] = m, m.T
    inv = np.zeros((4, N))
    for g, w in enumerate(WINDOWS):
        for a, n, _ in GROUPS:
            t = np.arange(n)
            inv[g, a:a + n] = 1.0 / (np.clip(t + w - w // 2, 0, n) - np.clip(t - w // 2, 0, n))
    out = {"k_squares": sq.reshape(P, -1), "k_level": level.reshape(P, -1), "k_inv": inv}

    for name, L in (("s", NS), ("p", NP_)):
        T = L // P
        pos = np.concatenate([np.arange(L), L - np.arange(L)]).astype(np.float32)
        t01 = (pos / np.float32(L - 1)).astype(np.float32)
        bands = np.linspace(1e-4, 15, 16, dtype=np.float32)
        ang = (np.float32(2.0 * math.pi / L) * pos[:, None] * bands[None, :]).astype(np.float32)
        feat = np.concatenate([t01[:, None], np.cos(ang), -np.sin(ang)], axis=-1)
        out["k_feat_" + name] = feat.T
        cols = np.zeros((P, 2, 2 * T))
        cols[:, 0] = -t01.reshape(2 * T, P).T
        cols[0, 1, T] = -1e4
        out["k_win_" + name] = cols.reshape(P, -1)
    lo, hi = math.log(1e-2) / 1.5, math.log(1e-2) / 0.3
    out["k_delta"] = np.abs(np.linspace(lo, hi, D, dtype=np.float32))[None, :]

    fwd, inv8, spec = np.zeros((P, 8, 2, 2, P)), np.zeros((P, 8, 2, 2, P)), np.zeros((P, 2, 2, P))
    n = j = np.arange(128.0)
    for leaf, th in enumerate(LEAF_ANGLES):
        if leaf == 0:
            for half in range(2):
                m = n + 128 * half
                a = 2 * math.pi * np.outer(m, j) / 256
                alt = (-1.0) ** m
                fwd[:, 0, half, 0] = np.cos(a)
                fwd[:, 0, half, 1] = np.sin(a)
                fwd[:, 0, half, 1, 0] = alt
                spec[:, half, 0] = np.sin(a)
                spec[:, half, 0, 0] = 0
                spec[:, half, 1] = np.cos(a)
                spec[:, half, 1, 0] = alt
                ci, si = np.cos(a).T / 128, np.sin(a).T / 128
                ci[0], si[0] = 1 / 256, alt / 256
                inv8[:, 0, 0, half], inv8[:, 0, 1, half] = ci / 8, si / 8
            continue
        a = np.outer(n, (th + 2 * math.pi * j) / 128)
        fwd[:, leaf, 0, 0], fwd[:, leaf, 1, 0] = np.cos(a), -np.sin(a)
        fwd[:, leaf, 0, 1], fwd[:, leaf, 1, 1] = np.sin(a), np.cos(a)
        b = a.T
        inv8[:, leaf, 0, 0], inv8[:, leaf, 1, 0] = np.cos(b) / 1024, np.sin(b) / 1024
        inv8[:, leaf, 0, 1], inv8[:, leaf, 1, 1] = -np.sin(b) / 1024, np.cos(b) / 1024
    def packed(m, sin, neg):
        rest = np.stack([m[:, 1:, 0, 0], m[:, 1:, sin[0], sin[1]], m[:, 1:, neg[0], neg[1]]], axis=2)
        return np.concatenate([m[:, 0].reshape(P, -1), rest.reshape(P, -1)], axis=1)
    out["k_fwd"], out["k_inv8"] = packed(fwd, (0, 1), (1, 0)), packed(inv8, (1, 0), (0, 1))
    out["k_spec"] = spec.reshape(P, -1)
    return {k: np.ascontiguousarray(v, dtype=np.float32) for k, v in out.items()}


LEAF_ANGLES = [0.0, math.pi / 2, math.pi / 4, 5 * math.pi / 4, math.pi / 8, 9 * math.pi / 8,
               5 * math.pi / 8, 13 * math.pi / 8]


class Steps:

    def __init__(self, sem, names, rounds=1, before=0):
        self.sem, self.names, self.rounds, self.before = sem, list(names), rounds, before
        self.index = {s: i for i, s in enumerate(self.names)}
        assert len(self.index) == len(self.names)
        self.made = 0

    def at(self, step, round_=0):
        return self.before + round_ * len(self.names) + self.index[step] + 1

    def end(self):
        return self.before + self.rounds * len(self.names)

    def did(self, step, round_=0):
        self.made += 1
        assert self.before + self.made == self.at(step, round_), (self.names, step, round_, self.made)
        return self.sem, 1


def build(nc, A, OUT):
    with ExitStack() as ctx:
        def sem(name):
            return ctx.enter_context(nc.semaphore(name))

        pieces = []
        PS = ctx.enter_context(nc.psum_tensor("PS", [P, 8, 512], F32))
        PSF = PS[:, :, :].rearrange("p b n -> p (b n)")

        class Region:

            def __init__(self, a, b):
                self.a, self.b = a, b

            def take(self, *shape, dtype=F32):
                n = math.prod(shape)
                self.a = -(-self.a // 8) * 8
                assert self.a + n <= self.b, (self.a, n, self.b)
                pieces.append(nc.alloc_sbuf_tensor_at(f"piece{len(pieces)}", [P, n], dtype, offset=BASE + 4 * self.a))
                v = pieces[-1][:, :]
                self.a += n
                if len(shape) == 2:
                    v = v.rearrange("p (a b) -> p a b", b=shape[1])
                if len(shape) == 3:
                    v = v.rearrange("p (a b c) -> p a b c", b=shape[1], c=shape[2])
                return v

            def half(self, *shape):
                v = self.take(*shape, dtype=F32R)
                return v, v.bitcast(F32)

        XT_AT, HT_AT, FIX_AT, W_AT = 0, KD * N, 3 * KD * N, 3 * KD * N + 1400
        XT = Region(XT_AT, HT_AT).take(KD, N)
        hr = Region(HT_AT, FIX_AT)
        (HH, HH32), (HL, HL32) = hr.half(KD, N), hr.half(KD, N)
        fix = Region(FIX_AT, W_AT)
        VC = fix.take(VTILES * P)
        ident = fix.take(P)
        ones = fix.take(P)
        MOD = fix.take(2, 48, 2)
        SCALE_A = fix.take(5, KD, 2)
        eps = fix.take(1)
        half_pi = fix.take(1)
        CS = fix.take(KD, 2)

        def vec(name, i=0, n=1):
            return VC[:, VCOL[name] + i:VCOL[name] + i + n]

        def psum(bank, n):
            return PSF[:, bank * 512:bank * 512 + n]

        def bcast(ap, n):
            return ap.unsqueeze(2).to_broadcast([P, ap.shape[1], n])

        def over(ap, n):
            return ap.unsqueeze(1).to_broadcast([P, n, ap.shape[1]])

        everything = []

        used = {}

        def steps(name, names, rounds=1):
            handle, before = used.get(name) or (sem(name), 0)
            s = Steps(handle, names, rounds, before)
            used[name] = handle, s.end()
            everything.append(s)
            return s

        landings = {}

        class Landing:

            def __init__(self, name, count):
                self.sem, self.before = landings.get(name) or (sem(name), 0)
                landings[name] = self.sem, self.before + 16 * count

            def at(self, k):
                return self.sem, self.before + 16 * k

        def ended(eng, *which):
            for s in which:
                eng.wait_ge(s.sem, s.end())

        progs = {"sp": [], "pe": [], "ve": [], "ac": [], "po": []}

        def program(engine):
            def add(f):
                progs[engine].append(f)
                return f
            return add

        w = Region(W_AT, ARENA)
        VR = w.take(VTILES, P)
        s_const, s_rows, s_cond = sem("const_landed"), sem("vector_rows_landed"), sem("cond_landed")
        ve0 = steps("ve_setup", ["zero_rows", "eps", "half_pi", "pair"])
        pe0 = steps("pe_setup", ["turn0", "turn1"])
        ac0 = steps("ac_setup", ["cols0", "cols1", "silu"])
        CR = w.take(2, KD)
        nvec = [0]

        @program("sp")
        def _(sp):
            for dst, k in ((ident, 0), (ones, 1)):
                sp.dma_start(dst, A["k_squares"][:, k * P:(k + 1) * P]).then_inc(s_const, 16)
            for j, name in enumerate(("c", "c_ctx")):
                src = A[name].rearrange("a b -> (a b)") if name == "c" else A[name]
                sp.dma_start(CR[:, j, :], src.rearrange("(p k) -> p k", p=P)).then_inc(s_cond, 16)
            sp.wait_ge(ve0.sem, ve0.at("zero_rows"))
            for name, rows in VECTORS:
                src = A[name]
                src = src if len(src.shape) == 1 else (src.rearrange("a b -> (a b)") if len(src.shape) == 2 else src.rearrange("a b c -> (a b c)"))
                width = min(P, src.shape[0])
                src = src.rearrange("(r c) -> r c", c=width)
                at, done = VCOL[name], 0
                while done < rows:
                    n = min(rows - done, P - at % P)
                    sp.dma_start(VR[at % P:at % P + n, at // P, 0:width], src[done:done + n, :]).then_inc(s_rows, 16)
                    nvec[0] += 1
                    done += n
                    at += n

        @program("pe")
        def _(pe):
            pe.wait_ge(s_const, 32)
            pe.wait_ge(s_rows, 16 * nvec[0])
            for half in range(2):
                for t in range(3):
                    m = pe.transpose(PS[:, half, t * P:(t + 1) * P], VR[:, 3 * half + t, :], ident)
                m.then_inc(*pe0.did(f"turn{half}"))

        @program("ve")
        def _(ve):
            ve.memset(VR, 0.0).then_inc(*ve0.did("zero_rows"))
            ve.memset(eps, EPS).then_inc(*ve0.did("eps"))
            ve.memset(half_pi, math.pi / 2).then_inc(*ve0.did("half_pi"))
            ve.wait_ge(s_cond, 32)
            ve.tensor_copy(CS.rearrange("p k j -> p j k"), CR).then_inc(*ve0.did("pair"))

        @program("ac")
        def _(ac):
            for half in range(2):
                ac.wait_ge(pe0.sem, pe0.at(f"turn{half}"))
                ac.activation(VC[:, half * 384:(half + 1) * 384], PS[:, half, 0:384], ACT.Copy)\
                    .then_inc(*ac0.did(f"cols{half}"))
            ac.wait_ge(ve0.sem, ve0.at("pair"))
            ac.activation(CS, CS, ACT.Silu).then_inc(*ac0.did("silu"))

        w = Region(W_AT + 1024, ARENA)
        AW = [w.take(KD, 512) for _ in range(2)]
        AR = [w.take(512) for _ in range(2)]
        NA = 24
        s_aw = [sem(f"ada_w_landed{i}") for i in range(2)]
        peA = steps("pe_ada", ["rows", "turn"], NA)
        veA = steps("ve_ada", ["rows"], NA)
        veM = steps("ve_mod", ["mod0", "mod1"] + [f"plus{i}" for i in range(4)] + [f"scale{i}" for i in range(5)])

        @program("sp")
        def _(sp):
            for n in range(NA):
                if n >= 2:
                    sp.wait_ge(peA.sem, peA.at("rows", n - 2))
                layer, m = divmod(n, 12)
                src = A[f"l{layer}_ada_w"].rearrange("(p k) n -> p k n", k=KD)[:, :, m * 512:(m + 1) * 512]
                sp.dma_start(AW[n % 2], src).then_inc(s_aw[n % 2], 16)

        @program("pe")
        def _(pe):
            pe.wait_ge(ac0.sem, ac0.at("silu"))
            for n in range(NA):
                pe.wait_ge(s_aw[n % 2], 16 * (n // 2 + 1))
                if n >= 2:
                    pe.wait_ge(veA.sem, veA.at("rows", n - 2))
                for k in range(KD):
                    m = pe.matmul(PS[0:2, 2 + n % 2, :], CS[:, k, :], AW[n % 2][:, k, :], start=k == 0, stop=k == KD - 1)
                m.then_inc(*peA.did("rows", n))
                pe.wait_ge(veA.sem, veA.at("rows", n))
                for j in range(4):
                    c = (4 * n + j) * 2
                    m = pe.transpose(PS[:, 4, c:c + 2], AR[n % 2][0:2, j * P:(j + 1) * P], ident[0:2, 0:2])
                m.then_inc(*peA.did("turn", n))

        @program("ve")
        def _(ve):
            for n in range(NA):
                ve.wait_ge(peA.sem, peA.at("rows", n))
                if n >= 2:
                    ve.wait_ge(peA.sem, peA.at("turn", n - 2))
                ve.tensor_copy(AR[n % 2][0:2, :], PS[0:2, 2 + n % 2, :]).then_inc(*veA.did("rows", n))
            ve.wait_ge(peA.sem, peA.at("turn", NA - 1))
            ve.wait_ge(ac0.sem, ac0.at("cols1"))
            for layer in range(2):
                ve.tensor_tensor(MOD[:, layer], PS[:, 4, 96 * layer:96 * layer + 96].rearrange("p (m j) -> p m j", j=2),
                                 bcast(vec(f"l{layer}_ada_b", 0, 48), 2), ALU.add).then_inc(*veM.did(f"mod{layer}"))
            ve.wait_ge(veM.sem, veM.at("mod1"))
            for i in range(4):
                layer, second = divmod(i, 2)
                at = 8 + 24 * second
                ve.tensor_scalar(SCALE_A[:, i], MOD[:, layer, at:at + 8, :], 1.0, None, ALU.add)\
                    .then_inc(*veM.did(f"plus{i}"))
            ve.wait_ge(veM.sem, veM.at("plus3"))
            for i in range(4):
                layer, second = divmod(i, 2)
                ve.tensor_tensor(SCALE_A[:, i], SCALE_A[:, i], bcast(vec(f"l{layer}_norm{second + 1}", 0, 8), 2),
                                 ALU.mult).then_inc(*veM.did(f"scale{i}"))
            ve.tensor_copy(SCALE_A[:, 4], bcast(vec("final_norm", 0, 8), 2)).then_inc(*veM.did("scale4"))

        prev = [pe0, ve0, ac0, peA, veA, veM]

        def load_x(prev, r):
            XR = [r.take(D) for _ in range(3)]
            s_x = [Landing(f"x_landed{i}", len(range(i, NT, 3))) for i in range(3)]
            pe = steps("pe_x", ["lo", "hi"], NT)
            ve = steps("ve_x", ["lo"], NT)
            ac = steps("ac_x", ["hi"], NT)

            @program("sp")
            def _(sp):
                ended(sp, *prev)
                for t in range(NT):
                    if t >= 3:
                        sp.wait_ge(pe.sem, pe.at("hi", t - 3))
                    src = A["x_sample"][0, t * P:(t + 1) * P, :] if t < NS // P else A["x_prompt"][0, t * P - NS:(t + 1) * P - NS, :]
                    sp.dma_start(XR[t % 3], src).then_inc(s_x[t % 3].sem, 16)

            @program("pe")
            def _(eng):
                ended(eng, *prev)
                for t in range(NT):
                    eng.wait_ge(*s_x[t % 3].at(t // 3 + 1))
                    for half, who in ((0, ve), (1, ac)):
                        b = (2 * t) % 8 + half
                        if t >= 4:
                            eng.wait_ge(who.sem, who.at(("lo", "hi")[half], t - 4))
                        for k in range(4):
                            kk = 4 * half + k
                            m = eng.transpose(PS[:, b, k * P:(k + 1) * P], XR[t % 3][:, kk * P:(kk + 1) * P], ident)
                        m.then_inc(*pe.did(("lo", "hi")[half], t))

            @program("ve")
            def _(eng):
                ended(eng, *prev)
                for t in range(NT):
                    eng.wait_ge(pe.sem, pe.at("lo", t))
                    eng.tensor_copy(XT[:, 0:4, t * P:(t + 1) * P], PS[:, (2 * t) % 8, :].rearrange("p (k t) -> p k t", t=P))\
                        .then_inc(*ve.did("lo", t))

            @program("ac")
            def _(eng):
                ended(eng, *prev)
                for t in range(NT):
                    eng.wait_ge(pe.sem, pe.at("hi", t))
                    eng.activation(XT[:, 4:8, t * P:(t + 1) * P], PS[:, (2 * t) % 8 + 1, :].rearrange("p (k t) -> p k t", t=P), ACT.Copy)\
                        .then_inc(*ac.did("hi", t))
            return [pe, ve, ac]

        prev = load_x(prev, Region(HT_AT, FIX_AT))

        def norm(prev, which, shift):
            r = Region(W_AT, W_AT + 5 * N)
            SQ = [r.take(N) for _ in range(2)]
            T = [r.take(N) for _ in range(2)]
            RS = r.take(N)
            ac = steps("ac_norm", ["sq"], KD)
            ac2 = steps("ac_norm_r", ["root"])
            ac3 = steps("ac_norm_m", ["hi"], KD)
            pe = steps("pe_norm", ["sum"], KD)
            ve = steps("ve_norm_r", ["inv"])
            ve2 = steps("ve_norm", ["mul", "s", "p"], KD)
            po = steps("po_norm", ["lo"], KD)

            @program("pe")
            def _(eng):
                ended(eng, *prev)
                for k in range(KD):
                    eng.wait_ge(ac.sem, ac.at("sq", k))
                    for b, (a, n) in enumerate(CHUNKS):
                        m = eng.matmul(PS[:, b, 0:n], ones, SQ[k % 2][:, a:a + n], start=k == 0, stop=k == KD - 1)
                    m.then_inc(*pe.did("sum", k))

            @program("ac")
            def _(eng):
                ended(eng, *prev)
                for k in range(KD):
                    if k >= 2:
                        eng.wait_ge(pe.sem, pe.at("sum", k - 2))
                    eng.activation(SQ[k % 2], XT[:, k, :], ACT.Square).then_inc(*ac.did("sq", k))
                eng.wait_ge(pe.sem, pe.end())
                eng.activation(RS, psum(0, N), ACT.Sqrt, scale=1.0 / D, bias=eps).then_inc(*ac2.did("root"))
                for k in range(KD):
                    eng.wait_ge(ve2.sem, ve2.at("p", k))
                    eng.activation(HH[:, k, :], T[k % 2], ACT.Copy).then_inc(*ac3.did("hi", k))

            @program("ve")
            def _(eng):
                eng.wait_ge(ac2.sem, ac2.at("root"))
                eng.reciprocal(RS, RS).then_inc(*ve.did("inv"))
                eng.wait_ge(ve.sem, ve.at("inv"))
                for k in range(KD):
                    if k >= 2:
                        eng.wait_ge(po.sem, po.at("lo", k - 2))
                    eng.tensor_tensor(T[k % 2], XT[:, k, :], RS, ALU.mult).then_inc(*ve2.did("mul", k))
                    eng.wait_ge(ve2.sem, ve2.at("mul", k))
                    for (a, n, j), g in zip(GROUPS, ("s", "p")):
                        eng.tensor_scalar(T[k % 2][:, a:a + n], T[k % 2][:, a:a + n], SCALE_A[:, which, k, j:j + 1],
                                          shift(k, j), ALU.mult, ALU.add).then_inc(*ve2.did(g, k))

            @program("po")
            def _(eng):
                for k in range(KD):
                    eng.wait_ge(ac3.sem, ac3.at("hi", k))
                    eng.tensor_tensor(HL[:, k, :], T[k % 2], HH32[:, k, :], ALU.subtract).then_inc(*po.did("lo", k))
            return [pe, ac, ac2, ac3, ve, ve2, po]


        def weight_ring(region, count):
            RAW = [region.take(1024) for _ in range(2)]
            HI = [region.half(1024) for _ in range(2)]
            LO = [region.half(1024) for _ in range(2)]

            class Ring:
                landed = [Landing(f"w_landed{i}", len(range(i, count, 2))) for i in range(2)]
                pe = steps("pe_w", ["used"], count)
                ac = steps("ac_w", ["hi"], count)
                po = steps("po_w", ["lo"], count)

                def load(self, eng, i, src, shape):
                    if i >= 2:
                        eng.wait_ge(self.po.sem, self.po.at("lo", i - 2))
                        eng.wait_ge(self.ac.sem, self.ac.at("hi", i - 2))
                    eng.dma_start(self.view(RAW[i % 2], shape), src).then_inc(self.landed[i % 2].sem, 16)

                def view(self, slot, shape):
                    return slot[:, 0:shape[0] * shape[1]].rearrange("p (a b) -> p a b", b=shape[1])

                def hi(self, eng, i, n=1024):
                    if i >= count:
                        return
                    eng.wait_ge(*self.landed[i % 2].at(i // 2 + 1))
                    if i >= 2:
                        eng.wait_ge(self.pe.sem, self.pe.at("used", i - 2))
                    eng.activation(HI[i % 2][0][:, 0:n], RAW[i % 2][:, 0:n], ACT.Copy).then_inc(*self.ac.did("hi", i))

                def lo(self, eng, i, n=1024):
                    if i >= count:
                        return
                    eng.wait_ge(self.ac.sem, self.ac.at("hi", i))
                    eng.tensor_tensor(LO[i % 2][0][:, 0:n], RAW[i % 2][:, 0:n], HI[i % 2][1][:, 0:n], ALU.subtract)\
                        .then_inc(*self.po.did("lo", i))

                def ready(self, eng, i):
                    eng.wait_ge(self.po.sem, self.po.at("lo", i))

                def get(self, i, shape):
                    return self.view(HI[i % 2][0], shape), self.view(LO[i % 2][0], shape)
            return Ring()

        def product(eng, bank, weights, halves_of, first, last):
            wh, wl = weights
            xh, xl = halves_of
            for n_, (w, x) in enumerate(((wh, xh), (wh, xl), (wl, xh))):
                for b, (a, n) in enumerate(CHUNKS):
                    m = eng.matmul(PS[:, bank + b, 0:n], w, x[:, a:a + n], start=first and n_ == 0, stop=last and n_ == 2)
            return m

        def mod(layer, part):
            return lambda k, j: MOD[:, layer, 8 * part + k, j:j + 1]

        def mixer_even(before_norm, prev):
            x_r = Region(XT_AT, HT_AT)
            PO, KT = x_r.take(HEADS, N), x_r.take(HEADS, N)
            r = Region(W_AT, ARENA)
            QT, VT = r.take(HEADS, N), r.take(HEADS, N)
            late = Region(r.a, r.a + 8712)
            ring_at = Region(r.a, r.a + 6144)
            r.a += 6144
            PADN = N + 4
            PAD, CV = r.take(PADN), r.take(PADN)
            POW, ABW = r.take(4, P), r.take(KD, 16)
            ABS, GG, BT, TA = r.take(NT, 16), r.take(NT, 8), r.take(NT, 8), r.take(NT, 8)
            DTB, ALOG = r.take(8), r.take(8)
            ABH, ABL = r.half(KD, 16), r.half(KD, 16)
            SQM, LVM = late.take(6, P), late.take(2, LEVELS, P)
            OT = Region(XT_AT, HT_AT).take(HEADS, N)
            top = Region(W_AT, W_AT + 2 * HEADS * N)
            GAP = 8
            WU = GAP + NS + GAP + NP_ + GAP
            UPAD, PA, PB, INV = top.take(WU), top.take(WU), top.take(WU), top.take(N)
            h = Region(HT_AT, HT_AT + HEADS * N)
            SQ = [h.take(N) for _ in range(2)]
            RB = [h.take(N) for _ in range(2)]
            z_dram = nc.dram_tensor("z_gate", (HEADS, P, N), F32, kind="Internal").ap()
            s_z = [sem(f"z_stored{i}") for i in range(2)]
            w_in = A["l0_w_in"].rearrange("(k p) n -> p k n", p=P)
            tiles = [("pool", g, POOL_AT + g * P) for g in range(4)]
            for kind, at in (("k", 512), ("q", 0), ("v", 1024), ("z", 1536)):
                tiles += [(kind, g, at + g * P) for g in range(HEADS)]
            n_t = len(tiles)
            dest = {"q": QT, "k": KT, "v": VT}
            pos = {"q": 0, "k": 4, "v": 8}
            ring = weight_ring(ring_at, n_t)
            s_small, s_mask, s_inv = sem("mix0_small_landed"), sem("masks_landed"), sem("inv_landed")
            pe = ring.pe
            acB, poB = steps("ac_abw", ["hi"]), steps("po_abw", ["lo"])
            peAB = steps("pe_ab", ["ab"])
            ac = steps("ac_in0", ["s", "p"], n_t)
            acS = steps("ac_silu0", ["s", "p"], 12)
            veZ = steps("ve_zero0", ["pad", "upad"])
            ve_names, doubled = [], {}
            for g, w in enumerate(WINDOWS):
                doubled[g] = int(math.log2(w))
                ve_names += [f"pool{g}.d{i}" for i in range(doubled[g])] + [f"pool{g}.m{j}" for j in "sp"] + [f"pool{g}.u{j}" for j in "sp"]
            ve_names += [f"conv{i}.{k}" for i in range(12) for k in range(3)]
            ve = steps("ve_in0", ve_names)

            @program("sp")
            def _(eng):
                ended(eng, *prev)
                for i, (kind, g, at) in enumerate(tiles):
                    ring.load(eng, i, w_in[:, :, at:at + P], (KD, P))
                    if i == 1:
                        eng.dma_start(POW, A["l0_pool_w"].rearrange("g i o -> i g o")).then_inc(s_small, 16)
                        eng.dma_start(ABW, w_in[:, :, AB_AT:AB_AT + 16]).then_inc(s_small, 16)
                        for dst, name in ((DTB, "l0_dn_dt_bias"), (ALOG, "l0_dn_a_log")):
                            eng.dma_start(dst, A[name].rearrange("a b -> (a b)").partition_broadcast(P)).then_inc(s_small, 16)
                    if i < 4:
                        if i:
                            eng.wait_ge(ve.sem, ve.at(f"pool{i - 1}.mp"))
                        else:
                            ended(eng, *prev)
                        eng.dma_start(INV, A["k_inv"][i, :].partition_broadcast(P)).then_inc(s_inv, 16)
                for g in range(HEADS):
                    eng.wait_ge(ac.sem, ac.at("p", n_t - HEADS + g))
                    eng.dma_start(z_dram[g], (PAD, CV)[g % 2][:, 0:N]).then_inc(s_z[g % 2], 16)

            @program("pe")
            def _(eng):
                ended(eng, *prev)
                for i in range(n_t):
                    ring.ready(eng, i)
                    if i >= 2:
                        eng.wait_ge(ac.sem, ac.at("p", i - 2))
                    wh, wl = ring.get(i, (KD, P))
                    for k in range(KD):
                        m = product(eng, 3 * (i % 2), (wh[:, k, :], wl[:, k, :]), (HH[:, k], HL[:, k]), k == 0, k == KD - 1)
                    m.then_inc(*pe.did("used", i))
                eng.wait_ge(poB.sem, poB.end())
                for c in range(NT):
                    for k in range(KD):
                        for n_, (x, w) in enumerate(((HH, ABH), (HL, ABH), (HH, ABL))):
                            m = eng.matmul(PS[:, 6, c * 16:(c + 1) * 16], x[:, k, c * P:(c + 1) * P], w[0][:, k, :],
                                           start=k == 0 and n_ == 0, stop=k == KD - 1 and n_ == 2)
                m.then_inc(*peAB.did("ab"))

            def silu(eng, i):
                kind, g, _ = tiles[4 + i]
                eng.wait_ge(ve.sem, ve.at(f"conv{i}.2"))
                for a, n, j in GROUPS:
                    eng.activation(dest[kind][:, g, a:a + n], CV[:, 1 + a + 2 * j:1 + a + 2 * j + n], ACT.Silu).then_inc(*acS.did("sp"[j], i))

            @program("ac")
            def _(eng):
                ended(eng, *prev)
                eng.wait_ge(veZ.sem, veZ.end())
                ring.hi(eng, 0)
                ring.hi(eng, 1)
                for i, (kind, g, _) in enumerate(tiles):
                    if i == 16:
                        silu(eng, 11)
                    eng.wait_ge(pe.sem, pe.at("used", i))
                    if kind == "z":
                        if g < 2:
                            eng.wait_ge(acS.sem, acS.end())
                        else:
                            eng.wait_ge(s_z[g % 2], 16)
                    if kind == "pool" and g:
                        eng.wait_ge(ve.sem, ve.at(f"pool{g - 1}.up"))
                    if 5 <= i < 16:
                        eng.wait_ge(ve.sem, ve.at(f"conv{i - 5}.2"))
                    for a, n, j in GROUPS:
                        src = PSF[:, 1536 * (i % 2) + a:1536 * (i % 2) + a + n]
                        if kind == "pool":
                            at = GAP + a + GAP * j
                            m = eng.activation(UPAD[:, at:at + n], src, ACT.Copy)
                        elif kind == "z":
                            m = eng.activation((PAD, CV)[g % 2][:, a:a + n], src, ACT.Silu)
                        else:
                            at = 1 + a + 2 * j
                            m = eng.activation(PAD[:, at:at + n], src, ACT.Copy)
                        m.then_inc(*ac.did("sp"[j], i))
                    ring.hi(eng, i + 2)
                    if 5 <= i < 16:
                        silu(eng, i - 5)
                    if i == 2:
                        eng.wait_ge(s_small, 64)
                        eng.activation(ABH[0], ABW, ACT.Copy).then_inc(*acB.did("hi"))

            @program("po")
            def _(eng):
                ended(eng, *prev)
                for i in range(n_t):
                    ring.lo(eng, i)
                    if i == 4:
                        eng.wait_ge(acB.sem, acB.end())
                        eng.tensor_tensor(ABL[0], ABW, ABH[1], ALU.subtract).then_inc(*poB.did("lo"))

            @program("ve")
            def _(eng):
                ended(eng, *prev)
                eng.memset(PAD, 0.0).then_inc(*veZ.did("pad"))
                eng.memset(UPAD, 0.0).then_inc(*veZ.did("upad"))
                for g, w in enumerate(WINDOWS):
                    eng.wait_ge(ac.sem, ac.at("p", g))
                    src = UPAD
                    for i in range(doubled[g]):
                        if i:
                            eng.wait_ge(ve.sem, ve.at(f"pool{g}.d{i - 1}"))
                        elif g:
                            eng.wait_ge(ve.sem, ve.at(f"pool{g - 1}.mp"))
                        dst, sh = (PA, PB)[i % 2], 1 << i
                        width = WU - (2 << i) + 1
                        eng.tensor_tensor(dst[:, 0:width], src[:, 0:width], src[:, sh:sh + width], ALU.add).then_inc(*ve.did(f"pool{g}.d{i}"))
                        src = dst
                    eng.wait_ge(s_inv, 16 * (g + 1))
                    eng.wait_ge(ve.sem, ve.at(f"pool{g}.d{doubled[g] - 1}"))
                    for a, n, j in GROUPS:
                        at = GAP + a + GAP * j
                        eng.tensor_tensor(PO[:, g, a:a + n], src[:, at - w // 2:at - w // 2 + n], INV[:, a:a + n], ALU.mult)\
                            .then_inc(*ve.did(f"pool{g}.m{'sp'[j]}"))
                    eng.wait_ge(ve.sem, ve.at(f"pool{g}.mp"))
                    for a, n, j in GROUPS:
                        at = GAP + a + GAP * j
                        eng.tensor_tensor(PO[:, g, a:a + n], PO[:, g, a:a + n], UPAD[:, at:at + n], ALU.subtract)\
                            .then_inc(*ve.did(f"pool{g}.u{'sp'[j]}"))
                for i in range(12):
                    kind, g, _ = tiles[4 + i]
                    eng.wait_ge(ac.sem, ac.at("p", 4 + i))
                    if i:
                        eng.wait_ge(acS.sem, acS.at("p", i - 1))
                    for k in range(3):
                        wcol = vec("l0_dn_conv_w", 12 * k + pos[kind] + g)
                        src, dst = PAD[:, k:k + PADN - 2], CV[:, 1:PADN - 1]
                        if k:
                            eng.wait_ge(ve.sem, ve.at(f"conv{i}.{k - 1}"))
                            m = eng.scalar_tensor_tensor(dst, src, wcol, dst, ALU.mult, ALU.add)
                        else:
                            m = eng.tensor_scalar(dst, src, wcol, None, ALU.mult)
                        m.then_inc(*ve.did(f"conv{i}.{k}"))

            part1 = [pe, peAB, ac, acS, ve, ring.ac, ring.po, acB, poB]

            peN = steps("pe_l2", ["t"], 12)
            acN = steps("ac_l2", ["sq"], 8)
            acR = steps("ac_l2r", ["root"], 8)
            acP = steps("ac_pool", ["p", "hi"], 4)
            poP = steps("po_pool", ["lo"], 4)
            acG = steps("ac_gate", ["exp_a", "ln", "sig", "a"])
            veN = steps("ve_l2", ["inv", "mul"], 8)
            veG = steps("ve_gate", ["copy", "dt", "abs", "g", "ga", "one", "beta"])
            norm_tiles = [(KT, g, 1.0) for g in range(4)] + [(QT, g, float(P) ** -0.5) for g in range(4)]
            a_cols = ABS.rearrange("p t (a b c) -> p t a b c", a=2, b=2)

            def pair(ap):
                return ap.rearrange("p t (a c) -> p t a c", a=2)

            @program("pe")
            def _(eng):
                for i in range(12):
                    if i < 8:
                        eng.wait_ge(acN.sem, acN.at("sq", i))
                        if i == 0:
                            ended(eng, *part1)
                        if i >= 2:
                            eng.wait_ge(acR.sem, acR.at("root", i - 2))
                    else:
                        eng.wait_ge(*((acR.sem, acR.at("root", i - 2)) if i < 10 else (acP.sem, acP.at("p", i - 10))))
                    for b, (a, n) in enumerate(CHUNKS):
                        lhs, rhs = (ones, SQ[i % 2]) if i < 8 else (POW[:, i - 8, :], PO[:, i - 8, :])
                        m = eng.matmul(PS[:, 3 * (i % 2) + b, 0:n], lhs, rhs[:, a:a + n], start=True, stop=True)
                    m.then_inc(*peN.did("t", i))

            @program("ac")
            def _(eng):
                ended(eng, *part1)
                for i in range(9):
                    if i < 8:
                        t, g, _ = norm_tiles[i]
                        if i >= 2:
                            eng.wait_ge(peN.sem, peN.at("t", i - 2))
                        eng.activation(SQ[i % 2], t[:, g, :], ACT.Square).then_inc(*acN.did("sq", i))
                    if i:
                        eng.wait_ge(peN.sem, peN.at("t", i - 1))
                        if i >= 3:
                            eng.wait_ge(veN.sem, veN.at("mul", i - 3))
                        eng.activation(RB[(i - 1) % 2], psum(3 * ((i - 1) % 2), N), ACT.Sqrt, bias=eps).then_inc(*acR.did("root", i - 1))
                for g in range(4):
                    eng.wait_ge(peN.sem, peN.at("t", 8 + g))
                    eng.activation(PO[:, g, :], psum(3 * (g % 2), N), ACT.Identity, bias=0.0, scale=vec("l0_pool_scale", g)).then_inc(*acP.did("p", g))
                    eng.wait_ge(acP.sem, acP.at("p", g))
                    eng.activation(HH[:, 4 + g, :], PO[:, g, :], ACT.Copy).then_inc(*acP.did("hi", g))
                eng.wait_ge(veG.sem, veG.at("abs"))
                eng.activation(TA, TA, ACT.Exp, scale=-1.0).then_inc(*acG.did("exp_a"))
                eng.wait_ge(acG.sem, acG.at("exp_a"))
                eng.activation(TA, TA, ACT.Ln, bias=1.0).then_inc(*acG.did("ln"))
                eng.activation(pair(BT), a_cols[:, :, :, 1, :], ACT.Exp, scale=-1.0).then_inc(*acG.did("sig"))
                eng.activation(ALOG, ALOG, ACT.Exp).then_inc(*acG.did("a"))

            @program("ve")
            def _(eng):
                eng.wait_ge(peAB.sem, peAB.end())
                eng.tensor_copy(ABS.rearrange("p t c -> p (t c)"), PS[:, 6, 0:160]).then_inc(*veG.did("copy"))
                eng.wait_ge(veG.sem, veG.at("copy"))
                eng.tensor_tensor(pair(GG), a_cols[:, :, :, 0, :], pair(over(DTB, NT)), ALU.add).then_inc(*veG.did("dt"))
                eng.wait_ge(veG.sem, veG.at("dt"))
                eng.scalar_tensor_tensor(TA, GG, -1.0, GG, ALU.mult, ALU.max).then_inc(*veG.did("abs"))
                for i in range(8):
                    t, g, scale = norm_tiles[i]
                    eng.wait_ge(acR.sem, acR.at("root", i))
                    eng.reciprocal(RB[i % 2], RB[i % 2]).then_inc(*veN.did("inv", i))
                    eng.wait_ge(veN.sem, veN.at("inv", i))
                    eng.scalar_tensor_tensor(t[:, g, :], RB[i % 2], scale, t[:, g, :], ALU.mult, ALU.mult).then_inc(*veN.did("mul", i))
                eng.wait_ge(acG.sem, acG.at("a"))
                eng.scalar_tensor_tensor(GG, GG, 0.0, TA, ALU.max, ALU.add).then_inc(*veG.did("g"))
                eng.wait_ge(veG.sem, veG.at("g"))
                eng.scalar_tensor_tensor(GG, GG, -1.0, over(ALOG, NT), ALU.mult, ALU.mult).then_inc(*veG.did("ga"))
                eng.tensor_scalar(BT, BT, 1.0, None, ALU.add).then_inc(*veG.did("one"))
                eng.wait_ge(veG.sem, veG.at("one"))
                eng.reciprocal(BT, BT).then_inc(*veG.did("beta"))

            @program("po")
            def _(eng):
                for g in range(4):
                    eng.wait_ge(acP.sem, acP.at("hi", g))
                    eng.tensor_tensor(HL[:, 4 + g, :], PO[:, g, :], HH32[:, 4 + g, :], ALU.subtract).then_inc(*poP.did("lo", g))

            part2 = [peN, acN, acR, acP, acG, veN, veG, poP]

            places = [Region(HT_AT, HT_AT + HEADS * N), Region(HT_AT + KD * N, HT_AT + KD * N + HEADS * N), late]

            def buf(name):
                return next(reg for reg in places if reg.a + 512 <= reg.b).take(HEADS, P)
            B = [{nm: buf(nm) for nm in ("L", "M0", "M1", "X", "Y", "R", "QK", "QD", "KD", "VB", "VN", "S")} for _ in range(2)]
            C = [{nm: late.take(4) for nm in ("gc", "gl", "eg", "egl", "cd", "nb")} for _ in range(2)]
            IT = NT
            LV = range(1, LEVELS)
            pn = ["gb", "gc", "kk", "qk", "kt", "vt", "xt"]
            for v in LV:
                pn += [f"r{v}"] + ([f"q{v}"] if v < LEVELS - 1 else []) + [f"u{v}"]
            pn += ["ks", "vn", "o", "ds"]
            vn = ["gu", "gc", "ta", "tb", "tc", "gl", "l", "qk", "nb", "kd", "vb", "x"]
            for v in LV:
                vn += ([f"x{v}"] if v < LEVELS - 1 else []) + [f"y{v}"]
            vn += ["r1", "r2", "o", "s1", "s2"]
            pe_d = [steps(f"pe_dn{d}", pn, IT) for d in "fb"]
            ve_d = [steps(f"ve_dn{d}", vn, IT) for d in "fb"]
            ac_d = [steps(f"ac_dn{d}", ["eb", "ea", "cd", "eq", "eg", "egl", "y"] + [f"r{v}" for v in LV] + ["vn"], IT) for d in "fb"]
            po_d = [steps(f"po_dn{d}", ["lb", "lm0", "qd"] + [f"lm{v}" for v in LV], IT) for d in "fb"]
            s_state, s_new = sem("state_landed"), sem("state_stored")

            def chunk(it, d):
                first, count = (0, NS // P) if it < NS // P else (NS // P, NP_ // P)
                return it if d == 0 else first + count - 1 - (it - first)

            def cols(it, d):
                c = chunk(it, d)
                return slice(c * P, (c + 1) * P)

            def bank(d, b):
                return PS[:, 4 * d + b, :].rearrange("p (h t) -> p h t", t=P)
            LAST = (P - 1, 0)
            DIRS = (0, 1)

            @program("sp")
            def _(eng):
                ended(eng, *part2)
                for i in range(2):
                    eng.wait_ge(s_z[i], 32)
                eng.dma_start(SQM, A["k_squares"][:, 2 * P:8 * P].rearrange("p (a b) -> p a b", b=P)).then_inc(s_mask, 16)
                eng.dma_start(LVM.rearrange("p a b c -> p (a b c)"), A["k_level"]).then_inc(s_mask, 16)
                for d, name in enumerate(("state_l0_fwd", "state_l0_bwd")):
                    eng.dma_start(B[d]["S"], A[name][0].rearrange("h k v -> k h v")).then_inc(s_state, 16)
                for d, name in enumerate(("new_f", "new_b")):
                    eng.wait_ge(ve_d[d].sem, ve_d[d].end())
                    eng.dma_start(OUT[name][0].rearrange("h k v -> k h v"), B[d]["S"]).then_inc(s_new, 16)
                eng.wait_ge(s_new, 32)

            @program("pe")
            def _(eng):
                ended(eng, *part2)
                eng.wait_ge(s_mask, 32)

                def heads(d, b, f):
                    for hd in range(HEADS):
                        m = f(bank(d, b)[:, hd, :], hd)
                    return m
                for it in range(IT):
                    for d in DIRS:
                        pe, ve, ac, po, bf = pe_d[d], ve_d[d], ac_d[d], po_d[d], B[d]
                        eng.wait_ge(ve.sem, ve.at("gu", it))
                        if it:
                            eng.wait_ge(ac.sem, ac.at("vn", it - 1))
                        eng.matmul(PS[:, 4 * d, :], ones, bf["R"].rearrange("p h t -> p (h t)"), start=True, stop=True).then_inc(*pe.did("gb", it))
                        eng.matmul(PS[:, 4 * d + 3, 0:4], SQM[:, d, :], GG[:, chunk(it, d), 4 * d:4 * d + 4], start=True, stop=True).then_inc(*pe.did("gc", it))
                        cs = cols(it, d)
                        heads(d, 1, lambda o, hd: eng.matmul(o, KT[:, hd, cs], KT[:, hd, cs], start=True, stop=True)).then_inc(*pe.did("kk", it))
                        heads(d, 2, lambda o, hd: eng.matmul(o, KT[:, hd, cs], QT[:, hd, cs], start=True, stop=True)).then_inc(*pe.did("qk", it))
                    for d in DIRS:
                        pe, ve, ac, po, bf = pe_d[d], ve_d[d], ac_d[d], po_d[d], B[d]
                        cs = cols(it, d)
                        eng.wait_ge(ve.sem, ve.at("gc", it))
                        heads(d, 3, lambda o, hd: eng.transpose(o, KT[:, hd, cs], ident)).then_inc(*pe.did("kt", it))
                        eng.wait_ge(ve.sem, ve.at("gl", it))
                        eng.wait_ge(ac.sem, ac.at("eq", it))
                        heads(d, 0, lambda o, hd: eng.transpose(o, VT[:, hd, cs], ident)).then_inc(*pe.did("vt", it))
                    for d in DIRS:
                        pe, ve, ac, po, bf = pe_d[d], ve_d[d], ac_d[d], po_d[d], B[d]
                        eng.wait_ge(ve.sem, ve.at("x", it))
                        heads(d, 3, lambda o, hd: eng.transpose(o, bf["X"][:, hd, :], ident)).then_inc(*pe.did("xt", it))
                    for v in LV:
                        for d in DIRS:
                            pe, ve, ac, po, bf = pe_d[d], ve_d[d], ac_d[d], po_d[d], B[d]
                            if v == 1:
                                eng.wait_ge(ac.sem, ac.at("y", it))
                            else:
                                eng.wait_ge(ve.sem, ve.at(f"y{v - 1}", it))
                            eng.wait_ge(po.sem, po.at(f"lm{v}", it))
                            lm = bf[f"M{v % 2}"]
                            heads(d, 0, lambda o, hd: eng.matmul(o, lm[:, hd, :], bf["Y"][:, hd, :], start=True, stop=True)).then_inc(*pe.did(f"r{v}", it))
                        for d in DIRS:
                            pe, ve, ac, po, bf = pe_d[d], ve_d[d], ac_d[d], po_d[d], B[d]
                            eng.wait_ge(ac.sem, ac.at(f"r{v}", it))
                            if v < LEVELS - 1:
                                heads(d, 1, lambda o, hd: eng.matmul(o, bf["R"][:, hd, :], bf["X"][:, hd, :], start=True, stop=True)).then_inc(*pe.did(f"q{v}", it))
                            heads(d, 2, lambda o, hd: eng.matmul(o, bf["X"][:, hd, :], bf["R"][:, hd, :], start=True, stop=True)).then_inc(*pe.did(f"u{v}", it))
                    for d in DIRS:
                        pe, ve, ac, po, bf = pe_d[d], ve_d[d], ac_d[d], po_d[d], B[d]
                        cs = cols(it, d)
                        if it == 0:
                            eng.wait_ge(s_state, 32)
                        else:
                            eng.wait_ge(ve.sem, ve.at("s2", it - 1))
                        heads(d, 3, lambda o, hd: eng.matmul(o, KT[:, hd, cs], bf["S"][:, hd, :], start=True, stop=True)).then_inc(*pe.did("ks", it))
                    for d in DIRS:
                        pe, ve, ac, po, bf = pe_d[d], ve_d[d], ac_d[d], po_d[d], B[d]
                        eng.wait_ge(ve.sem, ve.at("r2", it))
                        heads(d, 0, lambda o, hd: eng.matmul(o, bf["Y"][:, hd, :], bf["R"][:, hd, :], start=True, stop=True)).then_inc(*pe.did("vn", it))
                    for d in DIRS:
                        pe, ve, ac, po, bf = pe_d[d], ve_d[d], ac_d[d], po_d[d], B[d]
                        eng.wait_ge(ac.sem, ac.at("vn", it))
                        eng.wait_ge(po.sem, po.at("qd", it))

                        def out(o, hd):
                            eng.matmul(o, bf["S"][:, hd, :], bf["QD"][:, hd, :], start=True, stop=False)
                            return eng.matmul(o, bf["VN"][:, hd, :], bf["QK"][:, hd, :], start=False, stop=True)
                        heads(d, 1, out).then_inc(*pe.did("o", it))
                        heads(d, 2, lambda o, hd: eng.matmul(o, bf["KD"][:, hd, :], bf["VN"][:, hd, :], start=True, stop=True)).then_inc(*pe.did("ds", it))

            @program("ve")
            def _(eng):
                ended(eng, *part2)
                eng.wait_ge(s_mask, 32)

                def tt(d, it, step, out, a, b, op):
                    eng.tensor_tensor(out, a, b, op).then_inc(*ve_d[d].did(step, it))
                for it in range(IT):
                    for d in DIRS:
                        ve, bf, cc, c = ve_d[d], B[d], C[d], chunk(it, d)
                        tt(d, it, "gu", bf["R"], over(SQM[:, d, :], HEADS), bcast(GG[:, c, 4 * d:4 * d + 4], P), ALU.mult)
                    for d in DIRS:
                        pe, ve, bf, cc, c = pe_d[d], ve_d[d], B[d], C[d], chunk(it, d)
                        eng.wait_ge(pe.sem, pe.at("gc", it))
                        eng.tensor_copy(cc["gc"], PS[:, 4 * d + 3, 0:4]).then_inc(*ve.did("gc", it))
                        eng.wait_ge(ve.sem, ve.at("gc", it))
                        tt(d, it, "ta", bf["L"], bank(d, 0), bcast(cc["gc"], P), ALU.subtract)
                        eng.wait_ge(ve.sem, ve.at("ta", it))
                        tt(d, it, "tb", bf["QK"], bf["L"], over(SQM[:, 3 + 2 * d, :], HEADS), ALU.add)
                        tt(d, it, "tc", bf["L"], bf["L"], over(SQM[:, 2 + 2 * d, :], HEADS), ALU.add)
                        tt(d, it, "gl", cc["gl"], bank(d, 0)[:, :, LAST[d]], cc["gc"], ALU.subtract)
                    for d in DIRS:
                        pe, ve, ac, po, bf, cc, c = pe_d[d], ve_d[d], ac_d[d], po_d[d], B[d], C[d], chunk(it, d)
                        beta = BT[:, c, 4 * d:4 * d + 4]
                        eng.wait_ge(ac.sem, ac.at("ea", it))
                        eng.wait_ge(pe.sem, pe.at("qk", it))
                        tt(d, it, "l", bf["L"], bf["L"], bank(d, 1), ALU.mult)
                        tt(d, it, "qk", bf["QK"], bf["QK"], bank(d, 2), ALU.mult)
                        eng.wait_ge(ac.sem, ac.at("egl", it))
                        eng.scalar_tensor_tensor(cc["nb"], cc["eg"], -1.0, beta, ALU.mult, ALU.mult).then_inc(*ve.did("nb", it))
                        eng.wait_ge(pe.sem, pe.at("kt", it))
                        tt(d, it, "kd", bf["KD"], bank(d, 3), bcast(cc["egl"], P), ALU.mult)
                        eng.wait_ge(pe.sem, pe.at("vt", it))
                        tt(d, it, "vb", bf["VB"], bank(d, 0), bcast(beta, P), ALU.mult)
                        eng.wait_ge(po.sem, po.at("lm0", it))
                        tt(d, it, "x", bf["X"], over(ident, HEADS), bf["M0"], ALU.subtract)
                    for v in LV:
                        for d in DIRS:
                            pe, ve, bf = pe_d[d], ve_d[d], B[d]
                            eng.wait_ge(pe.sem, pe.at(f"u{v}", it))
                            if v == 1:
                                eng.wait_ge(ve.sem, ve.at("x", it))
                                eng.wait_ge(ac_d[d].sem, ac_d[d].at("y", it))
                            else:
                                eng.wait_ge(ve.sem, ve.at(f"y{v - 1}", it))
                            if v < LEVELS - 1:
                                tt(d, it, f"x{v}", bf["X"], bf["X"], bank(d, 1), ALU.subtract)
                            tt(d, it, f"y{v}", bf["Y"], bf["Y"], bank(d, 2), ALU.subtract)
                    for d in DIRS:
                        pe, ve, bf, cc = pe_d[d], ve_d[d], B[d], C[d]
                        eng.wait_ge(pe.sem, pe.at("ks", it))
                        tt(d, it, "r1", bf["R"], bank(d, 3), bcast(cc["nb"], P), ALU.mult)
                        eng.wait_ge(ve.sem, ve.at("r1", it))
                        tt(d, it, "r2", bf["R"], bf["R"], bf["VB"], ALU.add)
                    for d in DIRS:
                        pe, ve, bf, cc = pe_d[d], ve_d[d], B[d], C[d]
                        eng.wait_ge(pe.sem, pe.at("ds", it))
                        o = OT[:, :, cols(it, d)]
                        seen = [j for j in range(it) if chunk(j, 1 - d) == chunk(it, d)]
                        if seen:
                            eng.wait_ge(ve_d[1 - d].sem, ve_d[1 - d].at("o", seen[0]))
                            tt(d, it, "o", o, o, bank(d, 1), ALU.add)
                        else:
                            eng.tensor_copy(o, bank(d, 1)).then_inc(*ve.did("o", it))
                        if it == 0:
                            eng.wait_ge(s_state, 32)
                        if it == NS // P - 1:
                            eng.memset(bf["S"], 0.0).then_inc(*ve.did("s1", it))
                            eng.wait_ge(ve.sem, ve.at("s1", it))
                            eng.memset(bf["S"], 0.0).then_inc(*ve.did("s2", it))
                        else:
                            if it:
                                eng.wait_ge(ve.sem, ve.at("s2", it - 1))
                            tt(d, it, "s1", bf["S"], bf["S"], bcast(cc["cd"], P), ALU.mult)
                            eng.wait_ge(ve.sem, ve.at("s1", it))
                            tt(d, it, "s2", bf["S"], bf["S"], bank(d, 2), ALU.add)

            @program("ac")
            def _(eng):
                ended(eng, *part2)
                eng.wait_ge(s_mask, 32)
                for it in range(IT):
                    for d in DIRS:
                        pe, ve, ac, bf, cc = pe_d[d], ve_d[d], ac_d[d], B[d], C[d]
                        eng.wait_ge(ve.sem, ve.at("gl", it))
                        eng.activation(bf["QK"], bf["QK"], ACT.Exp).then_inc(*ac.did("eb", it))
                        eng.activation(bf["L"], bf["L"], ACT.Exp, scale=-1.0).then_inc(*ac.did("ea", it))
                        eng.activation(cc["cd"], bank(d, 0)[:, :, LAST[d]], ACT.Exp).then_inc(*ac.did("cd", it))
                        eng.activation(bf["QD"], bank(d, 0), ACT.Exp).then_inc(*ac.did("eq", it))
                        eng.activation(cc["eg"], cc["gc"], ACT.Exp).then_inc(*ac.did("eg", it))
                        eng.activation(cc["egl"], cc["gl"], ACT.Exp).then_inc(*ac.did("egl", it))
                    for d in DIRS:
                        pe, ac, bf = pe_d[d], ac_d[d], B[d]
                        eng.wait_ge(pe.sem, pe.at("xt", it))
                        eng.activation(bf["Y"], bank(d, 3), ACT.Copy).then_inc(*ac.did("y", it))
                    for v in LV:
                        for d in DIRS:
                            pe, ac, bf = pe_d[d], ac_d[d], B[d]
                            eng.wait_ge(pe.sem, pe.at(f"r{v}", it))
                            eng.activation(bf["R"], bank(d, 0), ACT.Copy).then_inc(*ac.did(f"r{v}", it))
                    for d in DIRS:
                        pe, ac, bf = pe_d[d], ac_d[d], B[d]
                        eng.wait_ge(pe.sem, pe.at("vn", it))
                        eng.activation(bf["VN"], bank(d, 0), ACT.Copy).then_inc(*ac.did("vn", it))

            @program("po")
            def _(eng):
                eng.wait_ge(s_mask, 32)
                for it in range(IT):
                    for d in DIRS:
                        pe, ve, ac, po, bf, c = pe_d[d], ve_d[d], ac_d[d], po_d[d], B[d], chunk(it, d)
                        eng.wait_ge(ve.sem, ve.at("l", it))
                        eng.tensor_tensor(bf["L"], bf["L"], bcast(BT[:, c, 4 * d:4 * d + 4], P), ALU.mult).then_inc(*po.did("lb", it))
                        eng.wait_ge(po.sem, po.at("lb", it))
                        eng.tensor_tensor(bf["M0"], bf["L"], over(LVM[:, d, 0, :], HEADS), ALU.mult).then_inc(*po.did("lm0", it))
                    for d in DIRS:
                        ac, po, bf = ac_d[d], po_d[d], B[d]
                        eng.wait_ge(ac.sem, ac.at("eq", it))
                        eng.tensor_tensor(bf["QD"], bf["QD"], QT[:, :, cols(it, d)], ALU.mult).then_inc(*po.did("qd", it))
                    for v in LV:
                        for d in DIRS:
                            pe, ve, po, bf = pe_d[d], ve_d[d], po_d[d], B[d]
                            if v == 2:
                                eng.wait_ge(ve.sem, ve.at("x", it))
                            if v > 2:
                                eng.wait_ge(pe.sem, pe.at(f"r{v - 2}", it))
                            eng.tensor_tensor(bf[f"M{v % 2}"], bf["L"], over(LVM[:, d, v, :], HEADS), ALU.mult).then_inc(*po.did(f"lm{v}", it))

            part3 = pe_d + ve_d + ac_d + po_d

            h = Region(W_AT, W_AT + HEADS * N)
            SQ2 = [h.take(N) for _ in range(2)]
            RB2 = [h.take(N) for _ in range(2)]
            ZT = VT
            s_zb = sem("z_back")
            peH = steps("pe_head", ["t"], HEADS)
            acH = steps("ac_head", ["sq", "root"], HEADS)
            acHi = steps("ac_headhi", ["hi"], HEADS)
            veH = steps("ve_head", ["inv", "mul", "gate"], HEADS)
            poH = steps("po_head", ["lo"], HEADS)

            @program("sp")
            def _(eng):
                ended(eng, *part3)
                eng.dma_start(ZT, z_dram.rearrange("h p n -> p h n")).then_inc(s_zb, 16)

            @program("pe")
            def _(eng):
                for i in range(HEADS):
                    eng.wait_ge(acH.sem, acH.at("sq", i))
                    if i == 0:
                        ended(eng, *part3)
                    if i >= 2:
                        eng.wait_ge(acH.sem, acH.at("root", i - 2))
                    for b, (a, n) in enumerate(CHUNKS):
                        m = eng.matmul(PS[:, 3 * (i % 2) + b, 0:n], ones, SQ2[i % 2][:, a:a + n], start=True, stop=True)
                    m.then_inc(*peH.did("t", i))

            @program("ac")
            def _(eng):
                ended(eng, *part3)
                eng.wait_ge(s_new, 32)
                for i in range(HEADS):
                    if i >= 2:
                        eng.wait_ge(peH.sem, peH.at("t", i - 2))
                    eng.activation(SQ2[i % 2], OT[:, i, :], ACT.Square).then_inc(*acH.did("sq", i))
                    eng.wait_ge(peH.sem, peH.at("t", i))
                    if i >= 2:
                        eng.wait_ge(veH.sem, veH.at("mul", i - 2))
                    eng.activation(RB2[i % 2], psum(3 * (i % 2), N), ACT.Sqrt, bias=eps, scale=1.0 / P).then_inc(*acH.did("root", i))
                for i in range(HEADS):
                    eng.wait_ge(veH.sem, veH.at("gate", i))
                    eng.activation(HH[:, i, :], OT[:, i, :], ACT.Copy).then_inc(*acHi.did("hi", i))

            @program("ve")
            def _(eng):
                ended(eng, *part3)
                eng.wait_ge(s_zb, 16)
                for i in range(HEADS):
                    eng.wait_ge(acH.sem, acH.at("root", i))
                    eng.reciprocal(RB2[i % 2], RB2[i % 2]).then_inc(*veH.did("inv", i))
                    eng.wait_ge(veH.sem, veH.at("inv", i))
                    eng.tensor_tensor(OT[:, i, :], OT[:, i, :], RB2[i % 2], ALU.mult).then_inc(*veH.did("mul", i))
                    eng.wait_ge(veH.sem, veH.at("mul", i))
                    eng.scalar_tensor_tensor(OT[:, i, :], OT[:, i, :], vec("l0_dn_norm_w"), ZT[:, i, :], ALU.mult, ALU.mult).then_inc(*veH.did("gate", i))

            @program("po")
            def _(eng):
                for i in range(HEADS):
                    eng.wait_ge(acHi.sem, acHi.at("hi", i))
                    eng.tensor_tensor(HL[:, i, :], OT[:, i, :], HH32[:, i, :], ALU.subtract).then_inc(*poH.did("lo", i))

            part4 = [peH, acH, acHi, veH, poH]
            part5 = load_x(part4, Region(W_AT, ARENA))
            return part5 + project(A["l0_w_out"], Region(W_AT + 3 * D, ARENA), part4, part5 + part4, 0)

        def project(weight, region, w_free, prev, layer, x_back=None):
            ring = weight_ring(region, KD)
            ve = steps("ve_proj", ["s", "p"], KD)
            wv = weight.rearrange("(k p) n -> p k n", p=P)

            @program("sp")
            def _(eng):
                ended(eng, *w_free)
                for i in range(KD):
                    ring.load(eng, i, wv[:, :, i * P:(i + 1) * P], (KD, P))

            @program("pe")
            def _(eng):
                ended(eng, *prev)
                for i in range(KD):
                    ring.ready(eng, i)
                    if i >= 2:
                        eng.wait_ge(ve.sem, ve.at("p", i - 2))
                    wh, wl = ring.get(i, (KD, P))
                    for k in range(KD):
                        m = product(eng, 3 * (i % 2), (wh[:, k, :], wl[:, k, :]), (HH[:, k], HL[:, k]), k == 0, k == KD - 1)
                    m.then_inc(*ring.pe.did("used", i))

            @program("ac")
            def _(eng):
                ended(eng, *w_free)
                for i in range(KD):
                    ring.hi(eng, i)

            @program("po")
            def _(eng):
                for i in range(KD):
                    ring.lo(eng, i)

            @program("ve")
            def _(eng):
                ended(eng, *prev)
                if x_back:
                    eng.wait_ge(*x_back)
                for i in range(KD):
                    eng.wait_ge(ring.pe.sem, ring.pe.at("used", i))
                    for a, n, j in GROUPS:
                        at = 1536 * (i % 2) + a
                        eng.scalar_tensor_tensor(XT[:, i, a:a + n], PSF[:, at:at + n], MOD[:, layer, 16 + i, j:j + 1],
                                                 XT[:, i, a:a + n], ALU.mult, ALU.add).then_inc(*ve.did("sp"[j], i))
            return [ring.pe, ring.ac, ring.po, ve]

        GROUPS_OF = [list(range(3 * g, 3 * g + 3)) for g in range(6)] + [[18, 19, 20, 21]]
        SLOTS = 4

        def conv_glu(layer, before_norm, prev):
            r = Region(W_AT, ARENA)
            HIDS = [(r.half(N), r.half(N)) for _ in range(SLOTS)]
            ring_at = r
            CV = [r.take(N) for _ in range(2)]
            GRID = (ROWS + 2) * (GRID_W + 2)
            PAD = r.take(GRID + NP_ + 2)
            items = []
            for j in range(KH):
                items += [("a", j, 0), ("g", j, 0)]
                for g, tiles in enumerate(GROUPS_OF):
                    if (j == tiles[-1] + 1) or (j == KH - 1 and tiles[-1] == j):
                        items += [("d", g, m) for m in range(4)]
            at = {it: i for i, it in enumerate(items)}
            ring = weight_ring(r, len(items))
            pe = ring.pe
            taps = [f"grid{i}" for i in range(9)] + [f"line{i}" for i in range(3)]
            ac = steps("ac_ffn", ["grid", "line", "gelu", "hi"], KH)
            veZ = steps("ve_zeroffn", ["pad"])
            ve = steps("ve_ffn", taps + ["hid"], KH)
            veD = steps("ve_resffn", ["s0", "p0", "s1", "p1"], 4 * len(GROUPS_OF))
            po = steps("po_ffn", ["lo"], KH)
            upv = A[f"l{layer}_ffn_up"].rearrange("(k p) n -> p k n", p=P)
            down = A[f"l{layer}_ffn_down"]
            w_name, b_name = f"l{layer}_ffn_conv_w", f"l{layer}_ffn_conv_b"

            def shape(item):
                return (len(GROUPS_OF[item[1]]), 2 * P) if item[0] == "d" else (KD, P)

            def size(i):
                return math.prod(shape(items[i])) if i < len(items) else 0

            @program("sp")
            def _(eng):
                ended(eng, *before_norm)
                for i, (kind, j, m) in enumerate(items):
                    if i == 0:
                        ended(eng, *prev)
                    if kind == "d":
                        a, b = GROUPS_OF[j][0] * P, (GROUPS_OF[j][-1] + 1) * P
                        src = down[a:b, m * 2 * P:(m + 1) * 2 * P].rearrange("(k p) n -> p k n", p=P)
                    else:
                        c = (HIDDEN if kind == "g" else 0) + j * P
                        src = upv[:, :, c:c + P]
                    ring.load(eng, i, src, shape(items[i]))

            @program("pe")
            def _(eng):
                ended(eng, *prev)
                for i, (kind, j, mp) in enumerate(items):
                    ring.ready(eng, i)
                    w = ring.get(i, shape(items[i]))
                    if kind == "a" and j:
                        eng.wait_ge(ac.sem, ac.at("line", j - 1))
                    if kind == "g" and j:
                        eng.wait_ge(ve.sem, ve.at("hid", j - 1))
                    if kind in "ag" and j > GROUPS_OF[0][-1] + 1:
                        q = max(q for q in range(i) if items[q][0] == "d")
                        rnd = 4 * items[q][1] + items[q][2]
                        eng.wait_ge(veD.sem, veD.at("p0" if kind == "a" else "p1", rnd))
                    if kind in "ag":
                        for k in range(KD):
                            m = product(eng, 0 if kind == "a" else 3, (w[0][:, k, :], w[1][:, k, :]), (HH[:, k], HL[:, k]), k == 0, k == KD - 1)
                        m.then_inc(*pe.did("used", i))
                        continue
                    tiles = GROUPS_OF[j]
                    if mp == 0:
                        eng.wait_ge(po.sem, po.at("lo", tiles[-1]))
                    before = [q for q in range(i) if items[q][0] in "ag"][-1]
                    rnd = 4 * j + mp
                    for half in range(2):
                        if mp == 0:
                            eng.wait_ge(*((ac.sem, ac.at("line", items[before][1])) if half == 0 else (ve.sem, ve.at("hid", items[before][1]))))
                        else:
                            eng.wait_ge(veD.sem, veD.at(f"p{half}", rnd - 1))
                        for n, tl in enumerate(tiles):
                            (hh, _), (hl, _) = HIDS[tl % SLOTS]
                            cs = slice(half * P, (half + 1) * P)
                            m = product(eng, 3 * half, (w[0][:, n, cs], w[1][:, n, cs]), (hh, hl), n == 0, n == len(tiles) - 1)
                    m.then_inc(*pe.did("used", i))

            @program("ac")
            def _(eng):
                ended(eng, *prev)
                eng.wait_ge(veZ.sem, veZ.end())
                ring.hi(eng, 0, size(0))
                ring.hi(eng, 1, size(1))
                for i, (kind, j, m) in enumerate(items):
                    if kind == "a":
                        eng.wait_ge(pe.sem, pe.at("used", i))
                        if j:
                            eng.wait_ge(ve.sem, ve.at("line2", j - 1))
                        inner = PAD[:, 0:GRID].rearrange("p (r c) -> p r c", c=GRID_W + 2)[:, 1:ROWS + 1, 1:GRID_W + 1]
                        eng.activation(inner, psum(0, NS).rearrange("p (r c) -> p r c", c=GRID_W), ACT.Copy).then_inc(*ac.did("grid", j))
                        eng.activation(PAD[:, GRID + 1:GRID + 1 + NP_], PSF[:, NS:N], ACT.Copy).then_inc(*ac.did("line", j))
                        ring.hi(eng, i + 2, size(i + 2))
                        eng.wait_ge(ve.sem, ve.at("line2", j))
                        eng.activation(CV[j % 2], CV[j % 2], ACT.Gelu_apprx_tanh).then_inc(*ac.did("gelu", j))
                    elif kind == "g":
                        ring.hi(eng, i + 2, size(i + 2))
                        eng.wait_ge(ve.sem, ve.at("hid", j))
                        eng.activation(HIDS[j % SLOTS][0][0], CV[j % 2], ACT.Copy).then_inc(*ac.did("hi", j))
                    else:
                        ring.hi(eng, i + 2, size(i + 2))

            @program("po")
            def _(eng):
                ended(eng, *prev)
                ring.lo(eng, 0, size(0))
                ring.lo(eng, 1, size(1))
                for i, (kind, j, m) in enumerate(items):
                    ring.lo(eng, i + 2, size(i + 2))
                    if kind == "g":
                        eng.wait_ge(ac.sem, ac.at("hi", j))
                        (_, hh), (hl, _) = HIDS[j % SLOTS]
                        eng.tensor_tensor(hl, CV[j % 2], hh, ALU.subtract).then_inc(*po.did("lo", j))

            @program("ve")
            def _(eng):
                ended(eng, *prev)
                eng.memset(PAD, 0.0).then_inc(*veZ.did("pad"))
                for i, (kind, j, mp) in enumerate(items):
                    if kind == "a":
                        grid = PAD[:, 0:GRID].rearrange("p (r c) -> p r c", c=GRID_W + 2)
                        acc = CV[j % 2][:, 0:NS].rearrange("p (r c) -> p r c", c=GRID_W)
                        if j >= 2:
                            eng.wait_ge(po.sem, po.at("lo", j - 2))
                        eng.wait_ge(ac.sem, ac.at("line", j))
                        for k in range(9):
                            w = vec(w_name, k * KH + j)
                            src = grid[:, k // 3:k // 3 + ROWS, k % 3:k % 3 + GRID_W]
                            if k == 0:
                                eng.tensor_scalar(acc, src, w, vec(b_name, j), ALU.mult, ALU.add).then_inc(*ve.did("grid0", j))
                            else:
                                eng.wait_ge(ve.sem, ve.at(f"grid{k - 1}", j))
                                eng.scalar_tensor_tensor(acc, src, w, acc, ALU.mult, ALU.add).then_inc(*ve.did(f"grid{k}", j))
                        for k in range(3):
                            w = vec(w_name, (3 + k) * KH + j)
                            src, dst = PAD[:, GRID + k:GRID + k + NP_], CV[j % 2][:, NS:N]
                            if k == 0:
                                eng.tensor_scalar(dst, src, w, vec(b_name, j), ALU.mult, ALU.add).then_inc(*ve.did("line0", j))
                            else:
                                eng.wait_ge(ve.sem, ve.at(f"line{k - 1}", j))
                                eng.scalar_tensor_tensor(dst, src, w, dst, ALU.mult, ALU.add).then_inc(*ve.did(f"line{k}", j))
                    elif kind == "g":
                        eng.wait_ge(ac.sem, ac.at("gelu", j))
                        eng.wait_ge(pe.sem, pe.at("used", i))
                        eng.tensor_tensor(CV[j % 2], CV[j % 2], psum(3, N), ALU.mult).then_inc(*ve.did("hid", j))
                    else:
                        eng.wait_ge(pe.sem, pe.at("used", i))
                        rnd = 4 * j + mp
                        for half in range(2):
                            mm = 2 * mp + half
                            for a, n, c in GROUPS:
                                at_ = 1536 * half + a
                                eng.scalar_tensor_tensor(XT[:, mm, a:a + n], PSF[:, at_:at_ + n], MOD[:, layer, 40 + mm, c:c + 1],
                                                         XT[:, mm, a:a + n], ALU.mult, ALU.add).then_inc(*veD.did("sp"[c] + str(half), rnd))
            return [ring.pe, ring.ac, ring.po, ac, veZ, ve, veD, po]

        def ffn_layer(layer, prev):
            before = prev
            prev = norm(prev, 2 * layer + 1, mod(layer, 3))
            return conv_glu(layer, before, prev)

        T_OF = {"s": NS // P, "p": NP_ // P}
        FIRST = {"s": 0, "p": NS // P}
        LEAVES = {"s": range(8), "p": range(2)}
        JOBS = [(c, order) for c in range(NCH) for order in range(2)]
        MAGIC = 1.5 * 2.0 ** 23
        TWO_PI_HI = 6.28125
        TWO_PI_LO = 2 * math.pi - TWO_PI_HI

        def row(ap, a, n):
            return ap[:, a:a + n, :].rearrange("p a c -> p (a c)")

        def pair(ap, a, b, n=1):
            step = b - a
            v = ap[:, a:a + 2 * step, :].rearrange("p (u v) c -> p u v c", v=step)[:, :, 0:n, :]
            return v.rearrange("p u v c -> p u (v c)")

        def chain(eng, st, tag, rnd):
            n = [0]

            def run(f, *args):
                if n[0]:
                    eng.wait_ge(st.sem, st.at(f"{tag}{n[0] - 1}", rnd))
                f(*args).then_inc(*st.did(f"{tag}{n[0]}", rnd))
                n[0] += 1
            return run

        def butterfly(eng, run, K, x0, x1r, x1i, m, th, plus, minus):
            c, s = math.cos(th), math.sin(th)
            run(eng.scalar_tensor_tensor, row(K, 8, m), x1r, c / s, x1i, ALU.mult, ALU.subtract)
            run(eng.scalar_tensor_tensor, row(K, 8 + m, m), x1i, c / s, x1r, ALU.mult, ALU.add)
            turned = row(K, 8, 2 * m).rearrange("p (u c) -> p u c", u=2)
            run(eng.scalar_tensor_tensor, plus.rearrange("p (u c) -> p u c", u=2), turned, s, x0, ALU.mult, ALU.add)
            run(eng.scalar_tensor_tensor, minus.rearrange("p (u c) -> p u c", u=2), turned, -s, x0, ALU.mult, ALU.add)

        N_TREE = 20

        def tree(eng, st, tag, rnd, R, r0, Q, q0, K, T):
            run = chain(eng, st, tag, rnd)
            run(eng.tensor_tensor, row(K, 0, 4), row(R, r0, 4), row(R, r0 + 4, 4), ALU.add)
            run(eng.tensor_tensor, row(K, 4, 4), row(R, r0, 4), row(R, r0 + 4, 4), ALU.subtract)
            run(eng.tensor_tensor, row(T, 0, 2), row(K, 0, 2), row(K, 2, 2), ALU.add)
            run(eng.tensor_tensor, row(T, 2, 2), row(K, 0, 2), row(K, 2, 2), ALU.subtract)
            butterfly(eng, run, K, pair(K, 4, 6), row(K, 5, 1), row(K, 7, 1), 1, math.pi / 4, row(T, 4, 2), row(T, 6, 2))
            butterfly(eng, run, K, pair(Q, q0, q0 + 4, 2), row(Q, q0 + 2, 2), row(Q, q0 + 6, 2), 2, math.pi / 4, row(K, 0, 4), row(K, 4, 4))
            butterfly(eng, run, K, pair(K, 0, 2), row(K, 1, 1), row(K, 3, 1), 1, math.pi / 8, row(T, 8, 2), row(T, 10, 2))
            butterfly(eng, run, K, pair(K, 4, 6), row(K, 5, 1), row(K, 7, 1), 1, 5 * math.pi / 8, row(T, 12, 2), row(T, 14, 2))

        def unfold(eng, run, K, a, b, m, th, out, dst):
            c, s = math.cos(th), math.sin(th)
            run(eng.tensor_tensor, pair(out, dst, dst + 2 * m, m), a.rearrange("p (u c) -> p u c", u=2), b.rearrange("p (u c) -> p u c", u=2), ALU.add)
            run(eng.tensor_tensor, row(K, 8, 2 * m), a, b, ALU.subtract)
            yr, yi = row(K, 8, m), row(K, 8 + m, m)
            ur, ui = row(K, 8 + 2 * m, m), row(K, 8 + 3 * m, m)
            run(eng.scalar_tensor_tensor, ur, yr, c / s, yi, ALU.mult, ALU.add)
            run(eng.scalar_tensor_tensor, ui, yi, c / s, yr, ALU.mult, ALU.subtract)
            x1 = out[:, dst:dst + 4 * m, :].rearrange("p (u v) c -> p u v c", u=2)[:, :, m:2 * m, :].rearrange("p u v c -> p u (v c)")
            run(eng.tensor_scalar, x1, row(K, 8 + 2 * m, 2 * m).rearrange("p (u c) -> p u c", u=2), s, None, ALU.mult)

        N_INV = 25

        def untree(eng, st, tag, rnd, K, T):
            run = chain(eng, st, tag, rnd)
            unfold(eng, run, K, row(T, 8, 2), row(T, 10, 2), 1, math.pi / 8, K, 0)
            unfold(eng, run, K, row(T, 12, 2), row(T, 14, 2), 1, 5 * math.pi / 8, K, 4)
            unfold(eng, run, K, row(K, 0, 4), row(K, 4, 4), 2, math.pi / 4, T, 8)
            unfold(eng, run, K, row(T, 4, 2), row(T, 6, 2), 1, math.pi / 4, K, 4)
            run(eng.tensor_tensor, row(K, 0, 2), row(T, 0, 2), row(T, 2, 2), ALU.add)
            run(eng.tensor_tensor, row(K, 2, 2), row(T, 0, 2), row(T, 2, 2), ALU.subtract)
            run(eng.tensor_tensor, row(T, 0, 4), row(K, 0, 4), row(K, 4, 4), ALU.add)
            run(eng.tensor_tensor, row(T, 4, 4), row(K, 0, 4), row(K, 4, 4), ALU.subtract)
            run(eng.tensor_tensor, row(T, 0, 8), row(T, 0, 8), row(T, 8, 8), ALU.add)

        def matrices(table, leaf, inverse):
            if leaf == 0:
                return [[table[:, 0, :], table[:, 1, :]], [table[:, 2, :], table[:, 3, :]]]
            b = 4 + 3 * (leaf - 1)
            cos, sin, neg = table[:, b, :], table[:, b + 1, :], table[:, b + 2, :]
            return [[cos, neg], [sin, cos]] if inverse else [[cos, sin], [neg, cos]]

        def transform(eng, bank, M, rhs):
            for o in range(2):
                for i in range(2):
                    m = eng.matmul(PS[:, bank, o * HC:(o + 1) * HC], M[i][o], rhs[i], start=i == 0, stop=i == 1)
            return m

        def mixer_hyena(before_norm, prev):
            x_r, r = Region(XT_AT, HT_AT), Region(W_AT, ARENA)
            FW = r.take(25, P)
            mid = Region(r.a, r.b)
            KF, TF, W4 = x_r.take(17, HC), x_r.take(16, HC), x_r.take(4, HC)
            KP, TP = r.take(5, HC), r.take(4, HC)
            SP_ = r.take(4, P)
            PADN = N + 4
            PAD, CV = r.take(PADN), [r.take(PADN) for _ in range(2)]
            STG = r.take(NT, P)
            NPOS = 2 * N
            HD = r.take(NPOS)
            DELTA, BIAS = r.take(HC), r.take(2, HC)
            WIN = {"s": r.take(2, 16), "p": r.take(2, 4)}
            m_r = Region(XT_AT, HT_AT)
            FEAT, ARG, TMP, RED, MLPW = m_r.take(NPOS), m_r.take(512), m_r.take(512), m_r.take(512), m_r.take(3, FFN64)
            n_t = 6 * NCH
            ring = weight_ring(r, n_t)
            tok_dram = nc.dram_tensor("hyena_tokens", (3, NCH, P, NT, HC), F32, kind="Internal").ap()
            filt_dram = {"s": nc.dram_tensor("filters_s", (len(JOBS), P, 17, HC), F32, kind="Internal").ap(),
                         "p": nc.dram_tensor("filters_p", (len(JOBS), P, 5, HC), F32, kind="Internal").ap()}
            spill = nc.dram_tensor("x_spill", (P, KD, N), F32, kind="Internal").ap()
            s_x, s_mlp, s_k, s_c = sem("x_spilled"), sem("mlp_landed"), sem("hyena_tables_landed"), sem("hyena_chunk_landed")
            s_tok = sem("tokens_stored")
            s_flt = {g: sem("filter_stored_" + g) for g in "sp"}
            KB, TB = {"s": KF, "p": KP}, {"s": TF, "p": TP}

            peT = steps("pe_tokens", ["t"], n_t)
            acW = steps("ac_in1", ["s", "p"], n_t)
            acT = steps("ac_tokens", ["e"], n_t)
            veZ = steps("ve_zero1", ["pad"])
            veW = steps("ve_in1", ["c0", "c1", "c2"], n_t)
            peM = steps("pe_mlp", ["t"], 15)
            veM_ = steps("ve_mlp", ["arg", "turns", "whole", "hi", "lo", "clamp"], 15)
            acM = steps("ac_mlp", ["sin"], 15)
            peF, acF, veF = {}, {}, {}
            for g in "sp":
                T = T_OF[g]
                peF[g] = steps("pe_filter_" + g, [f"tap{b}" for b in range(T)] + [f"h{l}" for l in LEAVES[g]] + ["hx"], len(JOBS))
                acF[g] = steps("ac_filter_" + g, [f"win{b}" for b in range(T)] + [f"h{l}" for l in LEAVES[g]] + ["hx"], len(JOBS))
                veF[g] = steps("ve_filter_" + g, [f"k{b}" for b in range(T)] + ["bias", "r", "q"] + ([f"ft{i}" for i in range(N_TREE)] if g == "s" else []), len(JOBS))
            leaves_made = {"s": f"ft{N_TREE - 1}", "p": "q"}

            EXTRA = {0: ("mlp", 0), 2: ("mlp", 1), 4: ("mlp", 2)}
            for f in range(len(JOBS)):
                EXTRA[6 + 2 * f], EXTRA[7 + 2 * f] = ("tap", f), ("leaf", f)

            small = []
            for n in sorted(EXTRA):
                kind, f = EXTRA[n]
                if kind == "mlp":
                    small += [(veM_, "arg", 5 * f + i) for i in range(5)]
                for g in "sp" if kind != "mlp" else "":
                    if kind == "tap":
                        small += [(veF[g], f"k{b}", f) for b in range(T_OF[g])]
                    else:
                        small += [(acF[g], f"h{l}", f) for l in LEAVES[g]] + [(acF[g], "hx", f)]
            place = {(id(st), step, rnd): q for q, (st, step, rnd) in enumerate(small)}

            def small_bank(st, step, rnd):
                return 6 + place[(id(st), step, rnd)] % 2

            def wait_bank(eng, st, step, rnd):
                q = place[(id(st), step, rnd)]
                if q >= 2:
                    who, what, when = small[q - 2]
                    eng.wait_ge(who.sem, who.at(what, when))

            w_in = A["l1_w_in"].rearrange("(k p) n -> p k n", p=P)

            def tile_of(n):
                c, i = divmod(n, 6)
                kind, half = divmod(i, 2)
                return c, kind, half, 8 * kind + 2 * c + half

            def slots():
                for n in range(n_t + 1):
                    yield n, EXTRA.get(n, (None, None))

            @program("sp")
            def _(eng):
                ended(eng, *before_norm)
                eng.dma_start(spill, XT).then_inc(s_x, 16)
                ended(eng, *prev)
                for n in range(2):
                    ring.load(eng, n, w_in[:, :, tile_of(n)[3] * P:(tile_of(n)[3] + 1) * P], (KD, P))
                eng.wait_ge(s_x, 16)
                for dst, name in ((FEAT[0:EMB, 0:2 * NS], "k_feat_s"), (FEAT[0:EMB, 2 * NS:NPOS], "k_feat_p"), (MLPW[0:EMB, 0, :], "l1_hy_w1"),
                                  (MLPW[0:FFN64, 1, :], "l1_hy_w2"), (MLPW[0:FFN64, 2, :], "l1_hy_w3")):
                    eng.dma_start(dst, A[name]).then_inc(s_mlp, 16)
                for dst, name in ((FW, "k_fwd"), (SP_, "k_spec"), (WIN["s"], "k_win_s"), (WIN["p"], "k_win_p")):
                    eng.dma_start(dst.rearrange("p a b -> p (a b)"), A[name]).then_inc(s_k, 16)
                for n, (kind, f) in slots():
                    if n + 2 < n_t:
                        col = tile_of(n + 2)[3] * P
                        ring.load(eng, n + 2, w_in[:, :, col:col + P], (KD, P))
                    if n >= 1:
                        c, knd, half, _ = tile_of(n - 1)
                        eng.wait_ge(acT.sem, acT.at("e", n - 1))
                        eng.dma_start(tok_dram[knd, c][:, :, half * P:(half + 1) * P], STG).then_inc(s_tok, 16)
                    if n in EXTRA and EXTRA[n][0] == "leaf":
                        for g in "sp":
                            eng.wait_ge(acF[g].sem, acF[g].at("hx", f))
                            eng.dma_start(filt_dram[g][f], KB[g]).then_inc(s_flt[g], 16)
                    if n % 4 == 1 and 5 <= n < 18:
                        c = (n - 5) // 4
                        if c:
                            eng.wait_ge(peF["p"].sem, peF["p"].at("tap1", 2 * c - 1))
                            eng.wait_ge(veF["p"].sem, veF["p"].at("bias", 2 * c - 1))
                            eng.wait_ge(acF["p"].sem, acF["p"].at("win1", 2 * c - 1))
                        else:
                            eng.wait_ge(acM.sem, acM.end())
                            eng.wait_ge(peM.sem, peM.end())
                        cs = slice(c * HC, (c + 1) * HC)
                        eng.dma_start(W4[0:FFN64, :, :], A["l1_hy_w4"].rearrange("k (a c) -> k a c", a=4)[:, :, cs]).then_inc(s_c, 16)
                        eng.dma_start(DELTA, A["k_delta"][0, cs].partition_broadcast(P)).then_inc(s_c, 16)
                        eng.dma_start(BIAS[0:1, :, :], A["l1_hy_bias"][:, cs].unsqueeze(0)).then_inc(s_c, 16)

            @program("pe")
            def _(eng):
                ended(eng, *prev)
                for n, (kind, f) in slots():
                    if n < n_t:
                        ring.ready(eng, n)
                        if n:
                            eng.wait_ge(acW.sem, acW.at("p", n - 1))
                        wh, wl = ring.get(n, (KD, P))
                        for k in range(KD):
                            m = product(eng, 0, (wh[:, k, :], wl[:, k, :]), (HH[:, k], HL[:, k]), k == 0, k == KD - 1)
                        m.then_inc(*ring.pe.did("used", n))
                    if n:
                        eng.wait_ge(veW.sem, veW.at("c2", n - 1))
                        if n >= 2:
                            eng.wait_ge(acT.sem, acT.at("e", n - 2))
                        for tt in range(NT):
                            at = 1 + tt * P + (2 if tt >= NS // P else 0)
                            m = eng.transpose(PS[:, 3 + tt // 4, (tt % 4) * P:(tt % 4 + 1) * P], CV[(n - 1) % 2][:, at:at + P], ident)
                        m.then_inc(*peT.did("t", n - 1))
                    if kind == "mlp":
                        if f == 0:
                            eng.wait_ge(s_mlp, 80)
                        kk = EMB if f == 0 else FFN64
                        src = FEAT if f == 0 else HD
                        for c in range(5):
                            i = 5 * f + c
                            if f:
                                eng.wait_ge(acM.sem, acM.at("sin", i - 5))
                            wait_bank(eng, veM_, "arg", i)
                            eng.matmul(PS[0:FFN64, small_bank(veM_, "arg", i), :], MLPW[0:kk, f, :], src[0:kk, c * 512:(c + 1) * 512],
                                       start=True, stop=True).then_inc(*peM.did("t", i))
                    if kind == "tap":
                        c, order = JOBS[f]
                        eng.wait_ge(s_c, 48 * (c + 1))
                        eng.wait_ge(acM.sem, acM.end())
                        for g, base in (("s", 0), ("p", 2 * NS)):
                            for b in range(T_OF[g]):
                                wait_bank(eng, veF[g], f"k{b}", f)
                                bank = small_bank(veF[g], f"k{b}", f)
                                for u in range(2):
                                    tap = 2 * b + u
                                    m = eng.matmul(PS[:, bank, u * HC:(u + 1) * HC], HD[0:FFN64, base + tap * P:base + (tap + 1) * P],
                                                   W4[0:FFN64, 2 * (tap // T_OF[g]) + order, :], start=True, stop=True)
                                m.then_inc(*peF[g].did(f"tap{b}", f))
                    if kind == "leaf":
                        eng.wait_ge(s_k, 64)
                        for g in "sp":
                            T = TB[g]
                            eng.wait_ge(veF[g].sem, veF[g].at(leaves_made[g], f))
                            for l in LEAVES[g]:
                                wait_bank(eng, acF[g], f"h{l}", f)
                                M = matrices(FW, l, False)
                                if l == 0:
                                    M = [[M[0][0], SP_[:, 0, :]], [M[1][0], SP_[:, 2, :]]]
                                transform(eng, small_bank(acF[g], f"h{l}", f), M, [T[:, 2 * l, :], T[:, 2 * l + 1, :]]).then_inc(*peF[g].did(f"h{l}", f))
                            wait_bank(eng, acF[g], "hx", f)
                            bank = small_bank(acF[g], "hx", f)
                            for i in range(2):
                                m = eng.matmul(PS[:, bank, 0:HC], SP_[:, 1 + 2 * i, :], T[:, i, :], start=i == 0, stop=i == 1)
                            m.then_inc(*peF[g].did("hx", f))

            @program("ac")
            def _(eng):
                ended(eng, *prev)
                eng.wait_ge(veZ.sem, veZ.end())
                ring.hi(eng, 0)
                ring.hi(eng, 1)
                for n, (kind, f) in slots():
                    if n < n_t:
                        eng.wait_ge(ring.pe.sem, ring.pe.at("used", n))
                        if n:
                            eng.wait_ge(veW.sem, veW.at("c2", n - 1))
                        for a, w, j in GROUPS:
                            at = 1 + a + 2 * j
                            eng.activation(PAD[:, at:at + w], PSF[:, a:a + w], ACT.Copy).then_inc(*acW.did("sp"[j], n))
                        ring.hi(eng, n + 2)
                    if n:
                        eng.wait_ge(peT.sem, peT.at("t", n - 1))
                        if n >= 2:
                            eng.wait_ge(s_tok, 16 * (n - 1))
                        eng.activation(STG, psum(3, N).rearrange("p (t c) -> p t c", c=P), ACT.Copy).then_inc(*acT.did("e", n - 1))
                    if kind == "mlp":
                        for i in range(5 * f, 5 * f + 5):
                            eng.wait_ge(veM_.sem, veM_.at("clamp", i))
                            eng.activation(HD[0:FFN64, (i % 5) * 512:(i % 5 + 1) * 512], RED[0:FFN64, :], ACT.Sin).then_inc(*acM.did("sin", i))
                    if kind == "tap":
                        eng.wait_ge(s_c, 48 * (JOBS[f][0] + 1))
                        eng.wait_ge(s_k, 64)
                        eng.wait_ge(peM.sem, peM.end())
                        for g in "sp":
                            if f:
                                eng.wait_ge(s_flt[g], 16 * f)
                            for b in range(T_OF[g]):
                                for tap in (2 * b, 2 * b + 1):
                                    m = eng.activation(KB[g][:, tap, :], DELTA, ACT.Exp, scale=WIN[g][:, 0, tap:tap + 1], bias=WIN[g][:, 1, tap:tap + 1])
                                m.then_inc(*acF[g].did(f"win{b}", f))
                    if kind == "leaf":
                        for g in "sp":
                            for l in LEAVES[g]:
                                eng.wait_ge(peF[g].sem, peF[g].at(f"h{l}", f))
                                eng.activation(row(KB[g], 2 * l, 2), PS[:, small_bank(acF[g], f"h{l}", f), :], ACT.Copy).then_inc(*acF[g].did(f"h{l}", f))
                            eng.wait_ge(peF[g].sem, peF[g].at("hx", f))
                            eng.activation(KB[g][:, 2 * len(LEAVES[g]), :], PS[:, small_bank(acF[g], "hx", f), 0:HC], ACT.Copy).then_inc(*acF[g].did("hx", f))

            @program("po")
            def _(eng):
                ended(eng, *prev)
                for n in range(n_t):
                    ring.lo(eng, n)

            @program("ve")
            def _(eng):
                ended(eng, *prev)
                eng.memset(PAD, 0.0).then_inc(*veZ.did("pad"))
                half = (slice(0, FFN64), slice(None))
                for n, (kind, f) in slots():
                    if n < n_t:
                        col = tile_of(n)[3]
                        eng.wait_ge(acW.sem, acW.at("p", n))
                        if n >= 2:
                            eng.wait_ge(peT.sem, peT.at("t", n - 2))
                        for k in range(3):
                            wcol = vec("l1_hy_short_w", 24 * k + col)
                            src, dst = PAD[:, k:k + PADN - 2], CV[n % 2][:, 1:PADN - 1]
                            if k:
                                eng.wait_ge(veW.sem, veW.at(f"c{k - 1}", n))
                                m = eng.scalar_tensor_tensor(dst, src, wcol, dst, ALU.mult, ALU.add)
                            else:
                                m = eng.tensor_scalar(dst, src, wcol, vec("l1_hy_short_b", col), ALU.mult, ALU.add)
                            m.then_inc(*veW.did(f"c{k}", n))
                    if kind == "mlp":
                        bias = vec(f"l1_hy_b{f + 1}")[0:FFN64, :]
                        for i in range(5 * f, 5 * f + 5):
                            ve = veM_
                            eng.wait_ge(peM.sem, peM.at("t", i))
                            if i:
                                eng.wait_ge(ve.sem, ve.at("clamp", i - 1))
                            eng.tensor_scalar(ARG[half], PS[0:FFN64, small_bank(ve, "arg", i), :], bias, vec("l1_hy_freq")[0:FFN64, :], ALU.add, ALU.mult)\
                                .then_inc(*ve.did("arg", i))
                            eng.wait_ge(ve.sem, ve.at("arg", i))
                            eng.tensor_scalar(TMP[half], ARG[half], 1 / (2 * math.pi), MAGIC, ALU.mult, ALU.add).then_inc(*ve.did("turns", i))
                            eng.wait_ge(ve.sem, ve.at("turns", i))
                            eng.tensor_scalar(TMP[half], TMP[half], MAGIC, None, ALU.subtract).then_inc(*ve.did("whole", i))
                            eng.wait_ge(ve.sem, ve.at("whole", i))
                            eng.scalar_tensor_tensor(ARG[half], TMP[half], -TWO_PI_HI, ARG[half], ALU.mult, ALU.add).then_inc(*ve.did("hi", i))
                            eng.wait_ge(ve.sem, ve.at("hi", i))
                            if i:
                                eng.wait_ge(acM.sem, acM.at("sin", i - 1))
                            eng.scalar_tensor_tensor(RED[half], TMP[half], -TWO_PI_LO, ARG[half], ALU.mult, ALU.add).then_inc(*ve.did("lo", i))
                            eng.wait_ge(ve.sem, ve.at("lo", i))
                            eng.tensor_scalar(RED[half], RED[half], 3.1415925, -3.1415925, ALU.min, ALU.max).then_inc(*ve.did("clamp", i))
                    if kind == "tap":
                        order = JOBS[f][1]
                        for g in "sp":
                            ve, K, T, tn = veF[g], KB[g], TB[g], T_OF[g]
                            for b in range(tn):
                                eng.wait_ge(peF[g].sem, peF[g].at(f"tap{b}", f))
                                eng.wait_ge(acF[g].sem, acF[g].at(f"win{b}", f))
                                eng.tensor_tensor(row(K, 2 * b, 2), row(K, 2 * b, 2), PS[:, small_bank(ve, f"k{b}", f), :], ALU.mult).then_inc(*ve.did(f"k{b}", f))
                            eng.wait_ge(ve.sem, ve.at(f"k{tn - 1}", f))
                            eng.tensor_tensor(K[0:1, 0, :], K[0:1, 0, :], BIAS[0:1, order, :], ALU.add).then_inc(*ve.did("bias", f))
                            eng.wait_ge(ve.sem, ve.at("bias", f))
                            if f:
                                eng.wait_ge(peF[g].sem, peF[g].at("hx", f - 1))
                            eng.tensor_tensor(row(T, 0, tn), row(K, 0, tn), row(K, tn, tn), ALU.add).then_inc(*ve.did("r", f))
                            eng.tensor_tensor(row(T, tn, tn), row(K, 0, tn), row(K, tn, tn), ALU.subtract).then_inc(*ve.did("q", f))
                            if g == "s":
                                eng.wait_ge(ve.sem, ve.at("q", f))
                                tree(eng, ve, "ft", f, T, 0, T, 8, K, T)

            part1 = [ring.pe, ring.ac, ring.po, peT, acW, acT, veW, peM, veM_, acM] + [x[g] for x in (peF, acF, veF) for g in "sp"]

            x_r = Region(XT_AT, HT_AT)
            K2, T2, KP2, TP2 = x_r.take(16, HC), x_r.take(16, HC), x_r.take(4, HC), x_r.take(4, HC)
            IV = mid.take(25, P)
            H2, HP2 = mid.take(17, HC), mid.take(5, HC)
            Z, X1, X2 = mid.take(NT, HC), mid.take(NT, HC), mid.take(NT, HC)
            KB2, TB2, HB = {"s": K2, "p": KP2}, {"s": T2, "p": TP2}, {"s": H2, "p": HP2}
            nj = len(JOBS)
            s_iv, s_z, s_x1, s_x2 = sem("inverse_landed"), sem("z_landed"), sem("x1_landed"), sem("x2_landed")
            s_h = {g: sem("filter_landed_" + g) for g in "sp"}
            ORDER = {"s": [("z", 0), ("z", 1), ("z", 2)] + sum([[("i", l), ("z", l + 3)] for l in range(5)], []) + [("i", l) for l in (5, 6, 7)],
                     "p": [("z", 0), ("z", 1), ("i", 0), ("i", 1)]}
            peC, acC, veC, poC = {}, {}, {}, {}
            for g in "sp":
                L = LEAVES[g]
                peC[g] = steps("pe_conv_" + g, [f"{k}{l}" for k, l in ORDER[g]], nj)
                acC[g] = steps("ac_conv_" + g, [f"i{l}" for l in L], nj)
                veC[g] = steps("ve_conv_" + g, ([f"zt{i}" for i in range(N_TREE)] if g == "s" else []) + [f"{t}{l}" for l in L for t in ("re", "im", "cross", "done")]
                               + [f"it{i}" for i in range(N_INV if g == "s" else 1)] + ["gate"], nj)
                poC[g] = steps("po_conv_" + g, [f"{t}{l}" for l in L for t in ("a", "b")], nj)
            peO, acO, veO = steps("pe_turn", ["t0", "t1"], NCH), steps("ac_turn", ["t0", "t1"], NCH), steps("ve_turn", ["t0", "t1"], NCH)

            def bank_of(g, i):
                return i % 6 if g == "s" else 6 + i % 2

            def emptied(g, rnd, i):
                k, l = ORDER[g][i]
                return (veC[g], f"done{l}", rnd) if k == "z" else (acC[g], f"i{l}", rnd)

            @program("sp")
            def _(eng):
                ended(eng, *part1)
                eng.wait_ge(s_tok, 16 * n_t)
                for g in "sp":
                    eng.wait_ge(s_flt[g], 16 * nj)
                eng.dma_start(Z, tok_dram[0, 0]).then_inc(s_z, 16)
                for g in "sp":
                    eng.dma_start(HB[g], filt_dram[g][0]).then_inc(s_h[g], 16)
                eng.dma_start(IV.rearrange("p a b -> p (a b)"), A["k_inv8"]).then_inc(s_iv, 16)
                eng.dma_start(X1, tok_dram[1, 0]).then_inc(s_x1, 16)
                eng.dma_start(X2, tok_dram[2, 0]).then_inc(s_x2, 16)
                for rnd, (c, order) in enumerate(JOBS):
                    for g in "sp":
                        if rnd + 1 < nj:
                            eng.wait_ge(veC[g].sem, veC[g].at(f"done{LEAVES[g][-1]}", rnd))
                            eng.dma_start(HB[g], filt_dram[g][rnd + 1]).then_inc(s_h[g], 16)
                    if c + 1 < NCH:
                        for g in "sp":
                            eng.wait_ge(veC[g].sem, veC[g].at("gate", rnd))
                        if order == 0:
                            eng.dma_start(X1, tok_dram[1, c + 1]).then_inc(s_x1, 16)
                        else:
                            eng.wait_ge(peO.sem, peO.at("t1", c))
                            eng.dma_start(Z, tok_dram[0, c + 1]).then_inc(s_z, 16)
                            eng.dma_start(X2, tok_dram[2, c + 1]).then_inc(s_x2, 16)
                for g in "sp":
                    eng.wait_ge(veC[g].sem, veC[g].end())
                eng.dma_start(XT, spill).then_inc(s_x, 16)

            @program("pe")
            def _(eng):
                ended(eng, *part1)
                eng.wait_ge(s_iv, 16)
                for rnd, (c, order) in enumerate(JOBS):
                    for g in "sp":
                        T = TB2[g]
                        if g == "s":
                            eng.wait_ge(veC[g].sem, veC[g].at(f"zt{N_TREE - 1}", rnd))
                        else:
                            eng.wait_ge(s_z, 16 * (c + 1))
                            if order:
                                eng.wait_ge(veC[g].sem, veC[g].at("gate", rnd - 1))
                        for i, (k, l) in enumerate(ORDER[g]):
                            n_banks = 6 if g == "s" else 2
                            if i >= n_banks:
                                who, what, when = emptied(g, rnd, i - n_banks)
                                eng.wait_ge(who.sem, who.at(what, when))
                            elif g == "s" and rnd and order == 0:
                                eng.wait_ge(acO.sem, acO.at("t1", c - 1))
                                eng.wait_ge(veO.sem, veO.at("t1", c - 1))
                            elif rnd:
                                eng.wait_ge(acC[g].sem, acC[g].at(f"i{LEAVES[g][-1]}", rnd - 1))
                            if k == "z":
                                rhs = [T[:, 2 * l, :], T[:, 2 * l + 1, :]] if g == "s" else [Z[:, NS // P + u, :] for u in range(2)]
                            else:
                                eng.wait_ge(poC[g].sem, poC[g].at(f"b{l}", rnd))
                                rhs = [KB2[g][:, 2 * l, :], KB2[g][:, 2 * l + 1, :]]
                            transform(eng, bank_of(g, i), matrices(FW if k == "z" else IV, l, k == "i"), rhs).then_inc(*peC[g].did(f"{k}{l}", rnd))
                    if order:
                        for g in "sp":
                            eng.wait_ge(veC[g].sem, veC[g].at("gate", rnd))
                        for half in range(2):
                            for tt in range(NT):
                                m = eng.transpose(PS[:, 3 * half + tt // 4, (tt % 4) * P:(tt % 4 + 1) * P], Z[:, tt, half * P:(half + 1) * P], ident)
                            m.then_inc(*peO.did(f"t{half}", c))

            @program("ac")
            def _(eng):
                ended(eng, *part1)
                for rnd, (c, order) in enumerate(JOBS):
                    for g in "sp":
                        for l in LEAVES[g]:
                            i = ORDER[g].index(("i", l))
                            eng.wait_ge(peC[g].sem, peC[g].at(f"i{l}", rnd))
                            eng.activation(row(TB2[g], 2 * l, 2), PS[:, bank_of(g, i), :], ACT.Copy).then_inc(*acC[g].did(f"i{l}", rnd))
                    if order:
                        for half in range(2):
                            eng.wait_ge(peO.sem, peO.at(f"t{half}", c))
                            eng.activation(HH[:, 2 * c + half, :], psum(3 * half, N), ACT.Copy).then_inc(*acO.did(f"t{half}", c))

            @program("po")
            def _(eng):
                for rnd, (c, order) in enumerate(JOBS):
                    for g in "sp":
                        K, T = KB2[g], TB2[g]
                        for l in LEAVES[g]:
                            eng.wait_ge(veC[g].sem, veC[g].at(f"done{l}", rnd))
                            eng.tensor_tensor(K[:, 2 * l, :], K[:, 2 * l, :], T[:, 2 * l, :], ALU.subtract).then_inc(*poC[g].did(f"a{l}", rnd))
                            eng.tensor_tensor(K[:, 2 * l + 1, :], K[:, 2 * l + 1, :], T[:, 2 * l + 1, :], ALU.add).then_inc(*poC[g].did(f"b{l}", rnd))

            @program("ve")
            def _(eng):
                ended(eng, *part1)

                def turned(c):
                    for half in range(2):
                        eng.wait_ge(acO.sem, acO.at(f"t{half}", c))
                        eng.tensor_tensor(HL[:, 2 * c + half, :], psum(3 * half, N), HH32[:, 2 * c + half, :], ALU.subtract).then_inc(*veO.did(f"t{half}", c))
                for rnd, (c, order) in enumerate(JOBS):
                    X, s_gate = (X1, s_x1) if order == 0 else (X2, s_x2)
                    for g in "sp":
                        ve, K, T, H = veC[g], KB2[g], TB2[g], HB[g]
                        if g == "s":
                            eng.wait_ge(s_z, 16 * (c + 1))
                            if order:
                                eng.wait_ge(ve.sem, ve.at("gate", rnd - 1))
                            tree(eng, ve, "zt", rnd, Z, 0, Z, 0, K, T)
                        eng.wait_ge(s_h[g], 16 * (rnd + 1))
                        for l in LEAVES[g]:
                            i = ORDER[g].index(("z", l))
                            bank = bank_of(g, i)
                            re, im = PS[:, bank, 0:HC], PS[:, bank, HC:2 * HC]
                            h_im = len(LEAVES[g]) * 2 if l == 0 else 2 * l
                            eng.wait_ge(peC[g].sem, peC[g].at(f"z{l}", rnd))
                            eng.tensor_tensor(K[:, 2 * l, :], re, H[:, 2 * l, :], ALU.mult).then_inc(*ve.did(f"re{l}", rnd))
                            eng.tensor_tensor(K[:, 2 * l + 1, :], im, H[:, h_im, :], ALU.mult).then_inc(*ve.did(f"im{l}", rnd))
                            eng.tensor_tensor(T[:, 2 * l, :], im, H[:, 2 * l + 1, :], ALU.mult).then_inc(*ve.did(f"cross{l}", rnd))
                            eng.tensor_tensor(T[:, 2 * l + 1, :], re, H[:, 2 * l + 1, :], ALU.mult).then_inc(*ve.did(f"done{l}", rnd))
                        eng.wait_ge(acC[g].sem, acC[g].at(f"i{LEAVES[g][-1]}", rnd))
                        if g == "s":
                            untree(eng, ve, "it", rnd, K, T)
                            last, scale = f"it{N_INV - 1}", 1.0
                        else:
                            eng.tensor_tensor(row(T, 0, 2), row(T, 0, 2), row(T, 2, 2), ALU.add).then_inc(*ve.did("it0", rnd))
                            last, scale = "it0", 4.0
                        eng.wait_ge(ve.sem, ve.at(last, rnd))
                        eng.wait_ge(s_gate, 16 * (c + 1))
                        f, n = FIRST[g], T_OF[g]
                        eng.scalar_tensor_tensor(row(Z, f, n), row(T, 0, n), scale, row(X, f, n), ALU.mult, ALU.mult).then_inc(*ve.did("gate", rnd))
                    if order:
                        turned(c)

            done = [peO, acO, veO] + [x[g] for x in (peC, acC, veC, poC) for g in "sp"]
            return done + project(A["l1_w_out"], Region(W_AT, ARENA), done, done, 1, (s_x, 32))
        before = prev
        prev = norm(prev, 0, mod(0, 0))
        prev = mixer_even(before, prev)
        prev = ffn_layer(0, prev)
        before = prev
        prev = norm(prev, 2, mod(1, 0))
        prev = mixer_hyena(before, prev)
        prev = ffn_layer(1, prev)

        def store(prev, final):
            r = Region(W_AT, ARENA)
            OR = [r.take(D) for _ in range(3)]
            SQ = [r.take(N) for _ in range(2)]
            RS = r.take(N)
            pe = steps("pe_out", ["lo", "hi"], NT)
            ve = steps("ve_out", ["lo"], NT)
            ac = steps("ac_out", ["hi"], NT)
            acn = steps("ac_nf", ["sq"], KD)
            acr = steps("ac_nfr", ["root"])
            pen = steps("pe_nf", ["sum"], KD)
            ven = steps("ve_nf", ["inv"] + [f"m{k}" for k in range(KD)])
            s_o = [sem(f"stored{i}") for i in range(3)]

            @program("pe")
            def _(eng):
                ended(eng, *prev)
                if final:
                    for k in range(KD):
                        eng.wait_ge(acn.sem, acn.at("sq", k))
                        for b, (a, n) in enumerate(CHUNKS):
                            m = eng.matmul(PS[:, b, 0:n], ones, SQ[k % 2][:, a:a + n], start=k == 0, stop=k == KD - 1)
                        m.then_inc(*pen.did("sum", k))
                    eng.wait_ge(ven.sem, ven.end())
                for t in range(NT):
                    for half, who in ((0, ve), (1, ac)):
                        if t >= 4:
                            eng.wait_ge(who.sem, who.at(("lo", "hi")[half], t - 4))
                        for k in range(4):
                            m = eng.transpose(PS[:, (2 * t) % 8 + half, k * P:(k + 1) * P], XT[:, 4 * half + k, t * P:(t + 1) * P], ident)
                        m.then_inc(*pe.did(("lo", "hi")[half], t))

            @program("ve")
            def _(eng):
                if final:
                    eng.wait_ge(acr.sem, acr.at("root"))
                    eng.reciprocal(RS, RS).then_inc(*ven.did("inv"))
                    eng.wait_ge(ven.sem, ven.at("inv"))
                    for k in range(KD):
                        eng.scalar_tensor_tensor(XT[:, k, :], XT[:, k, :], vec("final_norm", k), RS, ALU.mult, ALU.mult).then_inc(*ven.did(f"m{k}"))
                for t in range(NT):
                    eng.wait_ge(pe.sem, pe.at("lo", t))
                    if t >= 3:
                        eng.wait_ge(s_o[t % 3], 16 * (t // 3))
                    eng.tensor_copy(OR[t % 3][:, 0:512], PS[:, (2 * t) % 8, :]).then_inc(*ve.did("lo", t))

            @program("ac")
            def _(eng):
                if final:
                    ended(eng, *prev)
                    for k in range(KD):
                        if k >= 2:
                            eng.wait_ge(pen.sem, pen.at("sum", k - 2))
                        eng.activation(SQ[k % 2], XT[:, k, :], ACT.Square).then_inc(*acn.did("sq", k))
                    eng.wait_ge(pen.sem, pen.end())
                    eng.activation(RS, psum(0, N), ACT.Sqrt, scale=1.0 / D, bias=eps).then_inc(*acr.did("root"))
                for t in range(NT):
                    eng.wait_ge(pe.sem, pe.at("hi", t))
                    if t >= 3:
                        eng.wait_ge(s_o[t % 3], 16 * (t // 3))
                    eng.activation(OR[t % 3][:, 512:1024], PS[:, (2 * t) % 8 + 1, :], ACT.Copy).then_inc(*ac.did("hi", t))

            @program("sp")
            def _(eng):
                for t in range(NT):
                    eng.wait_ge(ve.sem, ve.at("lo", t))
                    eng.wait_ge(ac.sem, ac.at("hi", t))
                    dst = OUT["y_sample"][0, t * P:(t + 1) * P, :] if t < NS // P else OUT["y_prompt"][0, t * P - NS:(t + 1) * P - NS, :]
                    eng.dma_start(dst, OR[t % 3]).then_inc(s_o[t % 3], 16)
                for i in range(3):
                    eng.wait_ge(s_o[i], 16 * len(range(i, NT, 3)))

        store(prev, True)

        block = ctx.enter_context(nc.Block())

        @block.sync
        def _(eng):
            for f in progs["sp"]:
                f(eng)

        @block.tensor
        def _(eng):
            for f in progs["pe"]:
                f(eng)

        @block.vector
        def _(eng):
            for f in progs["ve"]:
                f(eng)

        @block.scalar
        def _(eng):
            for f in progs["ac"]:
                f(eng)

        @block.gpsimd
        def _(eng):
            for f in progs["po"]:
                f(eng)


_OUTS = {"y_prompt": (1, NP_, D), "y_sample": (1, NS, D), "new_f": (1, HEADS, P, P), "new_b": (1, HEADS, P, P)}


def kernel(**inputs):
    import concourse.bacc as bacc
    from concourse.bass_utils import run_bass_kernel_spmd

    nc = bacc.Bacc("TRN2", target_bir_lowering=False, num_devices=1)
    arrays, A, OUT = {}, {}, {}
    for name, a in {**inputs, **constants()}.items():
        a = np.ascontiguousarray(a)
        arrays[f"in_{name}"] = a
        A[name] = nc.dram_tensor(f"in_{name}", a.shape, mybir.dt.from_np(a.dtype), kind="ExternalInput").ap()
    for name, shape in _OUTS.items():
        OUT[name] = nc.dram_tensor(f"out_{name}", shape, F32, kind="ExternalOutput").ap()
    build(nc, A, OUT)
    r = run_bass_kernel_spmd(nc, [arrays], core_ids=[0])
    return tuple(r.results[0][f"out_{name}"] for name in _OUTS)
```

```python
import math
from contextlib import ExitStack

import concourse.bass as bass
import numpy as np
from concourse import mybir

F32 = mybir.dt.float32
F32R = mybir.dt.float32r
ALU = mybir.AluOpType
ACT = mybir.ActivationFunctionType

P = 128
D = 1024
KD = D // P
NS, NP_ = 1024, 256
N = NS + NP_
NT = N // P
GROUPS = [(0, NS, 0), (NS, NP_, 1)]
CHUNKS = [(0, 512), (512, 512), (1024, 256)]
EPS = 1e-6
HEADS = 4
GRID_W = 64
ROWS = NS // GRID_W
HIDDEN = 2816
KH = HIDDEN // P
WINDOWS = (2, 4, 8, 16)
AB_AT = 2048
POOL_AT = 2064
BIG = 1e30
BASE, ARENA = 16512, 53200
FFN64 = 64
EMB = 33
HC = 256
NCH = D // HC
LEVELS = 7

VECTORS = [("l0_ada_b", 48), ("l0_norm1", 8), ("l0_norm2", 8), ("l0_dn_conv_w", 36), ("l0_dn_norm_w", 1),
           ("l0_pool_scale", 4), ("l0_ffn_conv_w", 198), ("l0_ffn_conv_b", 22), ("l1_ada_b", 48),
           ("l1_norm1", 8), ("l1_norm2", 8), ("l1_hy_short_w", 72), ("l1_hy_short_b", 24),
           ("l1_ffn_conv_w", 198), ("l1_ffn_conv_b", 22), ("final_norm", 8),
           ("l1_hy_freq", 1), ("l1_hy_b1", 1), ("l1_hy_b2", 1), ("l1_hy_b3", 1)]
VCOL, _at = {}, 0
for _n, _r in VECTORS:
    VCOL[_n] = _at
    _at += _r
VTILES = -(-_at // P)



def constants():
    i = np.arange(P)
    r, c = i[:, None], i[None, :]
    sq = np.zeros((P, 8, P))
    sq[:, 0] = r == c
    sq[:, 1] = 1
    sq[:, 2] = r <= c
    sq[:, 3] = r >= c
    sq[:, 4] = np.where(c < r, 0, BIG)
    sq[:, 5] = np.where(c >= r, 0, -BIG)
    sq[:, 6] = np.where(c > r, 0, BIG)
    sq[:, 7] = np.where(c <= r, 0, -BIG)
    level = np.zeros((P, 2, LEVELS, P))
    for v in range(LEVELS):
        b = 1 << v
        m = (r // (2 * b) == c // (2 * b)) & ((r // b) % 2 == 1) & ((c // b) % 2 == 0)
        level[:, 0, v], level[:, 1, v] = m, m.T
    inv = np.zeros((4, N))
    for g, w in enumerate(WINDOWS):
        for a, n, _ in GROUPS:
            t = np.arange(n)
            inv[g, a:a + n] = 1.0 / (np.clip(t + w - w // 2, 0, n) - np.clip(t - w // 2, 0, n))
    out = {"k_squares": sq.reshape(P, -1), "k_level": level.reshape(P, -1), "k_inv": inv}

    for name, L in (("s", NS), ("p", NP_)):
        T = L // P
        pos = np.concatenate([np.arange(L), L - np.arange(L)]).astype(np.float32)
        t01 = (pos / np.float32(L - 1)).astype(np.float32)
        bands = np.linspace(1e-4, 15, 16, dtype=np.float32)
        ang = (np.float32(2.0 * math.pi / L) * pos[:, None] * bands[None, :]).astype(np.float32)
        feat = np.concatenate([t01[:, None], np.cos(ang), -np.sin(ang)], axis=-1)
        out["k_feat_" + name] = feat.T
        cols = np.zeros((P, 2, 2 * T))
        cols[:, 0] = -t01.reshape(2 * T, P).T
        cols[0, 1, T] = -1e4
        out["k_win_" + name] = cols.reshape(P, -1)
    lo, hi = math.log(1e-2) / 1.5, math.log(1e-2) / 0.3
    out["k_delta"] = np.abs(np.linspace(lo, hi, D, dtype=np.float32))[None, :]

    fwd, inv8, spec = np.zeros((P, 8, 2, 2, P)), np.zeros((P, 8, 2, 2, P)), np.zeros((P, 2, 2, P))
    n = j = np.arange(128.0)
    for leaf, th in enumerate(LEAF_ANGLES):
        if leaf == 0:
            for half in range(2):
                m = n + 128 * half
                a = 2 * math.pi * np.outer(m, j) / 256
                alt = (-1.0) ** m
                fwd[:, 0, half, 0] = np.cos(a)
                fwd[:, 0, half, 1] = np.sin(a)
                fwd[:, 0, half, 1, 0] = alt
                spec[:, half, 0] = np.sin(a)
                spec[:, half, 0, 0] = 0
                spec[:, half, 1] = np.cos(a)
                spec[:, half, 1, 0] = alt
                ci, si = np.cos(a).T / 128, np.sin(a).T / 128
                ci[0], si[0] = 1 / 256, alt / 256
                inv8[:, 0, 0, half], inv8[:, 0, 1, half] = ci / 8, si / 8
            continue
        a = np.outer(n, (th + 2 * math.pi * j) / 128)
        fwd[:, leaf, 0, 0], fwd[:, leaf, 1, 0] = np.cos(a), -np.sin(a)
        fwd[:, leaf, 0, 1], fwd[:, leaf, 1, 1] = np.sin(a), np.cos(a)
        b = a.T
        inv8[:, leaf, 0, 0], inv8[:, leaf, 1, 0] = np.cos(b) / 1024, np.sin(b) / 1024
        inv8[:, leaf, 0, 1], inv8[:, leaf, 1, 1] = -np.sin(b) / 1024, np.cos(b) / 1024
    def packed(m, sin, neg):
        rest = np.stack([m[:, 1:, 0, 0], m[:, 1:, sin[0], sin[1]], m[:, 1:, neg[0], neg[1]]], axis=2)
        return np.concatenate([m[:, 0].reshape(P, -1), rest.reshape(P, -1)], axis=1)
    out["k_fwd"], out["k_inv8"] = packed(fwd, (0, 1), (1, 0)), packed(inv8, (1, 0), (0, 1))
    out["k_spec"] = spec.reshape(P, -1)
    return {k: np.ascontiguousarray(v, dtype=np.float32) for k, v in out.items()}


LEAF_ANGLES = [0.0, math.pi / 2, math.pi / 4, 5 * math.pi / 4, math.pi / 8, 9 * math.pi / 8,
               5 * math.pi / 8, 13 * math.pi / 8]


class Steps:

    def __init__(self, sem, names, rounds=1, before=0):
        self.sem, self.names, self.rounds, self.before = sem, list(names), rounds, before
        self.index = {s: i for i, s in enumerate(self.names)}
        assert len(self.index) == len(self.names)
        self.made = 0

    def at(self, step, round_=0):
        return self.before + round_ * len(self.names) + self.index[step] + 1

    def end(self):
        return self.before + self.rounds * len(self.names)

    def did(self, step, round_=0):
        self.made += 1
        assert self.before + self.made == self.at(step, round_), (self.names, step, round_, self.made)
        return self.sem, 1


def build(nc, A, OUT):
    with ExitStack() as ctx:
        def sem(name):
            return ctx.enter_context(nc.semaphore(name))

        pieces = []
        PS = ctx.enter_context(nc.psum_tensor("PS", [P, 8, 512], F32))
        PSF = PS[:, :, :].rearrange("p b n -> p (b n)")

        class Region:

            def __init__(self, a, b):
                self.a, self.b = a, b

            def take(self, *shape, dtype=F32):
                n = math.prod(shape)
                self.a = -(-self.a // 8) * 8
                assert self.a + n <= self.b, (self.a, n, self.b)
                pieces.append(nc.alloc_sbuf_tensor_at(f"piece{len(pieces)}", [P, n], dtype, offset=BASE + 4 * self.a))
                v = pieces[-1][:, :]
                self.a += n
                if len(shape) == 2:
                    v = v.rearrange("p (a b) -> p a b", b=shape[1])
                if len(shape) == 3:
                    v = v.rearrange("p (a b c) -> p a b c", b=shape[1], c=shape[2])
                return v

            def half(self, *shape):
                v = self.take(*shape, dtype=F32R)
                return v, v.bitcast(F32)

        XT_AT, HT_AT, FIX_AT, W_AT = 0, KD * N, 3 * KD * N, 3 * KD * N + 1400
        XT = Region(XT_AT, HT_AT).take(KD, N)
        hr = Region(HT_AT, FIX_AT)
        (HH, HH32), (HL, _) = hr.half(KD, N), hr.half(KD, N)
        fix = Region(FIX_AT, W_AT)
        VC = fix.take(VTILES * P)
        ident = fix.take(P)
        ones = fix.take(P)
        MOD = fix.take(2, 48, 2)
        SCALE_A = fix.take(5, KD, 2)
        eps = fix.take(1)
        half_pi = fix.take(1)
        CS = fix.take(KD, 2)
        CH, CH32 = fix.half(KD, 4)

        def vec(name, i=0, n=1):
            return VC[:, VCOL[name] + i:VCOL[name] + i + n]

        def psum(bank, n):
            return PSF[:, bank * 512:bank * 512 + n]

        def bcast(ap, n):
            return ap.unsqueeze(2).to_broadcast([ap.shape[0], ap.shape[1], n])

        def over(ap, n):
            return ap.unsqueeze(1).to_broadcast([P, n, ap.shape[1]])

        used = {}

        def steps(name, names, rounds=1):
            handle, before = used.get(name) or (sem(name), 0)
            s = Steps(handle, names, rounds, before)
            used[name] = handle, s.end()
            return s

        landings = {}

        class Landing:

            def __init__(self, name, count):
                self.sem, self.before = landings.get(name) or (sem(name), 0)
                landings[name] = self.sem, self.before + 16 * count

            def at(self, k):
                return self.sem, self.before + 16 * k

        def ended(eng, *which):
            for s in which:
                eng.wait_ge(s.sem, s.end())

        progs = {"sp": [], "pe": [], "ve": [], "ac": [], "po": []}

        def program(engine):
            def add(f):
                progs[engine].append(f)
                return f
            return add

        w = Region(W_AT, ARENA)
        VR = w.take(VTILES, P)
        s_const, s_rows, s_cond = sem("const_landed"), sem("vector_rows_landed"), sem("cond_landed")
        ve0 = steps("ve_setup", ["zero_rows", "eps", "half_pi", "pair"])
        pe0 = steps("pe_setup", ["turn0", "turn1"])
        ac0 = steps("ac_setup", ["cols0", "cols1", "silu", "hi"])
        ve00 = steps("ve_setup_cond", ["lo"])
        CR = w.take(2, KD)
        nvec = [0]

        @program("sp")
        def _(sp):
            for dst, k in ((ident, 0), (ones, 1)):
                sp.dma_start(dst, A["k_squares"][:, k * P:(k + 1) * P]).then_inc(s_const, 16)
            for j, name in enumerate(("c", "c_ctx")):
                src = A[name].rearrange("a b -> (a b)") if name == "c" else A[name]
                sp.dma_start(CR[:, j, :], src.rearrange("(p k) -> p k", p=P)).then_inc(s_cond, 16)
            sp.wait_ge(ve0.sem, ve0.at("zero_rows"))
            for name, rows in VECTORS:
                src = A[name]
                src = src if len(src.shape) == 1 else (src.rearrange("a b -> (a b)") if len(src.shape) == 2 else src.rearrange("a b c -> (a b c)"))
                width = min(P, src.shape[0])
                src = src.rearrange("(r c) -> r c", c=width)
                at, done = VCOL[name], 0
                while done < rows:
                    n = min(rows - done, P - at % P)
                    sp.dma_start(VR[at % P:at % P + n, at // P, 0:width], src[done:done + n, :]).then_inc(s_rows, 16)
                    nvec[0] += 1
                    done += n
                    at += n

        @program("pe")
        def _(pe):
            pe.wait_ge(s_const, 32)
            pe.wait_ge(s_rows, 16 * nvec[0])
            for half in range(2):
                for t in range(3):
                    m = pe.transpose(PS[:, half, t * P:(t + 1) * P], VR[:, 3 * half + t, :], ident)
                m.then_inc(*pe0.did(f"turn{half}"))

        @program("ve")
        def _(ve):
            ve.memset(VR, 0.0).then_inc(*ve0.did("zero_rows"))
            ve.memset(eps, EPS).then_inc(*ve0.did("eps"))
            ve.memset(half_pi, math.pi / 2).then_inc(*ve0.did("half_pi"))
            ve.wait_ge(s_cond, 32)
            ve.tensor_copy(CS.rearrange("p k j -> p j k"), CR).then_inc(*ve0.did("pair"))
            ve.wait_ge(ac0.sem, ac0.at("hi"))
            ve.tensor_tensor(CH[:, :, 2:4], CS, CH32[:, :, 0:2], ALU.subtract).then_inc(*ve00.did("lo"))

        @program("ac")
        def _(ac):
            for half in range(2):
                ac.wait_ge(pe0.sem, pe0.at(f"turn{half}"))
                ac.activation(VC[:, half * 384:(half + 1) * 384], PS[:, half, 0:384], ACT.Copy)\
                    .then_inc(*ac0.did(f"cols{half}"))
            ac.wait_ge(ve0.sem, ve0.at("pair"))
            ac.activation(CS, CS, ACT.Silu).then_inc(*ac0.did("silu"))
            ac.wait_ge(ac0.sem, ac0.at("silu"))
            ac.activation(CH[:, :, 0:2], CS, ACT.Copy).then_inc(*ac0.did("hi"))

        def load_x(r, slots, pairs):
            XR = [r.take(D) for _ in range(slots)]
            s_x = [sem(f"x_landed{slots}_{i}") for i in range(slots)]
            pe = steps("pe_x", ["lo", "hi"], NT)
            ve = steps("ve_x", ["lo"], NT)
            ac = steps("ac_x", ["hi"], NT)

            def bank(t):
                return pairs[t % len(pairs)]

            def fetch(eng, t):
                if t >= slots:
                    eng.wait_ge(pe.sem, pe.at("hi", t - slots))
                src = A["x_sample"][0, t * P:(t + 1) * P, :] if t < NS // P else A["x_prompt"][0, t * P - NS:(t + 1) * P - NS, :]
                eng.dma_start(XR[t % slots], src).then_inc(s_x[t % slots], 16)

            def turn(eng, t):
                eng.wait_ge(s_x[t % slots], 16 * (t // slots + 1))
                for half, who in ((0, ve), (1, ac)):
                    if t >= len(pairs):
                        eng.wait_ge(who.sem, who.at(("lo", "hi")[half], t - len(pairs)))
                    for k in range(4):
                        kk = 4 * half + k
                        m = eng.transpose(PS[:, bank(t) + half, k * P:(k + 1) * P], XR[t % slots][:, kk * P:(kk + 1) * P], ident)
                    m.then_inc(*pe.did(("lo", "hi")[half], t))

            def low_channels(eng, t):
                eng.wait_ge(pe.sem, pe.at("lo", t))
                eng.tensor_copy(XT[:, 0:4, t * P:(t + 1) * P], PS[:, bank(t), :].rearrange("p (k t) -> p k t", t=P)).then_inc(*ve.did("lo", t))

            def high_channels(eng, t):
                eng.wait_ge(pe.sem, pe.at("hi", t))
                eng.activation(XT[:, 4:8, t * P:(t + 1) * P], PS[:, bank(t) + 1, :].rearrange("p (k t) -> p k t", t=P), ACT.Copy).then_inc(*ac.did("hi", t))
            return [pe, ve, ac], fetch, turn, low_channels, high_channels

        w = Region(W_AT + 1024, ARENA)
        RAWS = 3
        AW = [w.take(KD, 512) for _ in range(RAWS)]
        ALO = [w.half(KD, 512)]
        w = Region(HT_AT, HT_AT + KD * N)
        AHI = [w.half(KD, 512) for _ in range(2)]
        AR = [w.take(512) for _ in range(2)]
        w = Region(HT_AT + KD * N, FIX_AT)
        ALO.append(w.half(KD, 512))
        x_steps, x_fetch, x_turn, x_low, x_high = load_x(w, 6, (6, 0))
        NA = 24
        s_aw = [sem(f"ada_w_landed{i}") for i in range(RAWS)]
        peA, peT0 = steps("pe_ada", ["rows"], NA), steps("pe_ada_turn", ["turn"], NA)
        acA = steps("ac_ada", ["hi"], NA)
        veL, veR = steps("ve_ada_low", ["lo"], NA), steps("ve_ada_rows", ["rows"], NA)
        veM = steps("ve_mod", ["hi0", "hi1", "mod0", "mod1"] + [f"plus{i}" for i in range(4)] + [f"scale{i}" for i in range(5)])

        @program("sp")
        def _(sp):
            for t in range(3):
                x_fetch(sp, t)
            for n in range(NA):
                if 3 <= n < NT:
                    x_fetch(sp, n)
                if n >= RAWS:
                    sp.wait_ge(veL.sem, veL.at("lo", n - RAWS))
                layer, m = divmod(n, 12)
                src = A[f"l{layer}_ada_w"].rearrange("(p k) n -> p k n", k=KD)[:, :, m * 512:(m + 1) * 512]
                sp.dma_start(AW[n % RAWS], src).then_inc(s_aw[n % RAWS], 16)

        @program("ac")
        def _(ac):
            for n in range(NA):
                ac.wait_ge(s_aw[n % RAWS], 16 * (n // RAWS + 1))
                if n >= 2:
                    ac.wait_ge(peA.sem, peA.at("rows", n - 2))
                ac.activation(AHI[n % 2][0], AW[n % RAWS], ACT.Copy).then_inc(*acA.did("hi", n))
                if 1 <= n <= NT:
                    x_high(ac, n - 1)

        @program("pe")
        def _(pe):
            pe.wait_ge(ve00.sem, ve00.at("lo"))
            for n in range(NA + 1):
                if n < NT:
                    x_turn(pe, n)
                if n < NA:
                    pe.wait_ge(veL.sem, veL.at("lo", n))
                    if n >= 2:
                        pe.wait_ge(veR.sem, veR.at("rows", n - 2))
                    for k in range(KD):
                        for w_n, w in enumerate((AHI, ALO)):
                            m = pe.matmul(PS[0:4, 2 + n % 2, :], CH[:, k, :], w[n % 2][0][:, k, :], start=k == 0 and w_n == 0, stop=k == KD - 1 and w_n == 1)
                    m.then_inc(*peA.did("rows", n))
                if n:
                    pe.wait_ge(veR.sem, veR.at("rows", n - 1))
                    for j in range(4):
                        c = (4 * (n - 1) + j) * 4
                        m = pe.transpose(PS[:, 4, c:c + 4], AR[(n - 1) % 2][0:4, j * P:(j + 1) * P], ident[0:4, 0:4])
                    m.then_inc(*peT0.did("turn", n - 1))

        @program("ve")
        def _(ve):
            for n in range(NA + 1):
                if n < NA:
                    ve.wait_ge(acA.sem, acA.at("hi", n))
                    if n >= 2:
                        ve.wait_ge(peA.sem, peA.at("rows", n - 2))
                    ve.tensor_tensor(ALO[n % 2][0], AW[n % RAWS], AHI[n % 2][1], ALU.subtract).then_inc(*veL.did("lo", n))
                if n:
                    ve.wait_ge(peA.sem, peA.at("rows", n - 1))
                    if n >= 3:
                        ve.wait_ge(peT0.sem, peT0.at("turn", n - 3))
                    ve.tensor_copy(AR[(n - 1) % 2][0:4, :], PS[0:4, 2 + (n - 1) % 2, :]).then_inc(*veR.did("rows", n - 1))
                if 1 <= n <= NT:
                    x_low(ve, n - 1)
            ve.wait_ge(peT0.sem, peT0.end())
            ve.wait_ge(ac0.sem, ac0.at("cols1"))
            for layer in range(2):
                two = PS[:, 4, 192 * layer:192 * layer + 192].rearrange("p (m h j) -> p m h j", h=2, j=2)
                ve.tensor_tensor(MOD[:, layer], two[:, :, 0, :], bcast(vec(f"l{layer}_ada_b", 0, 48), 2), ALU.add).then_inc(*veM.did(f"hi{layer}"))
            ve.wait_ge(veM.sem, veM.at("hi1"))
            for layer in range(2):
                two = PS[:, 4, 192 * layer:192 * layer + 192].rearrange("p (m h j) -> p m h j", h=2, j=2)
                ve.tensor_tensor(MOD[:, layer], MOD[:, layer], two[:, :, 1, :], ALU.add).then_inc(*veM.did(f"mod{layer}"))
            ve.wait_ge(veM.sem, veM.at("mod1"))
            for i in range(4):
                layer, second = divmod(i, 2)
                at = 8 + 24 * second
                ve.tensor_scalar(SCALE_A[:, i], MOD[:, layer, at:at + 8, :], 1.0, None, ALU.add)\
                    .then_inc(*veM.did(f"plus{i}"))
            ve.wait_ge(veM.sem, veM.at("plus3"))
            for i in range(4):
                layer, second = divmod(i, 2)
                ve.tensor_tensor(SCALE_A[:, i], SCALE_A[:, i], bcast(vec(f"l{layer}_norm{second + 1}", 0, 8), 2),
                                 ALU.mult).then_inc(*veM.did(f"scale{i}"))
            ve.tensor_copy(SCALE_A[:, 4], bcast(vec("final_norm", 0, 8), 2)).then_inc(*veM.did("scale4"))

        prev = [pe0, ve0, ve00, ac0, peA, peT0, acA, veL, veR, veM] + x_steps

        LO_ON_VE = (2, 5, 7)

        W_FREE, HL_END = (W_AT, W_AT + 3 * N), (FIX_AT - 3 * N, FIX_AT)

        def norm(prev, x_ready, squares, which, shift, early):
            r = Region(*squares)
            SQ = [r.take(N) for _ in range(3)]
            r = Region(W_AT + 3 * N, W_AT + 8 * N)
            T = [r.take(N) for _ in range(4)]
            RS = r.take(N)
            ac = steps("ac_norm", ["sq"], KD)
            ac2 = steps("ac_norm_r", ["root"])
            ac3 = steps("ac_norm_m", sum([[f"s{k}", f"p{k}"] + ([] if k in LO_ON_VE else [f"hi{k}"]) for k in range(KD)], []))
            pe = steps("pe_norm", ["sum"])
            poS = steps("po_norm_sum", [f"add{k}" for k in range(1, KD)])
            ve = steps("ve_norm_r", ["inv"])
            names = []
            for k in range(KD + 1):
                names += [f"s{k}", f"p{k}"] if k < KD else []
                names += [f"lo_s{k - 1}", f"lo_p{k - 1}"] if k - 1 in LO_ON_VE else []
            ve2 = steps("ve_norm", names)
            po_tiles = [k for k in range(KD) if k not in LO_ON_VE]
            po = steps("po_norm", [f"lo{k}" for k in po_tiles])

            def wait_lo(eng, k):
                eng.wait_ge(*((ve2.sem, ve2.at(f"lo_p{k}")) if k in LO_ON_VE else (po.sem, po.at(f"lo{k}"))))

            @program("pe")
            def _(eng):
                ended(eng, *prev)
                eng.wait_ge(poS.sem, poS.end())
                for b, (a, n) in enumerate(CHUNKS):
                    m = eng.matmul(PS[:, b, 0:n], ones, SQ[0][:, a:a + n], start=True, stop=True)
                m.then_inc(*pe.did("sum"))

            def slot(k):
                return SQ[1 + k % 2 if k else 0]

            @program("ac")
            def _(eng):
                for k in range(KD):
                    x_ready(eng, k)
                    if k >= 3:
                        eng.wait_ge(poS.sem, poS.at(f"add{k - 2}"))
                    eng.activation(slot(k), XT[:, k, :], ACT.Square).then_inc(*ac.did("sq", k))
                ended(eng, *prev)
                eng.wait_ge(pe.sem, pe.end())
                eng.activation(RS, psum(0, N), ACT.Sqrt, scale=1.0 / D, bias=eps).then_inc(*ac2.did("root"))
                early["ac"](eng)
                for k in range(KD):
                    eng.wait_ge(ve2.sem, ve2.at(f"p{k}"))
                    for (a, n, j), g in zip(GROUPS, "sp"):
                        dst = (HH[:, k] if k in LO_ON_VE else T[k % 4])[:, a:a + n]
                        eng.activation(dst, T[k % 4][:, a:a + n], ACT.Identity, bias=shift(k, j)).then_inc(*ac3.did(f"{g}{k}"))
                    if k not in LO_ON_VE:
                        eng.wait_ge(ac3.sem, ac3.at(f"p{k}"))
                        eng.activation(HH[:, k, :], T[k % 4], ACT.Copy).then_inc(*ac3.did(f"hi{k}"))

            @program("ve")
            def _(eng):
                eng.wait_ge(ac2.sem, ac2.at("root"))
                eng.reciprocal(RS, RS).then_inc(*ve.did("inv"))
                eng.wait_ge(ve.sem, ve.at("inv"))
                for k in range(KD + 1):
                    if k < KD:
                        if k >= 4:
                            wait_lo(eng, k - 4)
                        for (a, n, j), g in zip(GROUPS, "sp"):
                            eng.scalar_tensor_tensor(T[k % 4][:, a:a + n], XT[:, k, a:a + n], SCALE_A[:, which, k, j:j + 1], RS[:, a:a + n],
                                                     ALU.mult, ALU.mult).then_inc(*ve2.did(f"{g}{k}"))
                    if k - 1 in LO_ON_VE:
                        eng.wait_ge(ac3.sem, ac3.at(f"p{k - 1}"))
                        for (a, n, j), g in zip(GROUPS, "sp"):
                            eng.scalar_tensor_tensor(HL[:, k - 1, a:a + n], T[(k - 1) % 4][:, a:a + n], shift(k - 1, j), HH32[:, k - 1, a:a + n],
                                                     ALU.add, ALU.subtract).then_inc(*ve2.did(f"lo_{g}{k - 1}"))

            @program("po")
            def _(eng):
                for k in range(1, KD):
                    eng.wait_ge(ac.sem, ac.at("sq", k))
                    if k > 1:
                        eng.wait_ge(poS.sem, poS.at(f"add{k - 1}"))
                    eng.tensor_tensor(SQ[0], SQ[0], slot(k), ALU.add).then_inc(*poS.did(f"add{k}"))
                early["po"](eng)
                for k in po_tiles:
                    eng.wait_ge(ac3.sem, ac3.at(f"hi{k}"))
                    eng.tensor_tensor(HL[:, k, :], T[k % 4], HH32[:, k, :], ALU.subtract).then_inc(*po.did(f"lo{k}"))
            return [pe, poS, ac, ac2, ac3, ve, ve2, po], wait_lo

        spill = nc.dram_tensor("x_spill", (P, KD, N), F32, kind="Internal").ap()

        def weight_ring(region, count):
            RAW = [region.take(1024) for _ in range(2)]
            HI = [region.half(1024) for _ in range(2)]
            LO = [region.half(1024) for _ in range(2)]

            class Ring:
                landed = [Landing(f"w_landed{i}", len(range(i, count, 2))) for i in range(2)]
                pe = steps("pe_w", ["used"], count)
                ac = steps("ac_w", ["hi"], count)
                po = steps("po_w", ["lo"], count)

                def load(self, eng, i, src, shape):
                    if i >= 2:
                        eng.wait_ge(self.po.sem, self.po.at("lo", i - 2))
                        eng.wait_ge(self.ac.sem, self.ac.at("hi", i - 2))
                    eng.dma_start(self.view(RAW[i % 2], shape), src).then_inc(self.landed[i % 2].sem, 16)

                def view(self, slot, shape):
                    return slot[:, 0:shape[0] * shape[1]].rearrange("p (a b) -> p a b", b=shape[1])

                def hi(self, eng, i, n=1024):
                    if i >= count:
                        return
                    eng.wait_ge(*self.landed[i % 2].at(i // 2 + 1))
                    if i >= 2:
                        eng.wait_ge(self.pe.sem, self.pe.at("used", i - 2))
                    eng.activation(HI[i % 2][0][:, 0:n], RAW[i % 2][:, 0:n], ACT.Copy).then_inc(*self.ac.did("hi", i))

                def lo(self, eng, i, n=1024):
                    if i >= count:
                        return
                    eng.wait_ge(self.ac.sem, self.ac.at("hi", i))
                    eng.tensor_tensor(LO[i % 2][0][:, 0:n], RAW[i % 2][:, 0:n], HI[i % 2][1][:, 0:n], ALU.subtract)\
                        .then_inc(*self.po.did("lo", i))

                def ready(self, eng, i):
                    eng.wait_ge(self.po.sem, self.po.at("lo", i))

                def get(self, i, shape):
                    return self.view(HI[i % 2][0], shape), self.view(LO[i % 2][0], shape)
            return Ring()

        def product(eng, bank, weights, halves_of, first, last):
            wh, wl = weights
            xh, xl = halves_of
            for n_, (w, x) in enumerate(((wh, xh), (wh, xl), (wl, xh))):
                for b, (a, n) in enumerate(CHUNKS):
                    m = eng.matmul(PS[:, bank + b, 0:n], w, x[:, a:a + n], start=first and n_ == 0, stop=last and n_ == 2)
            return m

        def mod(layer, part):
            return lambda k, j: MOD[:, layer, 8 * part + k, j:j + 1]

        def mixer_even(before_norm, prev, h_ready, early):
            x_r = Region(XT_AT, HT_AT)
            PO, KT = x_r.take(HEADS, N), x_r.take(HEADS, N)
            r = Region(W_AT, ARENA)
            QT, VT = r.take(HEADS, N), r.take(HEADS, N)
            late = Region(r.a, r.a + 8712)
            ring_at = Region(r.a, r.a + 6144)
            r.a += 6144
            PADN = N + 4
            PAD, CV = r.take(PADN), r.take(PADN)
            POW, ABW = r.take(4, P), r.take(KD, 16)
            ABS, GG, BT, TA = r.take(NT, 16), r.take(NT, 8), r.take(NT, 8), r.take(NT, 8)
            DTB, ALOG = r.take(8), r.take(8)
            ABH, ABL = r.half(KD, 16), r.half(KD, 16)
            SQM, LVM = late.take(6, P), late.take(2, LEVELS, P)
            OT = Region(XT_AT, HT_AT).take(HEADS, N)
            top = Region(W_AT, W_AT + 2 * HEADS * N)
            GAP = 8
            WU = GAP + NS + GAP + NP_ + GAP
            UPAD, PA, PB, INV = top.take(WU), top.take(WU), top.take(WU), top.take(N)
            SQ = VT[:, 2, :]
            RBS = [VT[:, 1 if n in (1, 3, 5) else 3, :] for n in range(2 * HEADS)]
            z_dram = nc.dram_tensor("z_gate", (HEADS, P, N), F32, kind="Internal").ap()
            s_z = [sem(f"z_stored{i}") for i in range(2)]
            w_in = A["l0_w_in"].rearrange("(k p) n -> p k n", p=P)
            tiles = [("pool", g, POOL_AT + g * P) for g in range(4)]
            for kind, at in (("k", 512), ("q", 0), ("v", 1024), ("z", 1536)):
                tiles += [(kind, g, at + g * P) for g in range(HEADS)]
            n_t = len(tiles)
            dest = {"q": QT, "k": KT, "v": VT}
            pos = {"q": 0, "k": 4, "v": 8}
            ring = weight_ring(ring_at, n_t)
            norm_tiles = [(KT, g, 1.0) for g in range(4)] + [(QT, g, float(P) ** -0.5) for g in range(4)]
            N_L2, SUM = len(norm_tiles), 6 * 512
            peN, veN = steps("pe_l2", ["s", "p"], N_L2), steps("ve_l2", ["inv", "mul"], N_L2)
            acN, acR = steps("ac_l2", ["sq"], N_L2), steps("ac_l2r", ["s", "p"], N_L2)
            s_spill = sem("x_spilled0")
            s_small, s_mask, s_inv = sem("mix0_small_landed"), sem("masks_landed"), sem("inv_landed")
            early.update(ac=lambda eng: [ring.hi(eng, i) for i in range(2)], po=lambda eng: [ring.lo(eng, i) for i in range(2)])
            pe = ring.pe
            acB, poB = steps("ac_abw", ["hi"]), steps("po_abw", ["lo"])
            peAB = steps("pe_ab", ["ab"])
            ac = steps("ac_in0", ["s", "p"], n_t)
            acS = steps("ac_silu0", ["s", "p"], 12)
            veZ = steps("ve_zero0", ["pad", "upad"])
            ve_names, doubled = [], {}
            for g, w in enumerate(WINDOWS):
                doubled[g] = int(math.log2(w))
                ve_names += [f"pool{g}.d{i}" for i in range(doubled[g])] + [f"pool{g}.m{j}" for j in "sp"] + [f"pool{g}.u{j}" for j in "sp"]
            ve_names += [f"conv{i}.{k}" for i in range(12) for k in range(3)]
            ve = steps("ve_in0", ve_names)

            @program("sp")
            def _(eng):
                ended(eng, *before_norm)
                for i, (kind, g, at) in enumerate(tiles):
                    ring.load(eng, i, w_in[:, :, at:at + P], (KD, P))
                    if i == 1:
                        eng.dma_start(spill, XT).then_inc(s_spill, 16)
                        ended(eng, *prev)
                        eng.dma_start(POW, A["l0_pool_w"].rearrange("g i o -> i g o")).then_inc(s_small, 16)
                        eng.dma_start(ABW, w_in[:, :, AB_AT:AB_AT + 16]).then_inc(s_small, 16)
                        for dst, name in ((DTB, "l0_dn_dt_bias"), (ALOG, "l0_dn_a_log")):
                            eng.dma_start(dst, A[name].rearrange("a b -> (a b)").partition_broadcast(P)).then_inc(s_small, 16)
                    if 1 <= i < 5:
                        if i > 1:
                            eng.wait_ge(ve.sem, ve.at(f"pool{i - 2}.mp"))
                        eng.dma_start(INV, A["k_inv"][i - 1, :].partition_broadcast(P)).then_inc(s_inv, 16)
                for g in range(HEADS):
                    eng.wait_ge(ac.sem, ac.at("p", n_t - HEADS + g))
                    eng.dma_start(z_dram[g], (PAD, CV)[g % 2][:, 0:N]).then_inc(s_z[g % 2], 16)

            @program("pe")
            def _(eng):
                for i in range(n_t):
                    ring.ready(eng, i)
                    if i >= 2:
                        eng.wait_ge(ac.sem, ac.at("p", i - 2))
                    n = i - 7
                    wh, wl = ring.get(i, (KD, P))
                    for k in range(KD):
                        if i == 0:
                            h_ready(eng, k)
                        if 0 <= n < N_L2 and k == KD // 2:
                            eng.wait_ge(acN.sem, acN.at("sq", n))
                            if n:
                                eng.wait_ge(acR.sem, acR.at("p", n - 1))
                            for a in (0, 512):
                                m = eng.matmul(PSF[:, SUM + a:SUM + a + 512], ones, SQ[:, a:a + 512], start=True, stop=True)
                            m.then_inc(*peN.did("s", n))
                        if 0 <= n < N_L2 and k == KD - 1:
                            eng.wait_ge(acR.sem, acR.at("s", n))
                            eng.matmul(PSF[:, SUM:SUM + NP_], ones, SQ[:, NS:N], start=True, stop=True).then_inc(*peN.did("p", n))
                        m = product(eng, 3 * (i % 2), (wh[:, k, :], wl[:, k, :]), (HH[:, k], HL[:, k]), k == 0, k == KD - 1)
                    m.then_inc(*pe.did("used", i))
                eng.wait_ge(poB.sem, poB.end())
                eng.wait_ge(acR.sem, acR.end())
                for c in range(NT):
                    for k in range(KD):
                        for n_, (x, w) in enumerate(((HH, ABH), (HL, ABH), (HH, ABL))):
                            m = eng.matmul(PS[:, 6, c * 16:(c + 1) * 16], x[:, k, c * P:(c + 1) * P], w[0][:, k, :],
                                           start=k == 0 and n_ == 0, stop=k == KD - 1 and n_ == 2)
                m.then_inc(*peAB.did("ab"))

            def silu(eng, i):
                kind, g, _ = tiles[4 + i]
                eng.wait_ge(ve.sem, ve.at(f"conv{i}.2"))
                if i == 0:
                    eng.wait_ge(s_spill, 16)
                if i == 10:
                    eng.wait_ge(peN.sem, peN.end())
                if i in (9, 11):
                    eng.wait_ge(veN.sem, veN.at("mul", 5 if i == 9 else 7))
                for a, n, j in GROUPS:
                    eng.activation(dest[kind][:, g, a:a + n], CV[:, 1 + a + 2 * j:1 + a + 2 * j + n], ACT.Silu).then_inc(*acS.did("sp"[j], i))

            @program("ac")
            def _(eng):
                ended(eng, *prev)
                eng.wait_ge(veZ.sem, veZ.end())
                for i, (kind, g, _) in enumerate(tiles):
                    if 0 <= i - 7 < N_L2:
                        eng.wait_ge(peN.sem, peN.at("s", i - 7))
                        RB, before = RBS[i - 7], i - 8 if i == 14 else i - 9
                        if before >= 0:
                            eng.wait_ge(veN.sem, veN.at("mul", before))
                        eng.activation(RB[:, 0:NS], PSF[:, SUM:SUM + NS], ACT.Sqrt, bias=eps).then_inc(*acR.did("s", i - 7))
                        eng.wait_ge(peN.sem, peN.at("p", i - 7))
                        eng.activation(RB[:, NS:N], PSF[:, SUM:SUM + NP_], ACT.Sqrt, bias=eps).then_inc(*acR.did("p", i - 7))
                    if i == 16:
                        silu(eng, 11)
                    eng.wait_ge(pe.sem, pe.at("used", i))
                    if kind == "z":
                        if g < 2:
                            eng.wait_ge(acS.sem, acS.end())
                        else:
                            eng.wait_ge(s_z[g % 2], 16)
                    if kind == "pool" and g:
                        eng.wait_ge(ve.sem, ve.at(f"pool{g - 1}.up"))
                    if 5 <= i < 16:
                        eng.wait_ge(ve.sem, ve.at(f"conv{i - 5}.2"))
                    for a, n, j in GROUPS:
                        src = PSF[:, 1536 * (i % 2) + a:1536 * (i % 2) + a + n]
                        if kind == "pool":
                            at = GAP + a + GAP * j
                            m = eng.activation(UPAD[:, at:at + n], src, ACT.Copy)
                        elif kind == "z":
                            m = eng.activation((PAD, CV)[g % 2][:, a:a + n], src, ACT.Silu)
                        else:
                            at = 1 + a + 2 * j
                            m = eng.activation(PAD[:, at:at + n], src, ACT.Copy)
                        m.then_inc(*ac.did("sp"[j], i))
                    ring.hi(eng, i + 2)
                    if 5 <= i < 16:
                        silu(eng, i - 5)
                    if 0 <= i - 6 < N_L2:
                        t, gg, _ = norm_tiles[i - 6]
                        if i > 6:
                            eng.wait_ge(peN.sem, peN.at("p", i - 7))
                        eng.activation(SQ, t[:, gg, :], ACT.Square).then_inc(*acN.did("sq", i - 6))
                    if i == 2:
                        eng.wait_ge(s_small, 64)
                        eng.activation(ABH[0], ABW, ACT.Copy).then_inc(*acB.did("hi"))

            @program("po")
            def _(eng):
                ended(eng, *prev)
                for i in range(n_t):
                    if i >= 2:
                        ring.lo(eng, i)
                    if i == 4:
                        eng.wait_ge(acB.sem, acB.end())
                        eng.tensor_tensor(ABL[0], ABW, ABH[1], ALU.subtract).then_inc(*poB.did("lo"))

            @program("ve")
            def _(eng):
                ended(eng, *prev)
                eng.memset(PAD, 0.0).then_inc(*veZ.did("pad"))
                eng.memset(UPAD, 0.0).then_inc(*veZ.did("upad"))
                for g, w in enumerate(WINDOWS):
                    eng.wait_ge(ac.sem, ac.at("p", g))
                    src = UPAD
                    for i in range(doubled[g]):
                        if i:
                            eng.wait_ge(ve.sem, ve.at(f"pool{g}.d{i - 1}"))
                        elif g:
                            eng.wait_ge(ve.sem, ve.at(f"pool{g - 1}.mp"))
                        dst, sh = (PA, PB)[i % 2], 1 << i
                        width = WU - (2 << i) + 1
                        eng.tensor_tensor(dst[:, 0:width], src[:, 0:width], src[:, sh:sh + width], ALU.add).then_inc(*ve.did(f"pool{g}.d{i}"))
                        src = dst
                    if g == 0:
                        eng.wait_ge(s_spill, 16)
                    eng.wait_ge(s_inv, 16 * (g + 1))
                    eng.wait_ge(ve.sem, ve.at(f"pool{g}.d{doubled[g] - 1}"))
                    for a, n, j in GROUPS:
                        at = GAP + a + GAP * j
                        eng.tensor_tensor(PO[:, g, a:a + n], src[:, at - w // 2:at - w // 2 + n], INV[:, a:a + n], ALU.mult)\
                            .then_inc(*ve.did(f"pool{g}.m{'sp'[j]}"))
                    eng.wait_ge(ve.sem, ve.at(f"pool{g}.mp"))
                    for a, n, j in GROUPS:
                        at = GAP + a + GAP * j
                        eng.tensor_tensor(PO[:, g, a:a + n], PO[:, g, a:a + n], UPAD[:, at:at + n], ALU.subtract)\
                            .then_inc(*ve.did(f"pool{g}.u{'sp'[j]}"))
                for i in range(12):
                    kind, g, _ = tiles[4 + i]
                    if 0 <= i - 3 < N_L2:
                        RB, (t, gg, scale) = RBS[i - 3], norm_tiles[i - 3]
                        eng.wait_ge(acR.sem, acR.at("p", i - 3))
                        eng.reciprocal(RB, RB).then_inc(*veN.did("inv", i - 3))
                        eng.wait_ge(veN.sem, veN.at("inv", i - 3))
                        eng.scalar_tensor_tensor(t[:, gg, :], RB, scale, t[:, gg, :], ALU.mult, ALU.mult).then_inc(*veN.did("mul", i - 3))
                    eng.wait_ge(ac.sem, ac.at("p", 4 + i))
                    if i:
                        eng.wait_ge(acS.sem, acS.at("p", i - 1))
                    for k in range(3):
                        wcol = vec("l0_dn_conv_w", 12 * k + pos[kind] + g)
                        src, dst = PAD[:, k:k + PADN - 2], CV[:, 1:PADN - 1]
                        if k:
                            eng.wait_ge(ve.sem, ve.at(f"conv{i}.{k - 1}"))
                            m = eng.scalar_tensor_tensor(dst, src, wcol, dst, ALU.mult, ALU.add)
                        else:
                            m = eng.tensor_scalar(dst, src, wcol, None, ALU.mult)
                        m.then_inc(*ve.did(f"conv{i}.{k}"))

            part1 = [pe, peAB, ac, acS, ve, ring.ac, ring.po, acB, poB, peN, veN, acN, acR]

            peP = steps("pe_pool", ["t"], 4)
            acP = steps("ac_pool", ["p", "hi"], 4)
            poP = steps("po_pool", ["lo"], 4)
            acG = steps("ac_gate", ["exp_a", "ln", "sig", "a"])
            veG = steps("ve_gate", ["copy", "dt", "abs", "g", "ga", "one", "beta"])
            a_cols = ABS.rearrange("p t (a b c) -> p t a b c", a=2, b=2)

            def pair(ap):
                return ap.rearrange("p t (a c) -> p t a c", a=2)

            @program("pe")
            def _(eng):
                ended(eng, *part1)
                for i in range(4):
                    if i >= 2:
                        eng.wait_ge(acP.sem, acP.at("p", i - 2))
                    for b, (a, n) in enumerate(CHUNKS):
                        m = eng.matmul(PS[:, 3 * (i % 2) + b, 0:n], POW[:, i, :], PO[:, i, a:a + n], start=True, stop=True)
                    m.then_inc(*peP.did("t", i))

            @program("ac")
            def _(eng):
                ended(eng, *part1)
                eng.wait_ge(veG.sem, veG.at("abs"))
                eng.activation(TA, TA, ACT.Exp, scale=-1.0).then_inc(*acG.did("exp_a"))
                eng.wait_ge(acG.sem, acG.at("exp_a"))
                eng.activation(TA, TA, ACT.Ln, bias=1.0).then_inc(*acG.did("ln"))
                eng.activation(pair(BT), a_cols[:, :, :, 1, :], ACT.Exp, scale=-1.0).then_inc(*acG.did("sig"))
                eng.activation(ALOG, ALOG, ACT.Exp).then_inc(*acG.did("a"))
                for g in range(4):
                    eng.wait_ge(peP.sem, peP.at("t", g))
                    eng.activation(PO[:, g, :], psum(3 * (g % 2), N), ACT.Identity, bias=0.0, scale=vec("l0_pool_scale", g)).then_inc(*acP.did("p", g))
                    eng.wait_ge(acP.sem, acP.at("p", g))
                    eng.activation(HH[:, 4 + g, :], PO[:, g, :], ACT.Copy).then_inc(*acP.did("hi", g))

            @program("ve")
            def _(eng):
                eng.wait_ge(peAB.sem, peAB.end())
                eng.tensor_copy(ABS.rearrange("p t c -> p (t c)"), PS[:, 6, 0:160]).then_inc(*veG.did("copy"))
                eng.wait_ge(veG.sem, veG.at("copy"))
                eng.tensor_tensor(pair(GG), a_cols[:, :, :, 0, :], pair(over(DTB, NT)), ALU.add).then_inc(*veG.did("dt"))
                eng.wait_ge(veG.sem, veG.at("dt"))
                eng.scalar_tensor_tensor(TA, GG, -1.0, GG, ALU.mult, ALU.max).then_inc(*veG.did("abs"))
                eng.wait_ge(acG.sem, acG.at("a"))
                eng.scalar_tensor_tensor(GG, GG, 0.0, TA, ALU.max, ALU.add).then_inc(*veG.did("g"))
                eng.wait_ge(veG.sem, veG.at("g"))
                eng.scalar_tensor_tensor(GG, GG, -1.0, over(ALOG, NT), ALU.mult, ALU.mult).then_inc(*veG.did("ga"))
                eng.tensor_scalar(BT, BT, 1.0, None, ALU.add).then_inc(*veG.did("one"))
                eng.wait_ge(veG.sem, veG.at("one"))
                eng.reciprocal(BT, BT).then_inc(*veG.did("beta"))

            @program("po")
            def _(eng):
                for g in range(4):
                    eng.wait_ge(acP.sem, acP.at("hi", g))
                    eng.tensor_tensor(HL[:, 4 + g, :], PO[:, g, :], HH32[:, 4 + g, :], ALU.subtract).then_inc(*poP.did("lo", g))

            part2 = [peP, acP, acG, veG, poP]

            places = [Region(HT_AT, HT_AT + HEADS * N), Region(HT_AT + KD * N, HT_AT + KD * N + HEADS * N), late]

            def buf(name):
                return next(reg for reg in places if reg.a + 512 <= reg.b).take(HEADS, P)
            B = [{nm: buf(nm) for nm in ("L", "M0", "M1", "X", "Y", "R", "QK", "QD", "KD", "VB", "VN", "S")} for _ in range(2)]
            C = [{nm: late.take(4) for nm in ("gc", "gl", "eg", "egl", "cd", "nb")} for _ in range(2)]
            IT = NT
            LV = range(1, LEVELS)
            pn = ["gb", "gc", "kk", "qk", "kt", "vt", "xt"]
            for v in LV:
                pn += [f"r{v}"] + ([f"q{v}"] if v < LEVELS - 1 else []) + [f"u{v}"]
            pn += ["ks", "vn", "o", "ds"]
            vn = ["gu", "gc", "ta", "tb", "tc", "gl", "l", "qk", "nb", "kd", "vb", "x"]
            for v in LV:
                vn += ([f"x{v}"] if v < LEVELS - 1 else []) + [f"y{v}"]
            vn += ["r1", "r2", "o", "s1", "s2"]
            pe_d = [steps(f"pe_dn{d}", pn, IT) for d in "fb"]
            ve_d = [steps(f"ve_dn{d}", vn, IT) for d in "fb"]
            ac_d = [steps(f"ac_dn{d}", ["eb", "ea", "cd", "eq", "eg", "egl", "y"] + [f"r{v}" for v in LV] + ["vn"], IT) for d in "fb"]
            po_d = [steps(f"po_dn{d}", ["lb", "lm0", "qd"] + [f"lm{v}" for v in LV], IT) for d in "fb"]
            s_state, s_new = sem("state_landed"), sem("state_stored")

            def chunk(it, d):
                first, count = (0, NS // P) if it < NS // P else (NS // P, NP_ // P)
                return it if d == 0 else first + count - 1 - (it - first)

            def cols(it, d):
                c = chunk(it, d)
                return slice(c * P, (c + 1) * P)

            def bank(d, b):
                return PS[:, 4 * d + b, :].rearrange("p (h t) -> p h t", t=P)
            LAST = (P - 1, 0)

            @program("sp")
            def _(eng):
                ended(eng, *part2)
                for i in range(2):
                    eng.wait_ge(s_z[i], 32)
                eng.dma_start(SQM, A["k_squares"][:, 2 * P:8 * P].rearrange("p (a b) -> p a b", b=P)).then_inc(s_mask, 16)
                eng.dma_start(LVM.rearrange("p a b c -> p (a b c)"), A["k_level"]).then_inc(s_mask, 16)
                for d, name in enumerate(("state_l0_fwd", "state_l0_bwd")):
                    eng.dma_start(B[d]["S"], A[name][0].rearrange("h k v -> k h v")).then_inc(s_state, 16)
                for d, name in enumerate(("new_f", "new_b")):
                    eng.wait_ge(ve_d[d].sem, ve_d[d].end())
                    eng.dma_start(OUT[name][0].rearrange("h k v -> k h v"), B[d]["S"]).then_inc(s_new, 16)
                eng.wait_ge(s_new, 32)

            STAGES = ["start", "decay", "rates", "exps", "scores", "mask", "inverse"] + [f"{k}{v}" for v in LV for k in "ru"] + ["state", "new", "out"]
            LAG = 3
            SCHEDULE = []
            for slot in range(IT * len(STAGES) + LAG):
                for d, at in ((0, slot), (1, slot - LAG)):
                    if 0 <= at < IT * len(STAGES):
                        SCHEDULE.append((STAGES[at % len(STAGES)], d, at // len(STAGES)))

            @program("pe")
            def _(eng):
                ended(eng, *part2)
                eng.wait_ge(s_mask, 32)
                eng.wait_ge(s_state, 32)

                def heads(d, b, f):
                    for hd in range(HEADS):
                        m = f(bank(d, b)[:, hd, :], hd)
                    return m
                for stage, d, it in SCHEDULE:
                    pe, ve, ac, po, bf, cs = pe_d[d], ve_d[d], ac_d[d], po_d[d], B[d], cols(it, d)
                    v = int(stage[1:]) if stage[1:].isdigit() else 0
                    if stage == "decay":
                        eng.wait_ge(ve.sem, ve.at("gu", it))
                        if it:
                            eng.wait_ge(ac.sem, ac.at("vn", it - 1))
                        eng.matmul(PS[:, 4 * d, :], ones, bf["R"].rearrange("p h t -> p (h t)"), start=True, stop=True).then_inc(*pe.did("gb", it))
                        eng.matmul(PS[:, 4 * d + 3, 0:4], SQM[:, d, :], GG[:, chunk(it, d), 4 * d:4 * d + 4], start=True, stop=True).then_inc(*pe.did("gc", it))
                        heads(d, 1, lambda o, hd: eng.matmul(o, KT[:, hd, cs], KT[:, hd, cs], start=True, stop=True)).then_inc(*pe.did("kk", it))
                        heads(d, 2, lambda o, hd: eng.matmul(o, KT[:, hd, cs], QT[:, hd, cs], start=True, stop=True)).then_inc(*pe.did("qk", it))
                    elif stage == "scores":
                        eng.wait_ge(ve.sem, ve.at("gc", it))
                        heads(d, 3, lambda o, hd: eng.transpose(o, KT[:, hd, cs], ident)).then_inc(*pe.did("kt", it))
                        eng.wait_ge(ve.sem, ve.at("gl", it))
                        eng.wait_ge(ac.sem, ac.at("eq", it))
                        heads(d, 0, lambda o, hd: eng.transpose(o, VT[:, hd, cs], ident)).then_inc(*pe.did("vt", it))
                    elif stage == "inverse":
                        eng.wait_ge(ve.sem, ve.at("x", it))
                        heads(d, 3, lambda o, hd: eng.transpose(o, bf["X"][:, hd, :], ident)).then_inc(*pe.did("xt", it))
                    elif v and stage[0] == "r":
                        if v == 1:
                            eng.wait_ge(ac.sem, ac.at("y", it))
                        else:
                            eng.wait_ge(ve.sem, ve.at(f"y{v - 1}", it))
                        eng.wait_ge(po.sem, po.at(f"lm{v}", it))
                        lm = bf[f"M{v % 2}"]
                        heads(d, 0, lambda o, hd: eng.matmul(o, lm[:, hd, :], bf["Y"][:, hd, :], start=True, stop=True)).then_inc(*pe.did(f"r{v}", it))
                    elif v:
                        eng.wait_ge(ac.sem, ac.at(f"r{v}", it))
                        if v < LEVELS - 1:
                            heads(d, 1, lambda o, hd: eng.matmul(o, bf["R"][:, hd, :], bf["X"][:, hd, :], start=True, stop=True)).then_inc(*pe.did(f"q{v}", it))
                        heads(d, 2, lambda o, hd: eng.matmul(o, bf["X"][:, hd, :], bf["R"][:, hd, :], start=True, stop=True)).then_inc(*pe.did(f"u{v}", it))
                    elif stage == "state":
                        if it:
                            eng.wait_ge(ve.sem, ve.at("s2", it - 1))
                        heads(d, 3, lambda o, hd: eng.matmul(o, KT[:, hd, cs], bf["S"][:, hd, :], start=True, stop=True)).then_inc(*pe.did("ks", it))
                    elif stage == "new":
                        eng.wait_ge(ve.sem, ve.at("r2", it))
                        heads(d, 0, lambda o, hd: eng.matmul(o, bf["Y"][:, hd, :], bf["R"][:, hd, :], start=True, stop=True)).then_inc(*pe.did("vn", it))
                    elif stage == "out":
                        eng.wait_ge(ac.sem, ac.at("vn", it))
                        eng.wait_ge(po.sem, po.at("qd", it))

                        def out(o, hd):
                            eng.matmul(o, bf["S"][:, hd, :], bf["QD"][:, hd, :], start=True, stop=False)
                            return eng.matmul(o, bf["VN"][:, hd, :], bf["QK"][:, hd, :], start=False, stop=True)
                        heads(d, 1, out).then_inc(*pe.did("o", it))
                        heads(d, 2, lambda o, hd: eng.matmul(o, bf["KD"][:, hd, :], bf["VN"][:, hd, :], start=True, stop=True)).then_inc(*pe.did("ds", it))

            @program("ve")
            def _(eng):
                ended(eng, *part2)
                eng.wait_ge(s_mask, 32)
                eng.wait_ge(s_state, 32)
                for stage, d, it in SCHEDULE:
                    pe, ve, ac, po, bf, cc, c = pe_d[d], ve_d[d], ac_d[d], po_d[d], B[d], C[d], chunk(it, d)
                    v = int(stage[1:]) if stage[1:].isdigit() else 0

                    def tt(step, out, a, b, op):
                        eng.tensor_tensor(out, a, b, op).then_inc(*ve.did(step, it))
                    if stage == "start":
                        tt("gu", bf["R"], over(SQM[:, d, :], HEADS), bcast(GG[:, c, 4 * d:4 * d + 4], P), ALU.mult)
                    elif stage == "rates":
                        eng.wait_ge(pe.sem, pe.at("gc", it))
                        eng.tensor_copy(cc["gc"], PS[:, 4 * d + 3, 0:4]).then_inc(*ve.did("gc", it))
                        eng.wait_ge(ve.sem, ve.at("gc", it))
                        tt("ta", bf["L"], bank(d, 0), bcast(cc["gc"], P), ALU.subtract)
                        eng.wait_ge(ve.sem, ve.at("ta", it))
                        tt("tb", bf["QK"], bf["L"], over(SQM[:, 3 + 2 * d, :], HEADS), ALU.add)
                        tt("tc", bf["L"], bf["L"], over(SQM[:, 2 + 2 * d, :], HEADS), ALU.add)
                        tt("gl", cc["gl"], bank(d, 0)[:, :, LAST[d]], cc["gc"], ALU.subtract)
                    elif stage == "scores":
                        eng.wait_ge(ac.sem, ac.at("ea", it))
                        eng.wait_ge(pe.sem, pe.at("qk", it))
                        tt("l", bf["L"], bf["L"], bank(d, 1), ALU.mult)
                        tt("qk", bf["QK"], bf["QK"], bank(d, 2), ALU.mult)
                    elif stage == "mask":
                        beta = BT[:, c, 4 * d:4 * d + 4]
                        eng.wait_ge(ac.sem, ac.at("egl", it))
                        eng.scalar_tensor_tensor(cc["nb"], cc["eg"], -1.0, beta, ALU.mult, ALU.mult).then_inc(*ve.did("nb", it))
                        eng.wait_ge(pe.sem, pe.at("kt", it))
                        tt("kd", bf["KD"], bank(d, 3), bcast(cc["egl"], P), ALU.mult)
                        eng.wait_ge(pe.sem, pe.at("vt", it))
                        tt("vb", bf["VB"], bank(d, 0), bcast(beta, P), ALU.mult)
                        eng.wait_ge(po.sem, po.at("lm0", it))
                        tt("x", bf["X"], over(ident, HEADS), bf["M0"], ALU.subtract)
                    elif v and stage[0] == "u":
                        eng.wait_ge(pe.sem, pe.at(f"u{v}", it))
                        if v == 1:
                            eng.wait_ge(ve.sem, ve.at("x", it))
                            eng.wait_ge(ac.sem, ac.at("y", it))
                        else:
                            eng.wait_ge(ve.sem, ve.at(f"y{v - 1}", it))
                        if v < LEVELS - 1:
                            tt(f"x{v}", bf["X"], bf["X"], bank(d, 1), ALU.subtract)
                        tt(f"y{v}", bf["Y"], bf["Y"], bank(d, 2), ALU.subtract)
                    elif stage == "state":
                        eng.wait_ge(pe.sem, pe.at("ks", it))
                        tt("r1", bf["R"], bank(d, 3), bcast(cc["nb"], P), ALU.mult)
                        eng.wait_ge(ve.sem, ve.at("r1", it))
                        tt("r2", bf["R"], bf["R"], bf["VB"], ALU.add)
                    elif stage == "out":
                        eng.wait_ge(pe.sem, pe.at("ds", it))
                        o = OT[:, :, cols(it, d)]
                        twin = [j for j in range(IT) if chunk(j, 1 - d) == c][0]
                        if twin < it:
                            eng.wait_ge(ve_d[1 - d].sem, ve_d[1 - d].at("o", twin))
                            tt("o", o, o, bank(d, 1), ALU.add)
                        else:
                            eng.tensor_copy(o, bank(d, 1)).then_inc(*ve.did("o", it))
                        if it == NS // P - 1:
                            eng.memset(bf["S"], 0.0).then_inc(*ve.did("s1", it))
                            eng.wait_ge(ve.sem, ve.at("s1", it))
                            eng.memset(bf["S"], 0.0).then_inc(*ve.did("s2", it))
                        else:
                            if it:
                                eng.wait_ge(ve.sem, ve.at("s2", it - 1))
                            tt("s1", bf["S"], bf["S"], bcast(cc["cd"], P), ALU.mult)
                            eng.wait_ge(ve.sem, ve.at("s1", it))
                            tt("s2", bf["S"], bf["S"], bank(d, 2), ALU.add)

            @program("ac")
            def _(eng):
                ended(eng, *part2)
                eng.wait_ge(s_mask, 32)
                for stage, d, it in SCHEDULE:
                    pe, ve, ac, bf, cc = pe_d[d], ve_d[d], ac_d[d], B[d], C[d]
                    v = int(stage[1:]) if stage[1:].isdigit() else 0
                    if stage == "exps":
                        eng.wait_ge(ve.sem, ve.at("gl", it))
                        eng.activation(bf["QK"], bf["QK"], ACT.Exp).then_inc(*ac.did("eb", it))
                        eng.activation(bf["L"], bf["L"], ACT.Exp, scale=-1.0).then_inc(*ac.did("ea", it))
                        eng.activation(cc["cd"], bank(d, 0)[:, :, LAST[d]], ACT.Exp).then_inc(*ac.did("cd", it))
                        eng.activation(bf["QD"], bank(d, 0), ACT.Exp).then_inc(*ac.did("eq", it))
                        eng.activation(cc["eg"], cc["gc"], ACT.Exp).then_inc(*ac.did("eg", it))
                        eng.activation(cc["egl"], cc["gl"], ACT.Exp).then_inc(*ac.did("egl", it))
                    elif stage == "inverse":
                        eng.wait_ge(pe.sem, pe.at("xt", it))
                        eng.activation(bf["Y"], bank(d, 3), ACT.Copy).then_inc(*ac.did("y", it))
                    elif v and stage[0] == "r":
                        eng.wait_ge(pe.sem, pe.at(f"r{v}", it))
                        eng.activation(bf["R"], bank(d, 0), ACT.Copy).then_inc(*ac.did(f"r{v}", it))
                    elif stage == "new":
                        eng.wait_ge(pe.sem, pe.at("vn", it))
                        eng.activation(bf["VN"], bank(d, 0), ACT.Copy).then_inc(*ac.did("vn", it))

            @program("po")
            def _(eng):
                eng.wait_ge(s_mask, 32)
                for stage, d, it in SCHEDULE:
                    pe, ve, ac, po, bf, c = pe_d[d], ve_d[d], ac_d[d], po_d[d], B[d], chunk(it, d)
                    v = int(stage[1:]) if stage[1:].isdigit() else 0
                    if stage == "scores":
                        eng.wait_ge(ve.sem, ve.at("l", it))
                        eng.tensor_tensor(bf["L"], bf["L"], bcast(BT[:, c, 4 * d:4 * d + 4], P), ALU.mult).then_inc(*po.did("lb", it))
                        eng.wait_ge(po.sem, po.at("lb", it))
                        eng.tensor_tensor(bf["M0"], bf["L"], over(LVM[:, d, 0, :], HEADS), ALU.mult).then_inc(*po.did("lm0", it))
                    elif stage == "inverse":
                        eng.wait_ge(ac.sem, ac.at("eq", it))
                        eng.tensor_tensor(bf["QD"], bf["QD"], QT[:, :, cols(it, d)], ALU.mult).then_inc(*po.did("qd", it))
                    elif v and stage[0] == "r":
                        if v == 2:
                            eng.wait_ge(ve.sem, ve.at("x", it))
                        if v > 2:
                            eng.wait_ge(pe.sem, pe.at(f"r{v - 2}", it))
                        eng.tensor_tensor(bf[f"M{v % 2}"], bf["L"], over(LVM[:, d, v, :], HEADS), ALU.mult).then_inc(*po.did(f"lm{v}", it))

            part3 = pe_d + ve_d + ac_d + po_d

            h = Region(W_AT, W_AT + HEADS * N)
            SQ2 = [h.take(N) for _ in range(2)]
            w = Region(W_AT + 2 * HEADS * N + 6144, ARENA)
            ROOTS, SELECT, COLUMN = w.take(N), w.take(HEADS, P), w.take(2 * HEADS)
            ZT = VT
            s_zb = sem("z_back")
            peH = steps("pe_head", ["t"], HEADS)
            peHb = steps("pe_head_over", ["b"], HEADS)
            acH = steps("ac_head", ["sq"], HEADS)
            acHr = steps("ac_head_root", ["root"])
            acHi = steps("ac_headhi", ["hi"], HEADS)
            veH = steps("ve_head", ["zero", "one", "select"] + [f"gate{i}" for i in range(HEADS)] + ["inv"] + [f"mul{i}" for i in range(HEADS)])
            poH = steps("po_head", ["lo"], HEADS)

            @program("sp")
            def _(eng):
                ended(eng, *part3)
                eng.dma_start(ZT, z_dram.rearrange("h p n -> p h n")).then_inc(s_zb, 16)

            @program("pe")
            def _(eng):
                eng.wait_ge(veH.sem, veH.at("one"))
                for i in range(HEADS):
                    eng.wait_ge(acH.sem, acH.at("sq", i))
                    if i == 0:
                        ended(eng, *part3)
                    for b, (a, n) in enumerate(CHUNKS):
                        m = eng.matmul(PS[0:HEADS, b, 0:n], COLUMN[:, HEADS - 1 - i:2 * HEADS - 1 - i], SQ2[i % 2][:, a:a + n], start=i == 0, stop=i == HEADS - 1)
                    m.then_inc(*peH.did("t", i))
                eng.wait_ge(veH.sem, veH.at("inv"))
                for i in range(HEADS):
                    if i:
                        eng.wait_ge(*((veH.sem, veH.at(f"mul{i - 2}")) if i >= 2 else (acHr.sem, acHr.end())))
                    for b, (a, n) in enumerate(CHUNKS):
                        m = eng.matmul(PS[:, 3 * ((i + 1) % 2) + b, 0:n], SELECT[0:HEADS, i, :], ROOTS[0:HEADS, a:a + n], start=True, stop=True)
                    m.then_inc(*peHb.did("b", i))

            @program("ac")
            def _(eng):
                ended(eng, *part3)
                eng.wait_ge(s_new, 32)
                for i in range(HEADS):
                    if i >= 2:
                        eng.wait_ge(peH.sem, peH.at("t", i - 2))
                    eng.activation(SQ2[i % 2], OT[:, i, :], ACT.Square).then_inc(*acH.did("sq", i))
                eng.wait_ge(peH.sem, peH.end())
                eng.activation(ROOTS[0:HEADS, :], PSF[0:HEADS, 0:N], ACT.Sqrt, bias=eps[0:HEADS, :], scale=1.0 / P).then_inc(*acHr.did("root"))
                for i in range(HEADS):
                    eng.wait_ge(veH.sem, veH.at(f"mul{i}"))
                    eng.activation(HH[:, i, :], OT[:, i, :], ACT.Copy).then_inc(*acHi.did("hi", i))

            @program("ve")
            def _(eng):
                ended(eng, *part3)
                eng.wait_ge(s_new, 32)
                eng.memset(COLUMN, 0.0).then_inc(*veH.did("zero"))
                eng.wait_ge(veH.sem, veH.at("zero"))
                eng.memset(COLUMN[:, HEADS - 1:HEADS], 1.0).then_inc(*veH.did("one"))
                eng.tensor_copy(SELECT[0:HEADS], bcast(ident[0:HEADS, 0:HEADS], P)).then_inc(*veH.did("select"))
                eng.wait_ge(s_zb, 16)
                for i in range(HEADS):
                    eng.wait_ge(acH.sem, acH.at("sq", i))
                    eng.scalar_tensor_tensor(OT[:, i, :], OT[:, i, :], vec("l0_dn_norm_w"), ZT[:, i, :], ALU.mult, ALU.mult).then_inc(*veH.did(f"gate{i}"))
                eng.wait_ge(acHr.sem, acHr.end())
                eng.reciprocal(ROOTS[0:HEADS, :], ROOTS[0:HEADS, :]).then_inc(*veH.did("inv"))
                for i in range(HEADS):
                    eng.wait_ge(peHb.sem, peHb.at("b", i))
                    eng.tensor_tensor(OT[:, i, :], OT[:, i, :], psum(3 * ((i + 1) % 2), N), ALU.mult).then_inc(*veH.did(f"mul{i}"))

            @program("po")
            def _(eng):
                for i in range(HEADS):
                    eng.wait_ge(acHi.sem, acHi.at("hi", i))
                    eng.tensor_tensor(HL[:, i, :], OT[:, i, :], HH32[:, i, :], ALU.subtract).then_inc(*poH.did("lo", i))

            part4 = [peH, peHb, acH, acHr, acHi, veH, poH]

            @program("sp")
            def _(eng):
                eng.dma_start(XT[:, HEADS:KD], spill[:, HEADS:KD]).then_inc(s_spill, 16)
                ended(eng, *part4)
                eng.dma_start(XT[:, 0:HEADS], spill[:, 0:HEADS]).then_inc(s_spill, 16)
            x_ready, part5 = project(A["l0_w_out"], part3, part4, 0, (s_spill, 48))
            return x_ready, part4 + part5

        def project(weight, w_free, prev, layer, x_back):
            ring = weight_ring(Region(W_AT + 8 * N, ARENA), KD)
            ve = steps("ve_proj", ["s", "p"], KD)
            wv = weight.rearrange("(k p) n -> p k n", p=P)

            @program("sp")
            def _(eng):
                ended(eng, *w_free)
                for i in range(KD):
                    ring.load(eng, i, wv[:, :, i * P:(i + 1) * P], (KD, P))

            @program("pe")
            def _(eng):
                ended(eng, *prev)
                for i in range(KD):
                    ring.ready(eng, i)
                    if i >= 2:
                        eng.wait_ge(ve.sem, ve.at("p", i - 2))
                    wh, wl = ring.get(i, (KD, P))
                    for k in range(KD):
                        m = product(eng, 3 * (i % 2), (wh[:, k, :], wl[:, k, :]), (HH[:, k], HL[:, k]), k == 0, k == KD - 1)
                    m.then_inc(*ring.pe.did("used", i))

            @program("ac")
            def _(eng):
                ended(eng, *w_free)
                for i in range(KD):
                    ring.hi(eng, i)

            @program("po")
            def _(eng):
                for i in range(KD):
                    ring.lo(eng, i)

            @program("ve")
            def _(eng):
                ended(eng, *prev)
                eng.wait_ge(*x_back)
                for i in range(KD):
                    eng.wait_ge(ring.pe.sem, ring.pe.at("used", i))
                    for a, n, j in GROUPS:
                        at = 1536 * (i % 2) + a
                        eng.scalar_tensor_tensor(XT[:, i, a:a + n], PSF[:, at:at + n], MOD[:, layer, 16 + i, j:j + 1],
                                                 XT[:, i, a:a + n], ALU.mult, ALU.add).then_inc(*ve.did("sp"[j], i))
            def x_ready(eng, k):
                eng.wait_ge(ve.sem, ve.at("p", k))
            return x_ready, [ring.pe, ring.ac, ring.po, ve]

        GROUPS_OF = [list(range(3 * g, 3 * g + 3)) for g in range(6)] + [[18, 19, 20, 21]]
        SLOTS = 4

        def conv_glu(layer, before_norm, prev, h_ready, early):
            r = Region(W_AT, ARENA)
            HIDS = [(r.half(N), r.half(N)) for _ in range(SLOTS)]
            ring_at = r
            CV = [r.take(N) for _ in range(2)]
            GRID = (ROWS + 2) * (GRID_W + 2)
            PAD = r.take(GRID + NP_ + 2)
            items = []
            for j in range(KH):
                items += [("a", j, 0), ("g", j, 0)]
                for g, tiles in enumerate(GROUPS_OF):
                    if (j == tiles[-1] + 1) or (j == KH - 1 and tiles[-1] == j):
                        items += [("d", g, m) for m in range(4)]
            at = {it: i for i, it in enumerate(items)}
            ring = weight_ring(r, len(items))
            early.update(ac=lambda eng: [ring.hi(eng, i, size(i)) for i in range(2)], po=lambda eng: [ring.lo(eng, i, size(i)) for i in range(2)])
            pe = ring.pe
            taps = [f"grid{i}" for i in range(9)] + [f"line{i}" for i in range(3)]
            ac = steps("ac_ffn", ["grid", "line", "gelu", "hi"], KH)
            veZ = steps("ve_zeroffn", ["pad"])
            ve = steps("ve_ffn", taps + ["hid"], KH)
            veD = steps("ve_resffn", ["s0", "p0", "s1", "p1"], 4 * len(GROUPS_OF))
            po = steps("po_ffn", ["lo"], KH)
            peD = steps("pe_down", ["half"], 4 * len(GROUPS_OF))
            upv = A[f"l{layer}_ffn_up"].rearrange("(k p) n -> p k n", p=P)
            down = A[f"l{layer}_ffn_down"]
            w_name, b_name = f"l{layer}_ffn_conv_w", f"l{layer}_ffn_conv_b"

            def shape(item):
                return (len(GROUPS_OF[item[1]]), 2 * P) if item[0] == "d" else (KD, P)

            def size(i):
                return math.prod(shape(items[i])) if i < len(items) else 0

            @program("sp")
            def _(eng):
                ended(eng, *before_norm)
                for i, (kind, j, m) in enumerate(items):
                    if kind == "d":
                        a, b = GROUPS_OF[j][0] * P, (GROUPS_OF[j][-1] + 1) * P
                        src = down[a:b, m * 2 * P:(m + 1) * 2 * P].rearrange("(k p) n -> p k n", p=P)
                    else:
                        c = (HIDDEN if kind == "g" else 0) + j * P
                        src = upv[:, :, c:c + P]
                    ring.load(eng, i, src, shape(items[i]))

            @program("pe")
            def _(eng):
                for i, (kind, j, mp) in enumerate(items):
                    ring.ready(eng, i)
                    w = ring.get(i, shape(items[i]))
                    if kind == "a" and j:
                        eng.wait_ge(ac.sem, ac.at("line", j - 1))
                    if kind == "g" and j:
                        eng.wait_ge(ve.sem, ve.at("hid", j - 1))
                    if kind in "ag" and j > GROUPS_OF[0][-1] + 1:
                        q = max(q for q in range(i) if items[q][0] == "d")
                        rnd = 4 * items[q][1] + items[q][2]
                        eng.wait_ge(veD.sem, veD.at("p0" if kind == "a" else "p1", rnd))
                    if kind in "ag":
                        for k in range(KD):
                            if i == 0:
                                h_ready(eng, k)
                            m = product(eng, 0 if kind == "a" else 3, (w[0][:, k, :], w[1][:, k, :]), (HH[:, k], HL[:, k]), k == 0, k == KD - 1)
                        m.then_inc(*pe.did("used", i))
                        continue
                    tiles = GROUPS_OF[j]
                    if mp == 0:
                        eng.wait_ge(po.sem, po.at("lo", tiles[-1]))
                    before = [q for q in range(i) if items[q][0] in "ag"][-1]
                    rnd = 4 * j + mp
                    for half in range(2):
                        if mp == 0:
                            eng.wait_ge(*((ac.sem, ac.at("line", items[before][1])) if half == 0 else (ve.sem, ve.at("hid", items[before][1]))))
                        else:
                            eng.wait_ge(veD.sem, veD.at(f"p{half}", rnd - 1))
                        for n, tl in enumerate(tiles):
                            (hh, _), (hl, _) = HIDS[tl % SLOTS]
                            cs = slice(half * P, (half + 1) * P)
                            m = product(eng, 3 * half, (w[0][:, n, cs], w[1][:, n, cs]), (hh, hl), n == 0, n == len(tiles) - 1)
                        if half == 0:
                            m.then_inc(*peD.did("half", rnd))
                    m.then_inc(*pe.did("used", i))

            @program("ac")
            def _(eng):
                ended(eng, *prev)
                eng.wait_ge(veZ.sem, veZ.end())
                for i, (kind, j, m) in enumerate(items):
                    if kind == "a":
                        eng.wait_ge(pe.sem, pe.at("used", i))
                        if j:
                            eng.wait_ge(ve.sem, ve.at("line2", j - 1))
                        inner = PAD[:, 0:GRID].rearrange("p (r c) -> p r c", c=GRID_W + 2)[:, 1:ROWS + 1, 1:GRID_W + 1]
                        eng.activation(inner, psum(0, NS).rearrange("p (r c) -> p r c", c=GRID_W), ACT.Copy).then_inc(*ac.did("grid", j))
                        eng.activation(PAD[:, GRID + 1:GRID + 1 + NP_], PSF[:, NS:N], ACT.Copy).then_inc(*ac.did("line", j))
                        ring.hi(eng, i + 2, size(i + 2))
                        eng.wait_ge(ve.sem, ve.at("line2", j))
                        eng.activation(CV[j % 2], CV[j % 2], ACT.Gelu_apprx_tanh).then_inc(*ac.did("gelu", j))
                    elif kind == "g":
                        ring.hi(eng, i + 2, size(i + 2))
                        eng.wait_ge(ve.sem, ve.at("hid", j))
                        eng.activation(HIDS[j % SLOTS][0][0], CV[j % 2], ACT.Copy).then_inc(*ac.did("hi", j))
                    else:
                        ring.hi(eng, i + 2, size(i + 2))

            @program("po")
            def _(eng):
                ended(eng, *prev)
                for i, (kind, j, m) in enumerate(items):
                    ring.lo(eng, i + 2, size(i + 2))
                    if kind == "g":
                        eng.wait_ge(ac.sem, ac.at("hi", j))
                        (_, hh), (hl, _) = HIDS[j % SLOTS]
                        eng.tensor_tensor(hl, CV[j % 2], hh, ALU.subtract).then_inc(*po.did("lo", j))

            @program("ve")
            def _(eng):
                ended(eng, *prev)
                eng.memset(PAD, 0.0).then_inc(*veZ.did("pad"))
                for i, (kind, j, mp) in enumerate(items):
                    if kind == "a":
                        grid = PAD[:, 0:GRID].rearrange("p (r c) -> p r c", c=GRID_W + 2)
                        acc = CV[j % 2][:, 0:NS].rearrange("p (r c) -> p r c", c=GRID_W)
                        if j >= 2:
                            eng.wait_ge(po.sem, po.at("lo", j - 2))
                        eng.wait_ge(ac.sem, ac.at("line", j))
                        for k in range(9):
                            w = vec(w_name, k * KH + j)
                            src = grid[:, k // 3:k // 3 + ROWS, k % 3:k % 3 + GRID_W]
                            if k == 0:
                                eng.tensor_scalar(acc, src, w, vec(b_name, j), ALU.mult, ALU.add).then_inc(*ve.did("grid0", j))
                            else:
                                eng.wait_ge(ve.sem, ve.at(f"grid{k - 1}", j))
                                eng.scalar_tensor_tensor(acc, src, w, acc, ALU.mult, ALU.add).then_inc(*ve.did(f"grid{k}", j))
                        for k in range(3):
                            w = vec(w_name, (3 + k) * KH + j)
                            src, dst = PAD[:, GRID + k:GRID + k + NP_], CV[j % 2][:, NS:N]
                            if k == 0:
                                eng.tensor_scalar(dst, src, w, vec(b_name, j), ALU.mult, ALU.add).then_inc(*ve.did("line0", j))
                            else:
                                eng.wait_ge(ve.sem, ve.at(f"line{k - 1}", j))
                                eng.scalar_tensor_tensor(dst, src, w, dst, ALU.mult, ALU.add).then_inc(*ve.did(f"line{k}", j))
                    elif kind == "g":
                        eng.wait_ge(ac.sem, ac.at("gelu", j))
                        eng.wait_ge(pe.sem, pe.at("used", i))
                        eng.tensor_tensor(CV[j % 2], CV[j % 2], psum(3, N), ALU.mult).then_inc(*ve.did("hid", j))
                    else:
                        rnd = 4 * j + mp
                        for half in range(2):
                            eng.wait_ge(*((pe.sem, pe.at("used", i)) if half else (peD.sem, peD.at("half", rnd))))
                            mm = 2 * mp + half
                            for a, n, c in GROUPS:
                                at_ = 1536 * half + a
                                eng.scalar_tensor_tensor(XT[:, mm, a:a + n], PSF[:, at_:at_ + n], MOD[:, layer, 40 + mm, c:c + 1],
                                                         XT[:, mm, a:a + n], ALU.mult, ALU.add).then_inc(*veD.did("sp"[c] + str(half), rnd))
            def x_ready(eng, k):
                eng.wait_ge(veD.sem, veD.at(f"p{k % 2}", 4 * (len(GROUPS_OF) - 1) + k // 2))
            return x_ready, [peD, ring.pe, ring.ac, ring.po, ac, veZ, ve, veD, po]

        def ffn_layer(layer, x_ready, prev):
            before, early = prev, {}
            prev, h_ready = norm(prev, x_ready, W_FREE, 2 * layer + 1, mod(layer, 3), early)
            return conv_glu(layer, before, prev, h_ready, early)


        T_OF = {"s": NS // P, "p": NP_ // P}
        FIRST = {"s": 0, "p": NS // P}
        LEAVES = {"s": range(8), "p": range(2)}
        JOBS = [(c, order) for c in range(NCH) for order in range(2)]
        MAGIC = 1.5 * 2.0 ** 23
        TWO_PI_HI = 6.28125
        TWO_PI_LO = 2 * math.pi - TWO_PI_HI

        def row(ap, a, n):
            return ap[:, a:a + n, :].rearrange("p a c -> p (a c)")

        def pair(ap, a, b, n=1):
            step = b - a
            v = ap[:, a:a + 2 * step, :].rearrange("p (u v) c -> p u v c", v=step)[:, :, 0:n, :]
            return v.rearrange("p u v c -> p u (v c)")

        def chain(eng, st, tag, rnd):
            n = [0]

            def run(f, *args):
                if n[0]:
                    eng.wait_ge(st.sem, st.at(f"{tag}{n[0] - 1}", rnd))
                f(*args).then_inc(*st.did(f"{tag}{n[0]}", rnd))
                n[0] += 1
            return run

        def butterfly(eng, run, K, x0, x1r, x1i, m, th, plus, minus):
            c, s = math.cos(th), math.sin(th)
            run(eng.scalar_tensor_tensor, row(K, 8, m), x1r, c / s, x1i, ALU.mult, ALU.subtract)
            run(eng.scalar_tensor_tensor, row(K, 8 + m, m), x1i, c / s, x1r, ALU.mult, ALU.add)
            turned = row(K, 8, 2 * m).rearrange("p (u c) -> p u c", u=2)
            run(eng.scalar_tensor_tensor, plus.rearrange("p (u c) -> p u c", u=2), turned, s, x0, ALU.mult, ALU.add)
            run(eng.scalar_tensor_tensor, minus.rearrange("p (u c) -> p u c", u=2), turned, -s, x0, ALU.mult, ALU.add)

        N_TREE = 20

        def tree(eng, st, tag, rnd, R, r0, Q, q0, K, T):
            run = chain(eng, st, tag, rnd)
            run(eng.tensor_tensor, row(K, 0, 4), row(R, r0, 4), row(R, r0 + 4, 4), ALU.add)
            run(eng.tensor_tensor, row(K, 4, 4), row(R, r0, 4), row(R, r0 + 4, 4), ALU.subtract)
            run(eng.tensor_tensor, row(T, 0, 2), row(K, 0, 2), row(K, 2, 2), ALU.add)
            run(eng.tensor_tensor, row(T, 2, 2), row(K, 0, 2), row(K, 2, 2), ALU.subtract)
            butterfly(eng, run, K, pair(K, 4, 6), row(K, 5, 1), row(K, 7, 1), 1, math.pi / 4, row(T, 4, 2), row(T, 6, 2))
            butterfly(eng, run, K, pair(Q, q0, q0 + 4, 2), row(Q, q0 + 2, 2), row(Q, q0 + 6, 2), 2, math.pi / 4, row(K, 0, 4), row(K, 4, 4))
            butterfly(eng, run, K, pair(K, 0, 2), row(K, 1, 1), row(K, 3, 1), 1, math.pi / 8, row(T, 8, 2), row(T, 10, 2))
            butterfly(eng, run, K, pair(K, 4, 6), row(K, 5, 1), row(K, 7, 1), 1, 5 * math.pi / 8, row(T, 12, 2), row(T, 14, 2))

        def unfold(eng, run, K, a, b, m, th, out, dst):
            c, s = math.cos(th), math.sin(th)
            run(eng.tensor_tensor, pair(out, dst, dst + 2 * m, m), a.rearrange("p (u c) -> p u c", u=2), b.rearrange("p (u c) -> p u c", u=2), ALU.add)
            run(eng.tensor_tensor, row(K, 8, 2 * m), a, b, ALU.subtract)
            yr, yi = row(K, 8, m), row(K, 8 + m, m)
            ur, ui = row(K, 8 + 2 * m, m), row(K, 8 + 3 * m, m)
            run(eng.scalar_tensor_tensor, ur, yr, c / s, yi, ALU.mult, ALU.add)
            run(eng.scalar_tensor_tensor, ui, yi, c / s, yr, ALU.mult, ALU.subtract)
            x1 = out[:, dst:dst + 4 * m, :].rearrange("p (u v) c -> p u v c", u=2)[:, :, m:2 * m, :].rearrange("p u v c -> p u (v c)")
            run(eng.tensor_scalar, x1, row(K, 8 + 2 * m, 2 * m).rearrange("p (u c) -> p u c", u=2), s, None, ALU.mult)

        N_INV = 25

        def untree(eng, st, tag, rnd, K, T):
            run = chain(eng, st, tag, rnd)
            unfold(eng, run, K, row(T, 8, 2), row(T, 10, 2), 1, math.pi / 8, K, 0)
            unfold(eng, run, K, row(T, 12, 2), row(T, 14, 2), 1, 5 * math.pi / 8, K, 4)
            unfold(eng, run, K, row(K, 0, 4), row(K, 4, 4), 2, math.pi / 4, T, 8)
            unfold(eng, run, K, row(T, 4, 2), row(T, 6, 2), 1, math.pi / 4, K, 4)
            run(eng.tensor_tensor, row(K, 0, 2), row(T, 0, 2), row(T, 2, 2), ALU.add)
            run(eng.tensor_tensor, row(K, 2, 2), row(T, 0, 2), row(T, 2, 2), ALU.subtract)
            run(eng.tensor_tensor, row(T, 0, 4), row(K, 0, 4), row(K, 4, 4), ALU.add)
            run(eng.tensor_tensor, row(T, 4, 4), row(K, 0, 4), row(K, 4, 4), ALU.subtract)
            run(eng.tensor_tensor, row(T, 0, 8), row(T, 0, 8), row(T, 8, 8), ALU.add)

        def matrices(table, leaf, inverse):
            if leaf == 0:
                return [[table[:, 0, :], table[:, 1, :]], [table[:, 2, :], table[:, 3, :]]]
            b = 4 + 3 * (leaf - 1)
            cos, sin, neg = table[:, b, :], table[:, b + 1, :], table[:, b + 2, :]
            return [[cos, neg], [sin, cos]] if inverse else [[cos, sin], [neg, cos]]

        def transform(eng, bank, M, rhs):
            for o in range(2):
                for i in range(2):
                    m = eng.matmul(PS[:, bank, o * HC:(o + 1) * HC], M[i][o], rhs[i], start=i == 0, stop=i == 1)
            return m

        def mixer_hyena(before_norm, prev, h_ready, early):
            x_r, r = Region(XT_AT, HT_AT), Region(W_AT, ARENA)
            FW = r.take(25, P)
            mid = Region(r.a, r.b)
            KF, TF, W4 = x_r.take(17, HC), x_r.take(16, HC), x_r.take(4, HC)
            KP, TP = r.take(5, HC), r.take(4, HC)
            SP_ = r.take(4, P)
            PADN = N + 4
            PAD, CV = r.take(PADN), [r.take(PADN) for _ in range(2)]
            STG = r.take(NT, P)
            NPOS = 2 * N
            HD = r.take(NPOS)
            DELTA, BIAS = r.take(HC), r.take(2, HC)
            WIN = {"s": r.take(2, 16), "p": r.take(2, 4)}
            m_r = Region(XT_AT, HT_AT)
            FEAT, ARG, TMP, RED, MLPW = m_r.take(NPOS), m_r.take(512), m_r.take(512), m_r.take(512), m_r.take(3, FFN64)
            n_t = 6 * NCH
            ring = weight_ring(r, n_t)
            early.update(ac=lambda eng: [ring.hi(eng, i) for i in range(2)], po=lambda eng: [ring.lo(eng, i) for i in range(2)])
            tok_dram = nc.dram_tensor("hyena_tokens", (3, NCH, P, NT, HC), F32, kind="Internal").ap()
            filt_dram = {"s": nc.dram_tensor("filters_s", (len(JOBS), P, 17, HC), F32, kind="Internal").ap(),
                         "p": nc.dram_tensor("filters_p", (len(JOBS), P, 5, HC), F32, kind="Internal").ap()}
            s_x, s_mlp, s_k, s_c = sem("x_spilled"), sem("mlp_landed"), sem("hyena_tables_landed"), sem("hyena_chunk_landed")
            s_tok = sem("tokens_stored")
            s_flt = {g: sem("filter_stored_" + g) for g in "sp"}
            KB, TB = {"s": KF, "p": KP}, {"s": TF, "p": TP}

            peT = steps("pe_tokens", ["t"], n_t)
            acW = steps("ac_in1", ["s", "p"], n_t)
            acT = steps("ac_tokens", ["e"], n_t)
            veZ = steps("ve_zero1", ["pad"])
            veW = steps("ve_in1", ["c0", "c1", "c2"], n_t)
            peM = steps("pe_mlp", ["t"], 15)
            veM_ = steps("ve_mlp", ["arg", "turns", "whole", "hi", "lo", "clamp"], 15)
            acM = steps("ac_mlp", ["sin"], 15)
            peF, acF, veF = {}, {}, {}
            for g in "sp":
                T = T_OF[g]
                peF[g] = steps("pe_filter_" + g, [f"tap{b}" for b in range(T)] + [f"h{l}" for l in LEAVES[g]] + ["hx"], len(JOBS))
                acF[g] = steps("ac_filter_" + g, [f"win{b}" for b in range(T)] + [f"h{l}" for l in LEAVES[g]] + ["hx"], len(JOBS))
                veF[g] = steps("ve_filter_" + g, [f"k{b}" for b in range(T)] + ["bias", "r", "q"] + ([f"ft{i}" for i in range(N_TREE)] if g == "s" else []), len(JOBS))
            leaves_made = {"s": f"ft{N_TREE - 1}", "p": "q"}

            EXTRA = {0: ("mlp", 0), 2: ("mlp", 1), 4: ("mlp", 2)}
            for f in range(len(JOBS)):
                EXTRA[6 + 2 * f], EXTRA[7 + 2 * f] = ("tap", f), ("leaf", f)

            small = []
            for n in sorted(EXTRA):
                kind, f = EXTRA[n]
                if kind == "mlp":
                    small += [(veM_, "arg", 5 * f + i) for i in range(5)]
                for g in "sp" if kind != "mlp" else "":
                    if kind == "tap":
                        small += [(veF[g], f"k{b}", f) for b in range(T_OF[g])]
                    else:
                        small += [(acF[g], f"h{l}", f) for l in LEAVES[g]] + [(acF[g], "hx", f)]
            place = {(id(st), step, rnd): q for q, (st, step, rnd) in enumerate(small)}

            def small_bank(st, step, rnd):
                return 6 + place[(id(st), step, rnd)] % 2

            def wait_bank(eng, st, step, rnd):
                q = place[(id(st), step, rnd)]
                if q >= 2:
                    who, what, when = small[q - 2]
                    eng.wait_ge(who.sem, who.at(what, when))

            w_in = A["l1_w_in"].rearrange("(k p) n -> p k n", p=P)

            def tile_of(n):
                c, i = divmod(n, 6)
                kind, half = divmod(i, 2)
                return c, kind, half, 8 * kind + 2 * c + half

            def slots():
                for n in range(n_t + 1):
                    yield n, EXTRA.get(n, (None, None))

            @program("sp")
            def _(eng):
                ended(eng, *before_norm)
                eng.dma_start(spill, XT).then_inc(s_x, 16)
                for n in range(2):
                    ring.load(eng, n, w_in[:, :, tile_of(n)[3] * P:(tile_of(n)[3] + 1) * P], (KD, P))
                ended(eng, *prev)
                eng.wait_ge(s_x, 16)
                for dst, name in ((FEAT[0:EMB, 0:2 * NS], "k_feat_s"), (FEAT[0:EMB, 2 * NS:NPOS], "k_feat_p"), (MLPW[0:EMB, 0, :], "l1_hy_w1"),
                                  (MLPW[0:FFN64, 1, :], "l1_hy_w2"), (MLPW[0:FFN64, 2, :], "l1_hy_w3")):
                    eng.dma_start(dst, A[name]).then_inc(s_mlp, 16)
                for dst, name in ((FW, "k_fwd"), (SP_, "k_spec"), (WIN["s"], "k_win_s"), (WIN["p"], "k_win_p")):
                    eng.dma_start(dst.rearrange("p a b -> p (a b)"), A[name]).then_inc(s_k, 16)
                for n, (kind, f) in slots():
                    if n + 2 < n_t:
                        col = tile_of(n + 2)[3] * P
                        ring.load(eng, n + 2, w_in[:, :, col:col + P], (KD, P))
                    if n >= 1:
                        c, knd, half, _ = tile_of(n - 1)
                        eng.wait_ge(acT.sem, acT.at("e", n - 1))
                        eng.dma_start(tok_dram[knd, c][:, :, half * P:(half + 1) * P], STG).then_inc(s_tok, 16)
                    if n in EXTRA and EXTRA[n][0] == "leaf":
                        for g in "sp":
                            eng.wait_ge(acF[g].sem, acF[g].at("hx", f))
                            eng.dma_start(filt_dram[g][f], KB[g]).then_inc(s_flt[g], 16)
                    if n % 4 == 1 and 5 <= n < 18:
                        c = (n - 5) // 4
                        if c:
                            eng.wait_ge(peF["p"].sem, peF["p"].at("tap1", 2 * c - 1))
                            eng.wait_ge(veF["p"].sem, veF["p"].at("bias", 2 * c - 1))
                            eng.wait_ge(acF["p"].sem, acF["p"].at("win1", 2 * c - 1))
                        else:
                            eng.wait_ge(acM.sem, acM.end())
                            eng.wait_ge(peM.sem, peM.end())
                        cs = slice(c * HC, (c + 1) * HC)
                        eng.dma_start(W4[0:FFN64, :, :], A["l1_hy_w4"].rearrange("k (a c) -> k a c", a=4)[:, :, cs]).then_inc(s_c, 16)
                        eng.dma_start(DELTA, A["k_delta"][0, cs].partition_broadcast(P)).then_inc(s_c, 16)
                        eng.dma_start(BIAS[0:1, :, :], A["l1_hy_bias"][:, cs].unsqueeze(0)).then_inc(s_c, 16)

            @program("pe")
            def _(eng):
                for n, (kind, f) in slots():
                    if n < n_t:
                        ring.ready(eng, n)
                        if n:
                            eng.wait_ge(acW.sem, acW.at("p", n - 1))
                        wh, wl = ring.get(n, (KD, P))
                        for k in range(KD):
                            if n == 0:
                                h_ready(eng, k)
                            m = product(eng, 0, (wh[:, k, :], wl[:, k, :]), (HH[:, k], HL[:, k]), k == 0, k == KD - 1)
                        m.then_inc(*ring.pe.did("used", n))
                    if n:
                        eng.wait_ge(veW.sem, veW.at("c2", n - 1))
                        if n >= 2:
                            eng.wait_ge(acT.sem, acT.at("e", n - 2))
                        for tt in range(NT):
                            at = 1 + tt * P + (2 if tt >= NS // P else 0)
                            m = eng.transpose(PS[:, 3 + tt // 4, (tt % 4) * P:(tt % 4 + 1) * P], CV[(n - 1) % 2][:, at:at + P], ident)
                        m.then_inc(*peT.did("t", n - 1))
                    if kind == "mlp":
                        if f == 0:
                            eng.wait_ge(s_mlp, 80)
                        kk = EMB if f == 0 else FFN64
                        src = FEAT if f == 0 else HD
                        for c in range(5):
                            i = 5 * f + c
                            if f:
                                eng.wait_ge(acM.sem, acM.at("sin", i - 5))
                            wait_bank(eng, veM_, "arg", i)
                            eng.matmul(PS[0:FFN64, small_bank(veM_, "arg", i), :], MLPW[0:kk, f, :], src[0:kk, c * 512:(c + 1) * 512],
                                       start=True, stop=True).then_inc(*peM.did("t", i))
                    if kind == "tap":
                        c, order = JOBS[f]
                        eng.wait_ge(s_c, 48 * (c + 1))
                        eng.wait_ge(acM.sem, acM.end())
                        for g, base in (("s", 0), ("p", 2 * NS)):
                            for b in range(T_OF[g]):
                                wait_bank(eng, veF[g], f"k{b}", f)
                                bank = small_bank(veF[g], f"k{b}", f)
                                for u in range(2):
                                    tap = 2 * b + u
                                    m = eng.matmul(PS[:, bank, u * HC:(u + 1) * HC], HD[0:FFN64, base + tap * P:base + (tap + 1) * P],
                                                   W4[0:FFN64, 2 * (tap // T_OF[g]) + order, :], start=True, stop=True)
                                m.then_inc(*peF[g].did(f"tap{b}", f))
                    if kind == "leaf":
                        eng.wait_ge(s_k, 64)
                        for g in "sp":
                            T = TB[g]
                            eng.wait_ge(veF[g].sem, veF[g].at(leaves_made[g], f))
                            for l in LEAVES[g]:
                                wait_bank(eng, acF[g], f"h{l}", f)
                                M = matrices(FW, l, False)
                                if l == 0:
                                    M = [[M[0][0], SP_[:, 0, :]], [M[1][0], SP_[:, 2, :]]]
                                transform(eng, small_bank(acF[g], f"h{l}", f), M, [T[:, 2 * l, :], T[:, 2 * l + 1, :]]).then_inc(*peF[g].did(f"h{l}", f))
                            wait_bank(eng, acF[g], "hx", f)
                            bank = small_bank(acF[g], "hx", f)
                            for i in range(2):
                                m = eng.matmul(PS[:, bank, 0:HC], SP_[:, 1 + 2 * i, :], T[:, i, :], start=i == 0, stop=i == 1)
                            m.then_inc(*peF[g].did("hx", f))

            @program("ac")
            def _(eng):
                ended(eng, *prev)
                eng.wait_ge(veZ.sem, veZ.end())
                for n, (kind, f) in slots():
                    if n < n_t:
                        eng.wait_ge(ring.pe.sem, ring.pe.at("used", n))
                        if n:
                            eng.wait_ge(veW.sem, veW.at("c2", n - 1))
                        for a, w, j in GROUPS:
                            at = 1 + a + 2 * j
                            eng.activation(PAD[:, at:at + w], PSF[:, a:a + w], ACT.Copy).then_inc(*acW.did("sp"[j], n))
                        ring.hi(eng, n + 2)
                    if n:
                        eng.wait_ge(peT.sem, peT.at("t", n - 1))
                        if n >= 2:
                            eng.wait_ge(s_tok, 16 * (n - 1))
                        eng.activation(STG, psum(3, N).rearrange("p (t c) -> p t c", c=P), ACT.Copy).then_inc(*acT.did("e", n - 1))
                    if kind == "mlp":
                        for i in range(5 * f, 5 * f + 5):
                            eng.wait_ge(veM_.sem, veM_.at("clamp", i))
                            eng.activation(HD[0:FFN64, (i % 5) * 512:(i % 5 + 1) * 512], RED[0:FFN64, :], ACT.Sin).then_inc(*acM.did("sin", i))
                    if kind == "tap":
                        eng.wait_ge(s_c, 48 * (JOBS[f][0] + 1))
                        eng.wait_ge(s_k, 64)
                        eng.wait_ge(peM.sem, peM.end())
                        for g in "sp":
                            if f:
                                eng.wait_ge(s_flt[g], 16 * f)
                            for b in range(T_OF[g]):
                                for tap in (2 * b, 2 * b + 1):
                                    m = eng.activation(KB[g][:, tap, :], DELTA, ACT.Exp, scale=WIN[g][:, 0, tap:tap + 1], bias=WIN[g][:, 1, tap:tap + 1])
                                m.then_inc(*acF[g].did(f"win{b}", f))
                    if kind == "leaf":
                        for g in "sp":
                            for l in LEAVES[g]:
                                eng.wait_ge(peF[g].sem, peF[g].at(f"h{l}", f))
                                eng.activation(row(KB[g], 2 * l, 2), PS[:, small_bank(acF[g], f"h{l}", f), :], ACT.Copy).then_inc(*acF[g].did(f"h{l}", f))
                            eng.wait_ge(peF[g].sem, peF[g].at("hx", f))
                            eng.activation(KB[g][:, 2 * len(LEAVES[g]), :], PS[:, small_bank(acF[g], "hx", f), 0:HC], ACT.Copy).then_inc(*acF[g].did("hx", f))

            @program("po")
            def _(eng):
                ended(eng, *prev)
                for n in range(2, n_t):
                    ring.lo(eng, n)

            @program("ve")
            def _(eng):
                ended(eng, *prev)
                eng.memset(PAD, 0.0).then_inc(*veZ.did("pad"))
                half = (slice(0, FFN64), slice(None))
                for n, (kind, f) in slots():
                    if n < n_t:
                        col = tile_of(n)[3]
                        eng.wait_ge(acW.sem, acW.at("p", n))
                        if n >= 2:
                            eng.wait_ge(peT.sem, peT.at("t", n - 2))
                        for k in range(3):
                            wcol = vec("l1_hy_short_w", 24 * k + col)
                            src, dst = PAD[:, k:k + PADN - 2], CV[n % 2][:, 1:PADN - 1]
                            if k:
                                eng.wait_ge(veW.sem, veW.at(f"c{k - 1}", n))
                                m = eng.scalar_tensor_tensor(dst, src, wcol, dst, ALU.mult, ALU.add)
                            else:
                                m = eng.tensor_scalar(dst, src, wcol, vec("l1_hy_short_b", col), ALU.mult, ALU.add)
                            m.then_inc(*veW.did(f"c{k}", n))
                    if kind == "mlp":
                        bias = vec(f"l1_hy_b{f + 1}")[0:FFN64, :]
                        for i in range(5 * f, 5 * f + 5):
                            ve = veM_
                            eng.wait_ge(peM.sem, peM.at("t", i))
                            if i:
                                eng.wait_ge(ve.sem, ve.at("clamp", i - 1))
                            eng.tensor_scalar(ARG[half], PS[0:FFN64, small_bank(ve, "arg", i), :], bias, vec("l1_hy_freq")[0:FFN64, :], ALU.add, ALU.mult)\
                                .then_inc(*ve.did("arg", i))
                            eng.wait_ge(ve.sem, ve.at("arg", i))
                            eng.tensor_scalar(TMP[half], ARG[half], 1 / (2 * math.pi), MAGIC, ALU.mult, ALU.add).then_inc(*ve.did("turns", i))
                            eng.wait_ge(ve.sem, ve.at("turns", i))
                            eng.tensor_scalar(TMP[half], TMP[half], MAGIC, None, ALU.subtract).then_inc(*ve.did("whole", i))
                            eng.wait_ge(ve.sem, ve.at("whole", i))
                            eng.scalar_tensor_tensor(ARG[half], TMP[half], -TWO_PI_HI, ARG[half], ALU.mult, ALU.add).then_inc(*ve.did("hi", i))
                            eng.wait_ge(ve.sem, ve.at("hi", i))
                            if i:
                                eng.wait_ge(acM.sem, acM.at("sin", i - 1))
                            eng.scalar_tensor_tensor(RED[half], TMP[half], -TWO_PI_LO, ARG[half], ALU.mult, ALU.add).then_inc(*ve.did("lo", i))
                            eng.wait_ge(ve.sem, ve.at("lo", i))
                            eng.tensor_scalar(RED[half], RED[half], 3.1415925, -3.1415925, ALU.min, ALU.max).then_inc(*ve.did("clamp", i))
                    if kind == "tap":
                        order = JOBS[f][1]
                        for g in "sp":
                            ve, K, T, tn = veF[g], KB[g], TB[g], T_OF[g]
                            for b in range(tn):
                                eng.wait_ge(peF[g].sem, peF[g].at(f"tap{b}", f))
                                eng.wait_ge(acF[g].sem, acF[g].at(f"win{b}", f))
                                eng.tensor_tensor(row(K, 2 * b, 2), row(K, 2 * b, 2), PS[:, small_bank(ve, f"k{b}", f), :], ALU.mult).then_inc(*ve.did(f"k{b}", f))
                            eng.wait_ge(ve.sem, ve.at(f"k{tn - 1}", f))
                            eng.tensor_tensor(K[0:1, 0, :], K[0:1, 0, :], BIAS[0:1, order, :], ALU.add).then_inc(*ve.did("bias", f))
                            eng.wait_ge(ve.sem, ve.at("bias", f))
                            if f:
                                eng.wait_ge(peF[g].sem, peF[g].at("hx", f - 1))
                            eng.tensor_tensor(row(T, 0, tn), row(K, 0, tn), row(K, tn, tn), ALU.add).then_inc(*ve.did("r", f))
                            eng.tensor_tensor(row(T, tn, tn), row(K, 0, tn), row(K, tn, tn), ALU.subtract).then_inc(*ve.did("q", f))
                            if g == "s":
                                eng.wait_ge(ve.sem, ve.at("q", f))
                                tree(eng, ve, "ft", f, T, 0, T, 8, K, T)

            part1 = [ring.pe, ring.ac, ring.po, peT, acW, acT, veW, peM, veM_, acM] + [x[g] for x in (peF, acF, veF) for g in "sp"]

            x_r = Region(XT_AT, HT_AT)
            K2, T2, KP2, TP2 = x_r.take(16, HC), x_r.take(16, HC), x_r.take(4, HC), x_r.take(4, HC)
            IV = mid.take(25, P)
            H2, HP2 = mid.take(17, HC), mid.take(5, HC)
            Z, X1, X2 = mid.take(NT, HC), mid.take(NT, HC), mid.take(NT, HC)
            TURNED = mid.take(N)
            KB2, TB2, HB = {"s": K2, "p": KP2}, {"s": T2, "p": TP2}, {"s": H2, "p": HP2}
            nj = len(JOBS)
            s_iv, s_z, s_x1, s_x2 = sem("inverse_landed"), sem("z_landed"), sem("x1_landed"), sem("x2_landed")
            s_h = {g: sem("filter_landed_" + g) for g in "sp"}
            N_BANKS, FIRST_BANK = {"s": 6, "p": 2}, {"s": 0, "p": 6}
            peC, acC, veC, poC = {}, {}, {}, {}
            for g in "sp":
                L = LEAVES[g]
                peC[g] = steps("pe_conv_" + g, [f"z{l}" for l in L] + [f"i{l}" for l in L], nj)
                acC[g] = steps("ac_conv_" + g, [f"i{l}" for l in L], nj)
                veC[g] = steps("ve_conv_" + g, ([f"zt{i}" for i in range(N_TREE)] if g == "s" else []) + [f"{t}{l}" for l in L for t in ("re", "im", "cross", "done")]
                               + [f"it{i}" for i in range(N_INV if g == "s" else 1)] + ["gate"], nj)
                poC[g] = steps("po_conv_" + g, [f"{t}{l}" for l in L for t in ("a", "b")], nj)
            peO, acO, poO = steps("pe_turn", ["t0", "t1"], NCH), steps("ac_turn", ["hi0", "all0", "hi1", "all1"], NCH), steps("po_turn", ["lo0", "lo1"], NCH)
            leaf_step = {l: f"zt{i}" for l, i in enumerate((2, 3, 6, 7, 14, 15, 18, 19))}

            def last_leaf(g):
                return LEAVES[g][-1]

            def bank_of(g, kind, l):
                item = l + (len(LEAVES[g]) if kind == "i" else 0)
                return FIRST_BANK[g] + item % N_BANKS[g]

            def wait_conv_bank(eng, g, rnd, kind, l):
                item = l + (len(LEAVES[g]) if kind == "i" else 0) - N_BANKS[g]
                if item >= 0:
                    m = item - len(LEAVES[g])
                    who, what = (veC[g], f"done{item}") if m < 0 else (acC[g], f"i{m}")
                    eng.wait_ge(who.sem, who.at(what, rnd))
                elif rnd:
                    eng.wait_ge(acC[g].sem, acC[g].at(f"i{last_leaf(g)}", rnd - 1))

            @program("sp")
            def _(eng):
                ended(eng, *part1)
                eng.wait_ge(s_tok, 16 * n_t)
                for g in "sp":
                    eng.wait_ge(s_flt[g], 16 * nj)
                eng.dma_start(Z, tok_dram[0, 0]).then_inc(s_z, 16)
                for g in "sp":
                    eng.dma_start(HB[g], filt_dram[g][0]).then_inc(s_h[g], 16)
                eng.dma_start(IV.rearrange("p a b -> p (a b)"), A["k_inv8"]).then_inc(s_iv, 16)
                eng.dma_start(X1, tok_dram[1, 0]).then_inc(s_x1, 16)
                eng.dma_start(X2, tok_dram[2, 0]).then_inc(s_x2, 16)
                for rnd, (c, order) in enumerate(JOBS):
                    if order and c + 1 < NCH:
                        eng.wait_ge(veC["s"].sem, veC["s"].at(f"zt{N_TREE - 1}", rnd))
                        eng.wait_ge(peC["p"].sem, peC["p"].at("z1", rnd))
                        eng.dma_start(Z, tok_dram[0, c + 1]).then_inc(s_z, 16)
                    for g in "ps":
                        if rnd + 1 < nj:
                            eng.wait_ge(veC[g].sem, veC[g].at(f"done{last_leaf(g)}", rnd))
                            eng.dma_start(HB[g], filt_dram[g][rnd + 1]).then_inc(s_h[g], 16)
                    if c + 1 < NCH:
                        if order == 0:
                            for g in "ps":
                                eng.wait_ge(veC[g].sem, veC[g].at("gate", rnd))
                            eng.dma_start(X1, tok_dram[1, c + 1]).then_inc(s_x1, 16)
                        else:
                            eng.wait_ge(peO.sem, peO.at("t1", c))
                            eng.dma_start(X2, tok_dram[2, c + 1]).then_inc(s_x2, 16)
                for g in "sp":
                    eng.wait_ge(veC[g].sem, veC[g].end())
                eng.dma_start(XT, spill).then_inc(s_x, 16)

            @program("pe")
            def _(eng):
                ended(eng, *part1)
                eng.wait_ge(s_iv, 16)

                def forward(g, l, rhs):
                    transform(eng, bank_of(g, "z", l), matrices(FW, l, False), rhs).then_inc(*peC[g].did(f"z{l}", rnd))

                def inverse(g, l):
                    wait_conv_bank(eng, g, rnd, "i", l)
                    eng.wait_ge(poC[g].sem, poC[g].at(f"b{l}", rnd))
                    transform(eng, bank_of(g, "i", l), matrices(IV, l, True), [KB2[g][:, 2 * l, :], KB2[g][:, 2 * l + 1, :]]).then_inc(*peC[g].did(f"i{l}", rnd))
                for rnd, (c, order) in enumerate(JOBS):
                    eng.wait_ge(s_z, 16 * (c + 1))
                    if order:
                        eng.wait_ge(veC["p"].sem, veC["p"].at("gate", rnd - 1))
                    for l in LEAVES["p"]:
                        wait_conv_bank(eng, "p", rnd, "z", l)
                        forward("p", l, [Z[:, NS // P + u, :] for u in range(2)])
                    if rnd and order == 0:
                        eng.wait_ge(acO.sem, acO.at("all1", c - 1))
                    for l in LEAVES["s"]:
                        if l == N_BANKS["s"]:
                            for lp in LEAVES["p"]:
                                inverse("p", lp)
                        wait_conv_bank(eng, "s", rnd, "z", l)
                        eng.wait_ge(veC["s"].sem, veC["s"].at(leaf_step[l], rnd))
                        forward("s", l, [T2[:, 2 * l, :], T2[:, 2 * l + 1, :]])
                    for l in LEAVES["s"]:
                        inverse("s", l)
                    if order:
                        for g in "ps":
                            eng.wait_ge(veC[g].sem, veC[g].at("gate", rnd))
                        for half in range(2):
                            for tt in range(NT):
                                m = eng.transpose(PS[:, 3 * half + tt // 4, (tt % 4) * P:(tt % 4 + 1) * P], X2[:, tt, half * P:(half + 1) * P], ident)
                            m.then_inc(*peO.did(f"t{half}", c))

            @program("ac")
            def _(eng):
                ended(eng, *part1)
                for rnd, (c, order) in enumerate(JOBS):
                    for g in "ps":
                        for l in LEAVES[g]:
                            eng.wait_ge(peC[g].sem, peC[g].at(f"i{l}", rnd))
                            eng.activation(row(TB2[g], 2 * l, 2), PS[:, bank_of(g, "i", l), :], ACT.Copy).then_inc(*acC[g].did(f"i{l}", rnd))
                    if order:
                        for half in range(2):
                            eng.wait_ge(peO.sem, peO.at(f"t{half}", c))
                            eng.activation(HH[:, 2 * c + half, :], psum(3 * half, N), ACT.Copy).then_inc(*acO.did(f"hi{half}", c))
                            if half:
                                eng.wait_ge(poO.sem, poO.at("lo0", c))
                            elif c:
                                eng.wait_ge(poO.sem, poO.at("lo1", c - 1))
                            eng.activation(TURNED, psum(3 * half, N), ACT.Copy).then_inc(*acO.did(f"all{half}", c))

            @program("po")
            def _(eng):
                for rnd, (c, order) in enumerate(JOBS):
                    for g in "ps":
                        K, T = KB2[g], TB2[g]
                        for l in LEAVES[g]:
                            eng.wait_ge(veC[g].sem, veC[g].at(f"done{l}", rnd))
                            eng.tensor_tensor(K[:, 2 * l, :], K[:, 2 * l, :], T[:, 2 * l, :], ALU.subtract).then_inc(*poC[g].did(f"a{l}", rnd))
                            eng.tensor_tensor(K[:, 2 * l + 1, :], K[:, 2 * l + 1, :], T[:, 2 * l + 1, :], ALU.add).then_inc(*poC[g].did(f"b{l}", rnd))
                    if order:
                        for half in range(2):
                            eng.wait_ge(acO.sem, acO.at(f"all{half}", c))
                            eng.tensor_tensor(HL[:, 2 * c + half, :], TURNED, HH32[:, 2 * c + half, :], ALU.subtract).then_inc(*poO.did(f"lo{half}", c))

            @program("ve")
            def _(eng):
                ended(eng, *part1)

                def multiply(g):
                    ve, K, T, H = veC[g], KB2[g], TB2[g], HB[g]
                    eng.wait_ge(s_h[g], 16 * (rnd + 1))
                    for l in LEAVES[g]:
                        bank = bank_of(g, "z", l)
                        re, im = PS[:, bank, 0:HC], PS[:, bank, HC:2 * HC]
                        h_im = len(LEAVES[g]) * 2 if l == 0 else 2 * l
                        eng.wait_ge(peC[g].sem, peC[g].at(f"z{l}", rnd))
                        eng.tensor_tensor(K[:, 2 * l, :], re, H[:, 2 * l, :], ALU.mult).then_inc(*ve.did(f"re{l}", rnd))
                        eng.tensor_tensor(K[:, 2 * l + 1, :], im, H[:, h_im, :], ALU.mult).then_inc(*ve.did(f"im{l}", rnd))
                        eng.tensor_tensor(T[:, 2 * l, :], im, H[:, 2 * l + 1, :], ALU.mult).then_inc(*ve.did(f"cross{l}", rnd))
                        eng.tensor_tensor(T[:, 2 * l + 1, :], re, H[:, 2 * l + 1, :], ALU.mult).then_inc(*ve.did(f"done{l}", rnd))

                def gate(g, last, scale):
                    dst, X, landed = (Z, X1, s_x1) if order == 0 else (X2, X2, s_x2)
                    eng.wait_ge(veC[g].sem, veC[g].at(last, rnd))
                    eng.wait_ge(landed, 16 * (c + 1))
                    f, n = FIRST[g], T_OF[g]
                    eng.scalar_tensor_tensor(row(dst, f, n), row(TB2[g], 0, n), scale, row(X, f, n), ALU.mult, ALU.mult).then_inc(*veC[g].did("gate", rnd))
                for rnd, (c, order) in enumerate(JOBS):
                    eng.wait_ge(s_z, 16 * (c + 1))
                    if rnd:
                        eng.wait_ge(veC["s"].sem, veC["s"].at("gate", rnd - 1))
                    tree(eng, veC["s"], "zt", rnd, Z, 0, Z, 0, K2, T2)
                    multiply("p")
                    eng.wait_ge(veC["s"].sem, veC["s"].at(f"zt{N_TREE - 1}", rnd))
                    multiply("s")
                    eng.wait_ge(acC["p"].sem, acC["p"].at(f"i{last_leaf('p')}", rnd))
                    eng.tensor_tensor(row(TP2, 0, 2), row(TP2, 0, 2), row(TP2, 2, 2), ALU.add).then_inc(*veC["p"].did("it0", rnd))
                    gate("p", "it0", 4.0)
                    eng.wait_ge(acC["s"].sem, acC["s"].at(f"i{last_leaf('s')}", rnd))
                    untree(eng, veC["s"], "it", rnd, K2, T2)
                    gate("s", f"it{N_INV - 1}", 1.0)

            done = [peO, acO, poO] + [x[g] for x in (peC, acC, veC, poC) for g in "sp"]
            x_ready, part3 = project(A["l1_w_out"], done, done, 1, (s_x, 32))
            return x_ready, done + part3

        def x_here(eng, k):
            ended(eng, *x_steps)

        before, early = prev, {}
        prev, h_ready = norm(prev, x_here, HL_END, 0, mod(0, 0), early)
        x_ready, prev = mixer_even(before, prev, h_ready, early)
        x_ready, prev = ffn_layer(0, x_ready, prev)
        before, early = prev, {}
        prev, h_ready = norm(prev, x_ready, HL_END, 2, mod(1, 0), early)
        x_ready, prev = mixer_hyena(before, prev, h_ready, early)
        x_ready, prev = ffn_layer(1, x_ready, prev)

        def store(prev, x_ready):
            r = Region(W_AT, ARENA)
            OR = [r.take(D) for _ in range(4)]
            GAIN, RS = r.take(D), r.take(NT)
            h = Region(HT_AT, FIX_AT)
            SQ = h.take(KD, N)
            pairs, SUMS = (0, 2, 4), 6
            EARLY = len(pairs)
            pe = steps("pe_out", ["lo", "hi"], NT)
            ve = steps("ve_out", ["lo"], NT)
            ac = steps("ac_out", ["hi"], NT)
            po = steps("po_out", ["gain"], NT)
            acn, acr = steps("ac_final_norm", ["sq"], KD), steps("ac_final_root", ["root"])
            poS = steps("po_final_norm", [f"add{k}" for k in range(1, KD)])
            pen, ven = steps("pe_final_norm", ["sum"]), steps("ve_final_norm", ["inv"])
            s_gain = sem("gain_landed")
            s_o = [sem(f"stored{i}") for i in range(len(OR))]

            def wait_room(eng, t):
                if t >= len(OR):
                    eng.wait_ge(s_o[t % len(OR)], 16 * (t // len(OR)))

            @program("pe")
            def _(eng):
                ended(eng, *prev)
                for t in range(NT):
                    if t == EARLY:
                        eng.wait_ge(poS.sem, poS.end())
                        for tt in range(NT):
                            m = eng.matmul(PS[:, SUMS, tt:tt + 1], SQ[:, 0, tt * P:(tt + 1) * P], ones[:, 0:1], start=True, stop=True)
                        m.then_inc(*pen.did("sum"))
                    for half, who in ((0, ve), (1, ac)):
                        if t >= EARLY:
                            eng.wait_ge(who.sem, who.at(("lo", "hi")[half], t - EARLY))
                        for k in range(4):
                            m = eng.transpose(PS[:, pairs[t % EARLY] + half, k * P:(k + 1) * P], XT[:, 4 * half + k, t * P:(t + 1) * P], ident)
                        m.then_inc(*pe.did(("lo", "hi")[half], t))

            @program("ve")
            def _(eng):
                eng.wait_ge(acr.sem, acr.end())
                eng.reciprocal(RS, RS).then_inc(*ven.did("inv"))
                eng.wait_ge(ven.sem, ven.end())
                eng.wait_ge(s_gain, 16)
                for t in range(NT):
                    eng.wait_ge(pe.sem, pe.at("lo", t))
                    wait_room(eng, t)
                    eng.scalar_tensor_tensor(OR[t % len(OR)][:, 0:512], PS[:, pairs[t % EARLY], :], RS[:, t:t + 1], GAIN[:, 0:512], ALU.mult, ALU.mult)\
                        .then_inc(*ve.did("lo", t))

            @program("ac")
            def _(eng):
                for k in range(KD):
                    x_ready(eng, k)
                    eng.activation(SQ[:, k, :], XT[:, k, :], ACT.Square).then_inc(*acn.did("sq", k))
                eng.wait_ge(pen.sem, pen.end())
                eng.activation(RS, PS[:, SUMS, 0:NT], ACT.Sqrt, scale=1.0 / D, bias=eps).then_inc(*acr.did("root"))
                eng.wait_ge(ven.sem, ven.end())
                for t in range(NT):
                    eng.wait_ge(pe.sem, pe.at("hi", t))
                    wait_room(eng, t)
                    eng.activation(OR[t % len(OR)][:, 512:1024], PS[:, pairs[t % EARLY] + 1, :], ACT.Identity, bias=0.0, scale=RS[:, t:t + 1])\
                        .then_inc(*ac.did("hi", t))

            @program("po")
            def _(eng):
                for k in range(1, KD):
                    eng.wait_ge(acn.sem, acn.at("sq", k))
                    if k > 1:
                        eng.wait_ge(poS.sem, poS.at(f"add{k - 1}"))
                    eng.tensor_tensor(SQ[:, 0, :], SQ[:, 0, :], SQ[:, k, :], ALU.add).then_inc(*poS.did(f"add{k}"))
                eng.wait_ge(s_gain, 16)
                for t in range(NT):
                    eng.wait_ge(ac.sem, ac.at("hi", t))
                    out = OR[t % len(OR)][:, 512:1024]
                    eng.tensor_tensor(out, out, GAIN[:, 512:1024], ALU.mult).then_inc(*po.did("gain", t))

            @program("sp")
            def _(eng):
                ended(eng, *prev)
                eng.dma_start(GAIN, A["final_norm"].partition_broadcast(P)).then_inc(s_gain, 16)
                for t in range(NT):
                    eng.wait_ge(ve.sem, ve.at("lo", t))
                    eng.wait_ge(po.sem, po.at("gain", t))
                    dst = OUT["y_sample"][0, t * P:(t + 1) * P, :] if t < NS // P else OUT["y_prompt"][0, t * P - NS:(t + 1) * P - NS, :]
                    eng.dma_start(dst, OR[t % len(OR)]).then_inc(s_o[t % len(OR)], 16)
                for i, done in enumerate(s_o):
                    eng.wait_ge(done, 16 * len(range(i, NT, len(OR))))

        store(prev, x_ready)

        block = ctx.enter_context(nc.Block())

        @block.sync
        def _(eng):
            for f in progs["sp"]:
                f(eng)

        @block.tensor
        def _(eng):
            for f in progs["pe"]:
                f(eng)

        @block.vector
        def _(eng):
            for f in progs["ve"]:
                f(eng)

        @block.scalar
        def _(eng):
            for f in progs["ac"]:
                f(eng)

        @block.gpsimd
        def _(eng):
            for f in progs["po"]:
                f(eng)


_OUTS = {"y_prompt": (1, NP_, D), "y_sample": (1, NS, D), "new_f": (1, HEADS, P, P), "new_b": (1, HEADS, P, P)}


def kernel(**inputs):
    import concourse.bacc as bacc
    from concourse.bass_utils import run_bass_kernel_spmd

    nc = bacc.Bacc("TRN2", target_bir_lowering=False, num_devices=1)
    arrays, A, OUT = {}, {}, {}
    for name, a in {**inputs, **constants()}.items():
        a = np.ascontiguousarray(a)
        arrays[f"in_{name}"] = a
        A[name] = nc.dram_tensor(f"in_{name}", a.shape, mybir.dt.from_np(a.dtype), kind="ExternalInput").ap()
    for name, shape in _OUTS.items():
        OUT[name] = nc.dram_tensor(f"out_{name}", shape, F32, kind="ExternalOutput").ap()
    build(nc, A, OUT)
    r = run_bass_kernel_spmd(nc, [arrays], core_ids=[0])
    return tuple(r.results[0][f"out_{name}"] for name in _OUTS)
```
